# Optimizing a Trainium2 kernel written in Bass

```python
import math
import jax, jax.numpy as jnp
from jax import lax
import numpy as np

D_MODEL = 1024
BATCH = 1
SEQ = 512
DEPTH = 1

CHUNK = 64
EPS = 1e-6
NEG = -1e30
SWA_HEADS = 8
SWA_KV_HEADS = 2
SWA_HEAD_DIM = 64
SWA_WINDOW = 128
SWA_WINDOW_CHUNKS = SWA_WINDOW // CHUNK
MLA_HEADS = 8
MLA_Q_RANK = 256
MLA_KV_RANK = 128
MLA_NOPE_DIM = 64
MLA_ROPE_DIM = 32
MLA_V_DIM = 64
MLA_Q_BLOCK = 128
ROPE_THETA = 10000.0
SWA_Q_COLS = SWA_HEADS * SWA_HEAD_DIM
SWA_KV_COLS = SWA_KV_HEADS * SWA_HEAD_DIM
IN_COLS = SWA_Q_COLS + 2 * SWA_KV_COLS + MLA_Q_RANK + MLA_KV_RANK + MLA_ROPE_DIM
D_MIX = SWA_HEADS * SWA_HEAD_DIM + MLA_HEADS * MLA_V_DIM
PEER_HEADS = 8
PEER_N_KEYS = 128
PEER_N_EXPERTS = PEER_N_KEYS * PEER_N_KEYS
PEER_KEY_DIM = 128
PEER_TOPK = 16
PEER_TOKEN_BLOCK = 128

kernel_name = "hybrid_swa_mla_peer_adaln_block"

def rms_norm(x, g):
    xf = x.astype(jnp.float32)
    y = xf * lax.rsqrt(jnp.mean(xf * xf, axis=-1, keepdims=True) + EPS)
    return (y * g.astype(jnp.float32)).astype(x.dtype)

def rope(x, positions):
    d = x.shape[-1]
    freqs = ROPE_THETA ** (-jnp.arange(0, d, 2, dtype=jnp.float32) / d)
    ang = positions.astype(jnp.float32)[..., None] * freqs
    cos = jnp.cos(ang)[:, :, None, :]
    sin = jnp.sin(ang)[:, :, None, :]
    xf = x.astype(jnp.float32)
    x1, x2 = xf[..., : d // 2], xf[..., d // 2:]
    return jnp.concatenate([x1 * cos - x2 * sin, x1 * sin + x2 * cos], axis=-1).astype(x.dtype)

def alibi_slopes(n_heads):
    return jnp.exp2(-8.0 * jnp.arange(1, n_heads + 1, dtype=jnp.float32) / n_heads)

def swa_mixer(q, k, v, positions, q_norm, k_norm, sinks):
    B, S = q.shape[0], q.shape[1]
    NC = S // CHUNK
    G = SWA_HEADS // SWA_KV_HEADS
    W = SWA_WINDOW_CHUNKS
    q = rms_norm(q, q_norm).astype(jnp.float32) * (SWA_HEAD_DIM ** -0.5)
    k = rms_norm(k, k_norm).astype(jnp.float32)
    qc = q.reshape(B, NC, CHUNK, SWA_KV_HEADS, G, SWA_HEAD_DIM)

    def band(t):
        tc = t.reshape((B, NC, CHUNK) + t.shape[2:])
        pad = [(0, 0), (W - 1, 0)] + [(0, 0)] * (tc.ndim - 2)
        tp = jnp.pad(tc, pad)
        return jnp.concatenate([tp[:, j:j + NC] for j in range(W)], axis=2)

    kb = band(k)
    vb = band(v.astype(jnp.float32))
    pb = band(positions)
    scores = jnp.einsum('bcqkgd,bcskd->bckgqs', qc, kb)
    pq = positions.reshape(B, NC, CHUNK)
    dist = jnp.abs(pq[..., :, None] - pb[..., None, :]).astype(jnp.float32)
    slopes = alibi_slopes(SWA_HEADS).reshape(SWA_KV_HEADS, G)
    scores = scores - slopes[None, None, :, :, None, None] * dist[:, :, None, None]
    key_chunk = jnp.arange(NC)[:, None] - (W - 1) + jnp.arange(W * CHUNK)[None, :] // CHUNK
    valid = key_chunk >= 0
    scores = jnp.where(valid[None, :, None, None, None, :], scores, NEG)
    sink = sinks.astype(jnp.float32).reshape(SWA_KV_HEADS, G)[None, None, :, :, None, None]
    m = jnp.maximum(jnp.max(scores, axis=-1, keepdims=True), sink)
    p = jnp.exp(scores - m)
    denom = jnp.sum(p, axis=-1, keepdims=True) + jnp.exp(sink - m)
    o = jnp.einsum('bckgqs,bcskd->bcqkgd', p / denom, vb)
    return o.reshape(B, S, SWA_HEADS * SWA_HEAD_DIM)

def mla_mixer(c_q, c_kv, k_rope, positions, q_a_norm, kv_a_norm, w_uq, w_ukv, q_norm, k_norm):
    B, S = c_q.shape[0], c_q.shape[1]
    H = MLA_HEADS
    q = (rms_norm(c_q, q_a_norm) @ w_uq).reshape(B, S, H, MLA_NOPE_DIM + MLA_ROPE_DIM)
    q = jnp.concatenate([q[..., :MLA_NOPE_DIM], rope(q[..., MLA_NOPE_DIM:], positions)], axis=-1)
    kv = (rms_norm(c_kv, kv_a_norm) @ w_ukv).reshape(B, S, H, MLA_NOPE_DIM + MLA_V_DIM)
    k_nope, v = kv[..., :MLA_NOPE_DIM], kv[..., MLA_NOPE_DIM:]
    kr = rope(k_rope[:, :, None, :], positions)
    k = jnp.concatenate([k_nope, jnp.broadcast_to(kr, (B, S, H, MLA_ROPE_DIM))], axis=-1)
    q = rms_norm(q, q_norm).astype(jnp.float32) * ((MLA_NOPE_DIM + MLA_ROPE_DIM) ** -0.5)
    k = rms_norm(k, k_norm).astype(jnp.float32)
    v = v.astype(jnp.float32)
    outs = []
    for i in range(S // MLA_Q_BLOCK):
        start, end = i * MLA_Q_BLOCK, (i + 1) * MLA_Q_BLOCK
        s = jnp.einsum('bqhd,bkhd->bhqk', q[:, start:end], k[:, :end])
        q_chunk = (start + jnp.arange(MLA_Q_BLOCK)) // CHUNK
        k_chunk = jnp.arange(end) // CHUNK
        s = jnp.where(k_chunk[None, :] <= q_chunk[:, None], s, NEG)
        p = jax.nn.softmax(s, axis=-1)
        outs.append(jnp.einsum('bhqk,bkhd->bqhd', p, v[:, :end]))
    return jnp.concatenate(outs, axis=1).reshape(B, S, H * MLA_V_DIM)

def peer_ffn(h, w_query, sub_keys, u_table, v_table):
    B, S, D = h.shape
    T = B * S
    K = PEER_TOPK
    xt = h.reshape(T, D)
    q = (xt @ w_query).reshape(T, PEER_HEADS, 2, PEER_KEY_DIM // 2).astype(jnp.float32)
    s = jnp.einsum('thpd,hpnd->thpn', q, sub_keys.astype(jnp.float32))
    s_top, i_top = lax.top_k(s, K)
    cand = (s_top[:, :, 0, :, None] + s_top[:, :, 1, None, :]).reshape(T, PEER_HEADS, K * K)
    best, bi = lax.top_k(cand, K)
    ia, ib = bi // K, bi % K
    e = (jnp.take_along_axis(i_top[:, :, 0], ia, axis=-1) * PEER_N_KEYS
         + jnp.take_along_axis(i_top[:, :, 1], ib, axis=-1))
    g = jax.nn.softmax(best, axis=-1).astype(h.dtype)

    def block_fn(args):
        xb, eb, gb = args
        a = jax.nn.gelu(jnp.einsum('tkd,td->tk', u_table[eb], xb), approximate=False)
        return jnp.einsum('tk,tkd->td', gb * a, v_table[eb])

    nb = T // PEER_TOKEN_BLOCK
    y = lax.map(block_fn, (xt.reshape(nb, PEER_TOKEN_BLOCK, D),
                           e.reshape(nb, PEER_TOKEN_BLOCK, PEER_HEADS * K),
                           g.reshape(nb, PEER_TOKEN_BLOCK, PEER_HEADS * K)))
    return y.reshape(B, S, D)

def hybrid_layer(x, c, positions, w_ada, b_ada, norm1_g, norm2_g, w_in,
                 swa_q_norm, swa_k_norm, swa_sinks, mla_q_a_norm, mla_kv_a_norm,
                 mla_w_uq, mla_w_ukv, mla_q_norm, mla_k_norm, w_out,
                 peer_w_query, peer_sub_keys, peer_u, peer_v):
    B, S, D = x.shape
    ada = c @ w_ada + b_ada
    shift1, scale1, gate1, shift2, scale2, gate2 = [t[:, None, :] for t in jnp.split(ada, 6, axis=-1)]
    h = rms_norm(x, norm1_g) * (1.0 + scale1) + shift1
    z = h @ w_in
    o0 = SWA_Q_COLS
    o1 = o0 + SWA_KV_COLS
    o2 = o1 + SWA_KV_COLS
    o3 = o2 + MLA_Q_RANK
    o4 = o3 + MLA_KV_RANK
    q_a = z[..., :o0].reshape(B, S, SWA_HEADS, SWA_HEAD_DIM)
    k_a = z[..., o0:o1].reshape(B, S, SWA_KV_HEADS, SWA_HEAD_DIM)
    v_a = z[..., o1:o2].reshape(B, S, SWA_KV_HEADS, SWA_HEAD_DIM)
    out_a = swa_mixer(q_a, k_a, v_a, positions, swa_q_norm, swa_k_norm, swa_sinks)
    out_b = mla_mixer(z[..., o2:o3], z[..., o3:o4], z[..., o4:], positions,
                      mla_q_a_norm, mla_kv_a_norm, mla_w_uq, mla_w_ukv, mla_q_norm, mla_k_norm)
    mix = jnp.concatenate([out_a, out_b], axis=-1).astype(x.dtype) @ w_out
    x = x + gate1 * mix
    h2 = rms_norm(x, norm2_g) * (1.0 + scale2) + shift2
    x = x + gate2 * peer_ffn(h2, peer_w_query, peer_sub_keys, peer_u, peer_v)
    return x

def setup_inputs(seed: int = 0) -> dict:
    key = jax.random.key(seed)
    ks = jax.random.split(key, 24)
    f32 = jnp.float32
    L = DEPTH

    def nrm(k, shape, scale):
        return jax.random.normal(k, shape, f32) * scale

    def gain(k, shape):
        return 1.0 + 0.05 * jax.random.normal(k, shape, f32)

    x = jax.random.normal(ks[0], (BATCH, SEQ, D_MODEL), f32)
    c = jax.random.normal(ks[1], (BATCH, D_MODEL), f32)
    positions = (jnp.arange(SEQ, dtype=jnp.int32)[None, :]
                 + jax.random.randint(ks[2], (BATCH, 1), 0, 1024, dtype=jnp.int32))
    return {
        'x': x,
        'c': c,
        'positions': positions,
        'w_ada': nrm(ks[3], (L, D_MODEL, 6 * D_MODEL), 0.5 * D_MODEL ** -0.5),
        'b_ada': nrm(ks[4], (L, 6 * D_MODEL), 0.02),
        'norm1_g': gain(ks[5], (L, D_MODEL)),
        'norm2_g': gain(ks[6], (L, D_MODEL)),
        'w_in': nrm(ks[7], (L, D_MODEL, IN_COLS), D_MODEL ** -0.5),
        'swa_q_norm': gain(ks[8], (L, SWA_HEAD_DIM)),
        'swa_k_norm': gain(ks[9], (L, SWA_HEAD_DIM)),
        'swa_sinks': nrm(ks[10], (L, SWA_HEADS), 1.0),
        'mla_q_a_norm': gain(ks[11], (L, MLA_Q_RANK)),
        'mla_kv_a_norm': gain(ks[12], (L, MLA_KV_RANK)),
        'mla_w_uq': nrm(ks[13], (L, MLA_Q_RANK, MLA_HEADS * (MLA_NOPE_DIM + MLA_ROPE_DIM)), MLA_Q_RANK ** -0.5),
        'mla_w_ukv': nrm(ks[14], (L, MLA_KV_RANK, MLA_HEADS * (MLA_NOPE_DIM + MLA_V_DIM)), MLA_KV_RANK ** -0.5),
        'mla_q_norm': gain(ks[15], (L, MLA_NOPE_DIM + MLA_ROPE_DIM)),
        'mla_k_norm': gain(ks[16], (L, MLA_NOPE_DIM + MLA_ROPE_DIM)),
        'w_out': nrm(ks[17], (L, D_MIX, D_MODEL), D_MIX ** -0.5),
        'peer_w_query': nrm(ks[18], (L, D_MODEL, PEER_HEADS * PEER_KEY_DIM), D_MODEL ** -0.5),
        'peer_sub_keys': nrm(ks[19], (L, PEER_HEADS, 2, PEER_N_KEYS, PEER_KEY_DIM // 2), (PEER_KEY_DIM // 2) ** -0.5),
        'peer_u': nrm(ks[20], (L, PEER_N_EXPERTS, D_MODEL), D_MODEL ** -0.5),
        'peer_v': nrm(ks[21], (L, PEER_N_EXPERTS, D_MODEL), PEER_HEADS ** -0.5),
    }

def reference(x, c, positions, w_ada, b_ada, norm1_g, norm2_g, w_in,
              swa_q_norm, swa_k_norm, swa_sinks, mla_q_a_norm, mla_kv_a_norm,
              mla_w_uq, mla_w_ukv, mla_q_norm, mla_k_norm, w_out,
              peer_w_query, peer_sub_keys, peer_u, peer_v):
    for l in range(DEPTH):
        x = hybrid_layer(x, c, positions, w_ada[l], b_ada[l], norm1_g[l], norm2_g[l], w_in[l],
                         swa_q_norm[l], swa_k_norm[l], swa_sinks[l], mla_q_a_norm[l], mla_kv_a_norm[l],
                         mla_w_uq[l], mla_w_ukv[l], mla_q_norm[l], mla_k_norm[l], w_out[l],
                         peer_w_query[l], peer_sub_keys[l], peer_u[l], peer_v[l])
    return x


_drawn_inputs = setup_inputs


def setup_inputs(seed=0):
    import zlib

    import numpy as np

    out = dict(_drawn_inputs(seed))
    spreads = {}
    factors = {'norm1_g': 4.591,
     'swa_q_norm': 6.842,
     'swa_k_norm': 7.026,
     'mla_q_a_norm': 8.0,
     'mla_kv_a_norm': 4.289,
     'mla_q_norm': 8.0,
     'mla_k_norm': 8.0,
     'norm2_g': 5.47}
    for name, (base, spread) in spreads.items():
        noise = np.random.default_rng([zlib.crc32(name.encode()), seed]).standard_normal(out[name].shape)
        drawn = base * np.exp(spread * noise) if base else spread * noise
        out[name] = __import__('jax').numpy.asarray(drawn.astype(out[name].dtype))
    for name, factor in factors.items():
        out[name] = (out[name] * factor).astype(out[name].dtype)
    return out
```

```python
import concourse.bass as bass
from concourse import mybir
from concourse.alu_op_type import AluOpType as ALU
from contextlib import ExitStack

F32 = mybir.dt.float32
F32R = mybir.dt.float32r
I32 = mybir.dt.int32
U32 = mybir.dt.uint32
ACT = mybir.ActivationFunctionType
X = mybir.AxisListType.X

P = 128
D = 1024
T = 512
KD = D // P
TT = T // P
EPS = 1e-6
NEG = -1e30
SH, SKV, SD = 8, 2, 64
SG = SH // SKV
MH, NOPE, ROPE, VD = 8, 64, 32, 64
QK = NOPE + ROPE
QRANK, KVRANK = 256, 128
IN_COLS = SH * SD + 2 * SKV * SD + QRANK + KVRANK + ROPE
Z_K = SH * SD
Z_V = Z_K + SKV * SD
Z_CQ = Z_V + SKV * SD
Z_CKV = Z_CQ + QRANK
Z_KR = Z_CKV + KVRANK
ROPE_THETA = 10000.0
PH, NK, KTOP, PD = 8, 128, 16, 64
NT = NK
HB = 4
SOLO, BOTH, GP = 12, P // (2 * HB), 8
SEG = SOLO + BOTH
CH = 512
MASKED = 1e33
PW = 260

PI2_A, PI2_B, PI2_C = 6.28125, 0.0019350051879882812, 3.019916050e-07
ROUND = 12582912.0


def slope(h):
    return 2.0 ** (-8.0 * (h + 1) / SH)


def build(nc, xT, c, positions, position_cols, w_ada, b_ada, norm1_g, norm2_g, w_in, swa_q_norm, swa_k_norm,
          swa_sinks, mla_q_a_norm, mla_kv_a_norm, mla_w_uq, mla_w_ukv, mla_q_norm, mla_k_norm,
          w_out, peer_w_query, sub_keys, u_tiles, v_tiles, outT):
    ctx = ExitStack()
    with ctx:
        def sem(name):
            return ctx.enter_context(nc.semaphore(name))

        BASE = 16512
        END = 229344

        def region(start, entries):
            out, at = [], start
            for name, shape, dt in entries:
                size = 4
                for s in shape[1:]:
                    size *= s
                out.append(nc.alloc_sbuf_tensor_at(name, shape, dt, offset=at))
                at += (size + 31) // 32 * 32
            assert at <= END, (name, at - END)
            return out, at

        (res, ident, ones, iota, cT, b_cols, ada, g1, g2, gs), at0 = region(BASE, [
            ("res", [P, KD, T], F32),
            ("ident", [P, P], F32), ("ones", [P, P], F32), ("iota", [P, P], F32),
            ("cT", [P, KD], F32), ("b_cols", [P, 6 * KD], F32), ("ada", [P, 6 * KD], F32),
            ("g1", [P, KD], F32), ("g2", [P, KD], F32), ("gs", [P, KD], F32)])
        ring, at1 = region(at0, [(f"ring{i}", [P, KD, CH], F32) for i in range(3)])
        (hT,), at2 = region(at1, [("hT", [P, KD, T], F32)])
        (oT,), _ = region(at1, [("oT", [P, KD, T], F32)])
        (z, qTs, kcT, wuq, wukv, kvm, m2, distm, pb, qkT, g_swa, g_cq, g_ckv, g_mla, trig, posq,
         posqf, ss, rz, mss, mrz, nm, sm, rsm, sinks, freq), _ = region(at2, [
            ("z", [P, TT, IN_COLS], F32), ("qTs", [P, SG, T], F32), ("kcT", [P, 4, T], F32),
            ("wuq", [P, 2, MH * QK], F32), ("wukv", [P, MH * (NOPE + VD)], F32),
            ("kvm", [P, TT, MH * (NOPE + VD)], F32), ("m2", [P, 2, 2 * MH, QK], F32),
            ("distm", [P, TT, 256], F32), ("pb", [P, 4, 2, PW], F32), ("qkT", [P, 2 * MH, T], F32),
            ("g_swa", [P, SH + SKV, SD], F32), ("g_cq", [P, QRANK], F32), ("g_ckv", [P, KVRANK], F32),
            ("g_mla", [P, 2, QK], F32), ("trig", [P, TT, 2, ROPE // 2], F32), ("posq", [P, TT], I32),
            ("posqf", [P, TT], F32), ("ss", [P, TT, 12], F32), ("rz", [P, TT, 12], F32),
            ("mss", [P, 2 * MH], F32), ("mrz", [P, 2 * MH], F32), ("nm", [P, 4, 2], F32),
            ("sm", [P, 4, 2], F32), ("rsm", [P, 4, 2], F32), ("sinks", [P, SH], F32),
            ("freq", [P, ROPE // 2], F32)])
        pt = m2[:].rearrange("p a h d -> p (a h d)")[:, 0:1024].rearrange("p (a s q) -> p a s q", a=2, q=P)
        accs = m2[:].rearrange("p a h d -> p (a h d)")[:, 1024:2048].rearrange("p (a c) -> p a c", a=2)
        zsq = qkT[:].rearrange("p a t -> p (a t)")[:, 0:TT * 640].rearrange("p (t c) -> p t c", t=TT)
        zsq_cq = qkT[:].rearrange("p a t -> p (a t)")[:, TT * 640:TT * 640 + 384]
        msq = pb[:].rearrange("p a j k -> p (a j k)")[:, 0:2 * MH * QK].rearrange("p (h d) -> p h d", h=2 * MH)
        kvm_flat = kvm[:].rearrange("p t c -> p (t c)")
        posk_i = kvm_flat[:, 0:T].bitcast(I32)
        posk = kvm_flat[:, T:2 * T]
        ang = kvm_flat[:, 1024:1024 + TT * 32].rearrange("p (t s f) -> p t s f", t=TT, s=2)
        turns = kvm_flat[:, 1280:1280 + TT * 32].rearrange("p (t s f) -> p t s f", t=TT, s=2)
        ropet = [pb[:].rearrange("p a j k -> p (a j k)")[:, 256 * n:256 * n + 256].rearrange("p (h d) -> p h d", h=16) for n in range(4)]
        rstd1 = pb[:].rearrange("p a j k -> p (a j k)")[:, 0:T]
        (stage,), at_c = region(at0, [("stage", [P, NT, P], F32)])
        assert at_c == at2
        (qpT,), _ = region(at1, [("qpT", [P, PH, T], F32)])
        (h2hi, h2lo), at3 = region(at2, [("h2hi", [P, KD, T], F32R), ("h2lo", [P, KD, T], F32R)])
        (h2T,), at_h = region(at3, [("h2T", [P, KD, T], F32)])
        (skT, rstd2), at_h = region(at_h, [("skT", [P, PH, NK], F32), ("rstd2", [P, T], F32)])
        (sout0, sout1), at_h = region(at_h, [("sout0", [P, 2 * PH, NK], F32), ("sout1", [P, 2 * PH, NK], F32)])
        sout = (sout0, sout1)
        (s, sv, six, sixf, cand, best, bi, bia, abf, IJW, slots, eW, eS, eR, eqI), at_t = region(at3, [
            ("s", [P, 2 * PH, NK], F32), ("sv", [P, PH, 2, KTOP], F32), ("six", [P, PH, 2, KTOP], U32),
            ("sixf", [P, PH, 2, KTOP], F32), ("cand", [P, PH, KTOP, KTOP], F32),
            ("best", [P, PH, KTOP], F32), ("bi", [P, PH, KTOP], U32), ("bia", [P, 2, PH, KTOP], U32),
            ("abf", [P, 2, PH, KTOP], F32), ("IJW", [P, 3, PH, KTOP], F32), ("slots", [P, 5, P], F32),
            ("eW", [P, PH, KTOP], F32), ("eS", [P, PH], F32), ("eR", [P, PH], F32), ("eqI", [P, 2, HB, P], F32)])
        eq = s[:].rearrange("p a (b c) -> p (a b c)", c=16).rearrange("p (h k m) -> p h k m", h=PH, k=KTOP)
        ohJ, at_t = region(at_t, [(f"ohJ{b}", [P, HB, P], F32R) for b in range(2)])
        ohH, at_t = region(at_t, [(f"ohH{b}", [P, HB, P], F32R) for b in range(2)])
        ohL, at_t = region(at_t, [(f"ohL{b}", [P, HB, P], F32R) for b in range(2)])
        at4 = max(at_t, at_h)
        uraw, at4 = region(at4, [(f"uraw{b}", [P, D], F32) for b in range(2)])
        uhi, at4 = region(at4, [(f"uhi{b}", [P, D], F32R) for b in range(2)])
        ulo, at4 = region(at4, [(f"ulo{b}", [P, D], F32R) for b in range(2)])
        act_out, at4 = region(at4, [(f"act_out{b}", [P, T], F32) for b in range(2)])
        vraw, at_v = region(at0, [(f"vraw{b}", [P, D], F32) for b in range(4)])
        vhi, at_v = region(at_v, [(f"vhi{b}", [P, D], F32R) for b in range(4)])
        vlo, at_v = region(at_v, [(f"vlo{b}", [P, D], F32R) for b in range(4)])
        assert at_v <= at2
        gate, at5 = region(at3, [(f"gate{b}", [P, T], F32) for b in range(4)])
        act_in, at5 = region(at5, [(f"act_in{b}", [P, T], F32) for b in range(4)])
        cf, at5 = region(at5, [(f"cf{b}", [P, T], F32) for b in range(2)])
        chi, at5 = region(at5, [(f"chi{b}", [P, T], F32R) for b in range(4)])
        clo, at5 = region(at5, [(f"clo{b}", [P, T], F32R) for b in range(4)])
        assert at5 <= at_t

        ps = ctx.enter_context(nc.psum_tensor("ps", [P, 8, 512], F32))
        ada_ps = ps[:, 7, 0:6 * KD]
        gates = nc.dram_tensor("gates", (NT, P, T), F32).ap()
        gelus = nc.dram_tensor("gelus", (NT, P, T), F32).ap()
        keys = nc.dram_tensor("keys", (TT, P, 2 * PH * NK), F32).ap()

        x_in = sem("x_in")
        small_in = sem("small_in")
        up_in = sem("up_in")
        ring_in = [sem(f"ring_in{i}") for i in range(3)]
        ring_free = [sem(f"ring_free{i}") for i in range(3)]
        acc_done = sem("acc_done")
        const = sem("const")
        sq1 = sem("sq1")
        ms1 = sem("ms1")
        var1 = sem("var1")
        sd1 = sem("sd1")
        ada_done = sem("ada_done")
        h_scaled = sem("h_scaled")
        h_ready = sem("h_ready")
        z_ps = sem("z_ps")
        z_sb = sem("z_sb")
        z_stat = sem("z_stat")
        z_var = sem("z_var")
        z_sd = sem("z_sd")
        zn_ready = sem("zn_ready")
        zt_ps = sem("zt_ps")
        zt_sb = sem("zt_sb")
        up_ps = sem("up_ps")
        up_sb = sem("up_sb")
        m_built = sem("m_built")
        m_roped = sem("m_roped")
        m_sq = sem("m_sq")
        m_var = sem("m_var")
        m_sd = sem("m_sd")
        m_ready = sem("m_ready")
        mt_ps = sem("mt_ps")
        mt_sb = sem("mt_sb")
        ang_ready = sem("ang_ready")
        trig_ready = sem("trig_ready")
        s_done = sem("s_done")
        biased = sem("biased")
        exp_done = sem("exp_done")
        p_ready = sem("p_ready")
        pt_ps = sem("pt_ps")
        pt_sb = sem("pt_sb")
        o_ps = sem("o_ps")
        o_sb = sem("o_sb")
        mix_ps = sem("mix_ps")
        x1_ready = sem("x1_ready")
        sq2 = sem("sq2")
        ms2 = sem("ms2")
        var2 = sem("var2")
        sd2 = sem("sd2")
        h2_scaled = sem("h2_scaled")
        h2_ready = sem("h2_ready")
        h2_hi = sem("h2_hi")
        h2_split = sem("h2_split")
        sk_in = sem("sk_in")
        qp_ps = sem("qp_ps")
        qp_sb = sem("qp_sb")
        key_ps = sem("key_ps")
        key_sb = sem("key_sb")
        best_ready = sem("best_ready")
        best_exp = sem("best_exp")
        ijw_ready = sem("ijw_ready")
        ijw_ps = sem("ijw_ps")
        slots_ready = sem("slots_ready")
        oh_ready = sem("oh_ready")
        oh_used = sem("oh_used")
        g_sb = sem("g_sb")
        g_out = sem("g_out")
        s_copied = sem("s_copied")
        s_out = [sem(f"s_out{b}") for b in range(2)]
        s_in = sem("s_in")
        s_free = sem("s_free")
        eq_ready = sem("eq_ready")
        c_space = sem("c_space")
        u_in = [sem(f"u_in{b}") for b in range(2)]
        v_in = [sem(f"v_in{b}") for b in range(4)]
        gate_in = [sem(f"gate_in{b}") for b in range(4)]
        act_back = [sem(f"act_back{b}") for b in range(4)]
        u_hi = sem("u_hi")
        u_lo = sem("u_lo")
        a_ps = sem("a_ps")
        gelu_done = sem("gelu_done")
        a_out = [sem(f"a_out{b}") for b in range(2)]
        v_hi = sem("v_hi")
        v_lo = sem("v_lo")
        c_mul = sem("c_mul")
        c_hi = sem("c_hi")
        c_lo = sem("c_lo")
        y_ps = sem("y_ps")
        y_sb = sem("y_sb")
        out_done = sem("out_done")
        dve_step = sem("dve_step")
        act_step = sem("act_step")
        pool_step = sem("pool_step")

        chunks = []
        for kind, w, j0, n in (("ada", w_ada, 2, 2), ("ada", w_ada, 0, 2), ("in", w_in, 0, 3), ("ada", w_ada, 4, 2),
                               ("ada", w_ada, 8, 2), ("ada", w_ada, 6, 2), ("ada", w_ada, 10, 2),
                               ("out", w_out, 0, 2), ("query", peer_w_query, 0, 2)):
            for j in range(j0, j0 + n):
                chunks.append((kind, w, j, min(CH, w.shape[1] - j * CH)))
        ada_order = [j for kind, _, j, _ in chunks if kind == "ada"]
        place = {(kind, j): n for n, (kind, _, j, _) in enumerate(chunks)}
        NSMALL = 13
        units = [("s", b, kv, j) for b in range(TT) for kv in range(SKV) for j in (0, 2)] + \
                [("m", b, h, 0) for b in range(TT) for h in range(MH)]
        NU = len(units)

        def heads_of(kind):
            return 2 if kind == "s" else 1

        def key_tiles(kind, b):
            if kind == "s":
                return [b] if b == 0 else [b - 1, b]
            return list(range(b + 1))

        def p_view(u, kind):
            if kind == "s":
                return pb[:, u % 4, :, :]
            return pb[:, u % 4, :, :].rearrange("p j k -> p (j k)")[:, 0:512].unsqueeze(1)

        def pt_slots(kind, b):
            if kind == "s":
                return [(2 * j + kb - (b - 1), j, (kb - (b - 1)) * P, kb) for j in range(2) for kb in key_tiles(kind, b)]
            return [(kb, 0, kb * P, kb) for kb in key_tiles(kind, b)]

        block = ctx.enter_context(nc.Block())

        @block.sync
        def _(sp):
            sp.dma_start(res[:], xT).then_inc(x_in, 16)

            def load_chunk(n):
                if n >= 3:
                    sp.wait_ge(ring_free[n % 3], n // 3)
                _, w, j, cols = chunks[n]
                sp.dma_start(ring[n % 3][:, :, 0:cols],
                             w[:, j * CH:j * CH + cols].rearrange("(k p) n -> p k n", p=P)).then_inc(ring_in[n % 3], 16)

            for n in range(3):
                load_chunk(n)
            for n in range(3, len(chunks)):
                load_chunk(n)
            sp.wait_ge(mix_ps, KD)
            sp.dma_start(skT[:], sub_keys).then_inc(sk_in, 16)

            def load_u(n, r):
                sp.wait_ge(u_lo, n + 1)
                sp.dma_start(uraw[r % 2][:], u_tiles[bass.ds(n, 1), :, :].rearrange("a p c -> p (a c)")).then_inc(u_in[r % 2], 16)

            load_u(0, 0)
            load_u(1, 1)
            for tt in range(TT):
                sp.wait_ge(s_copied, tt + 1)
                sp.dma_start(keys[tt], sout[tt % 2][:].rearrange("p a n -> p (a n)")).then_inc(s_out[tt % 2], 16)
            for b in range(2):
                sp.wait_ge(s_out[b], 16 * TT // 2)
            sp.wait_ge(h2_split, KD)
            sp.dma_start(s[:].rearrange("p a n -> p (a n)"), keys[0]).then_inc(s_in, 16)

            def load_us(first, steps):
                with sp.Fori(0, steps // 4) as i:
                    for r in range(4):
                        load_u(first + i * 4 + (r + 2), r)

            load_us(0, SOLO)
            with sp.Fori(0, TT - 1) as tt:
                sp.wait_ge(s_free, tt + 1)
                sp.dma_start(s[:].rearrange("p a n -> p (a n)"),
                             keys[bass.ds(tt + 1, 1), :, :].rearrange("a p c -> p (a c)")).then_inc(s_in, 16)
                load_us(tt * SEG + SOLO, SEG)
            load_us((TT - 1) * SEG + SOLO, SEG)
            for n in range(TT * SEG + SOLO + 2, NT):
                load_u(n, n)

            sp.wait_ge(g_out, 16 * GP * (TT + 1))
            sp.wait_ge(c_space, TT)

            def load_v(n, r, first):
                if not first:
                    sp.wait_ge(v_lo, n - 3)
                sp.dma_start(vraw[r][:], v_tiles[bass.ds(n, 1), :, :].rearrange("a p c -> p (a c)")).then_inc(v_in[r], 16)
                if not first:
                    sp.wait_ge(c_mul, n - 3)
                sp.dma_start(gate[r][:], gates[bass.ds(n, 1), :, :].rearrange("a p c -> p (a c)")).then_inc(gate_in[r], 16)
                sp.dma_start(act_in[r][:], gelus[bass.ds(n, 1), :, :].rearrange("a p c -> p (a c)")).then_inc(act_back[r], 16)

            for b in range(2):
                sp.wait_ge(a_out[b], 16 * 3)
            for r in range(4):
                load_v(r, r, True)
            for b in range(2):
                sp.wait_ge(a_out[b], 16 * (NT // 2 + 1))
            with sp.Fori(1, NT // 4) as i:
                for r in range(4):
                    load_v(i * 4 + r, r, False)
            for d in range(KD):
                sp.wait_ge(y_sb, d + 1)
                sp.dma_start(outT[d], res[:, d, :]).then_inc(out_done, 16)
            sp.wait_ge(out_done, 16 * KD)
        @block.gpsimd
        def _(pool):
            nc.gpsimd.memset(ones[:], 1.0).then_inc(const, 1)
            nc.gpsimd.iota(iota[:], pattern=[[1, P]], base=0, channel_multiplier=0,
                           allow_small_or_imprecise_dtypes=True).then_inc(const, 1)
            nc.gpsimd.memset(ident[:], 0.0).then_inc(pool_step, 1)
            pool.wait_ge(pool_step, 1)
            nc.gpsimd.affine_select(out=ident[:], in_=ident[:], compare_op=ALU.not_equal, fill=1.0, base=0,
                                    pattern=[[-1, P]], channel_multiplier=1).then_inc(const, 1)
            for tt in range(TT):
                pool.wait_ge(up_sb, tt + 1)
                mk = m2[:, tt % 2, MH:2 * MH, :]
                nc.gpsimd.tensor_copy(mk[:, :, 0:NOPE],
                                      kvm[:, tt, :].rearrange("p (h c) -> p h c", h=MH)[:, :, 0:NOPE])
                nc.gpsimd.tensor_copy(mk[:, :, NOPE:QK],
                                      z[:, tt, Z_KR:Z_KR + ROPE].unsqueeze(1).to_broadcast([P, MH, ROPE])).then_inc(m_built, 1)
            pool.sem_inc(u_lo, 2)

            def split_u(n, r):
                pool.wait_ge(u_hi, n + 1)
                nc.gpsimd.tensor_tensor(ulo[r % 2][:], uraw[r % 2][:], uhi[r % 2][:].bitcast(F32), ALU.subtract).then_inc(u_lo, 1)

            with pool.Fori(0, NT // 4) as i:
                for r in range(4):
                    split_u(i * 4 + r, r)

        @block.scalar
        def _(act):
            steps = [0]

            def settled(ins):
                steps[0] += 1
                ins.then_inc(act_step, 1)
                act.wait_ge(act_step, steps[0])

            act.sem_inc(gelu_done, 2)
            act.sem_inc(g_sb, 2)
            act.sem_inc(g_out, 16 * GP)
            for b in range(2):
                act.sem_inc(a_out[b], 16)
            act.dma_start(cT[:], c).then_inc(small_in, 16)
            act.dma_start(b_cols[:], b_ada).then_inc(small_in, 16)
            act.dma_start(g1[:], norm1_g).then_inc(small_in, 16)
            act.dma_start(g2[:], norm2_g).then_inc(small_in, 16)
            act.dma_start(posq[:], position_cols).then_inc(small_in, 16)
            act.dma_start(g_swa[:, 0, :], swa_q_norm.partition_broadcast(P)).then_inc(small_in, 16)
            act.dma_start(g_swa[:, SH, :], swa_k_norm.partition_broadcast(P)).then_inc(small_in, 16)
            act.dma_start(g_cq[:], mla_q_a_norm.partition_broadcast(P)).then_inc(small_in, 16)
            act.dma_start(g_ckv[:], mla_kv_a_norm.partition_broadcast(P)).then_inc(small_in, 16)
            act.dma_start(g_mla[:, 0, :], mla_q_norm.partition_broadcast(P)).then_inc(small_in, 16)
            act.dma_start(g_mla[:, 1, :], mla_k_norm.partition_broadcast(P)).then_inc(small_in, 16)
            act.dma_start(sinks[:], swa_sinks.partition_broadcast(P)).then_inc(small_in, 16)
            act.dma_start(posk_i, positions.partition_broadcast(P)).then_inc(small_in, 16)
            act.dma_start(wuq[:], mla_w_uq.rearrange("(k p) n -> p k n", p=P)).then_inc(up_in, 16)
            act.dma_start(wukv[:], mla_w_ukv).then_inc(up_in, 16)
            act.wait_ge(x_in, 16)
            for k in range(KD):
                nc.scalar.activation(hT[:, k, :], res[:, k, :], ACT.Square).then_inc(sq1, 1)
            act.wait_ge(var1, 1)
            nc.scalar.activation(rstd1, rstd1, ACT.Sqrt).then_inc(sd1, 1)
            for k in range(KD):
                act.wait_ge(h_scaled, k + 1)
                nc.scalar.activation(hT[:, k, :], hT[:, k, :], ACT.Identity, bias=ada[:, k:k + 1]).then_inc(h_ready, 1)
            for n in range(3):
                if n == 1:
                    act.wait_ge(ang_ready, 1)
                    nc.scalar.activation(trig[:].rearrange("p t s f -> p (t s f)"), kvm_flat[:, 1024:1024 + TT * 32],
                                         ACT.Sin).then_inc(trig_ready, 1)
                cols = chunks[place["in", n]][3]
                for tt in range(TT):
                    q = n * TT + tt
                    act.wait_ge(z_ps, q + 1)
                    dst, src = z[:, tt, n * CH:n * CH + cols], ps[:, q % 6, 0:cols]
                    if n == 0:
                        dst = dst.rearrange("p (g v d) -> p v g d", v=SKV, g=SG)
                        src = src.rearrange("p (v g d) -> p v g d", v=SKV, g=SG)
                    nc.scalar.activation(dst, src, ACT.Copy).then_inc(z_sb, 1)
                    act.wait_ge(z_sb, q + 1)
                    if n == 1:
                        nc.scalar.activation(zsq[:, tt, :], z[:, tt, 0:640], ACT.Square).then_inc(z_stat, 1)
                    if n == 2:
                        settled(nc.scalar.activation(zsq_cq[:, 0:QRANK], z[:, tt, Z_CQ:Z_CKV], ACT.Square,
                                                     accum_out=ss[:, tt, 10:11]))
                        nc.scalar.activation(zsq_cq[:, QRANK:QRANK + KVRANK], z[:, tt, Z_CKV:Z_KR], ACT.Square,
                                             accum_out=ss[:, tt, 11:12]).then_inc(z_stat, 1)
            act.wait_ge(z_var, 1)
            nc.scalar.activation(rz[:], rz[:], ACT.Sqrt).then_inc(z_sd, 1)
            for tt in range(TT):
                act.wait_ge(zt_ps, tt + 1)
                cols = slice(tt * P, (tt + 1) * P)
                b0 = 2 * (tt % 2)
                nc.scalar.activation(qTs[:, :, cols], ps[:, b0, :].rearrange("p (g t) -> p g t", g=SG), ACT.Copy)
                nc.scalar.activation(kcT[:, :, cols], ps[:, b0 + 1, :].rearrange("p (g t) -> p g t", g=4),
                                     ACT.Copy).then_inc(zt_sb, 1)
            def copy_projections(tt):
                act.wait_ge(up_ps, tt + 1)
                if tt >= 2:
                    act.wait_ge(mt_ps, 4 * (tt - 1))
                mq = m2[:, tt % 2, :, :].rearrange("p h d -> p (h d)")
                nc.scalar.activation(mq[:, 0:512], ps[:, 0, :], ACT.Copy)
                nc.scalar.activation(mq[:, 512:768], ps[:, 1, 0:256], ACT.Copy)
                nc.scalar.activation(kvm[:, tt, :], ps[:, 2:4, :].rearrange("p a b -> p (a b)"), ACT.Copy).then_inc(up_sb, 1)

            copy_projections(0)
            for tt in range(TT):
                if tt + 1 < TT:
                    copy_projections(tt + 1)
                act.wait_ge(m_roped, tt + 1)
                nc.scalar.activation(msq, m2[:, tt % 2, :, :], ACT.Square).then_inc(m_sq, 1)
                act.wait_ge(m_var, tt + 1)
                nc.scalar.activation(mrz[:], mrz[:], ACT.Sqrt).then_inc(m_sd, 1)
                for f in range(4):
                    act.wait_ge(mt_ps, 4 * tt + f + 1)
                    nc.scalar.activation(qkT[0:QK, 4 * f:4 * f + 4, tt * P:(tt + 1) * P],
                                         ps[0:QK, 4 + f % 2, :].rearrange("p (h t) -> p h t", h=4), ACT.Copy).then_inc(mt_sb, 1)

            def exponentials(u):
                kind, b, _, _ = units[u]
                act.wait_ge(biased, u + 1)
                nk = len(key_tiles(kind, b)) * P
                for j in range(heads_of(kind)):
                    if kind == "s":
                        src = pb[:, u % 4, j, 256 - nk:257]
                        dst = src
                    else:
                        src = ps[:, u % 3, 0:nk]
                        dst = p_view(u, kind)[:, 0, 0:nk]
                    last = nc.scalar.activation(dst, src, ACT.Exp, bias=nm[:, u % 4, j:j + 1], scale=1.0,
                                                accum_out=sm[:, u % 4, j:j + 1])
                last.then_inc(exp_done, 1)

            def copy_pt(u):
                kind, b, _, _ = units[u]
                act.wait_ge(pt_ps, u + 1)
                if u >= 2:
                    act.wait_ge(o_ps, u - 1)
                slots_ = slice(0, 4) if kind == "s" and b > 0 else slice(1, 4, 2) if kind == "s" else slice(0, b + 1)
                nc.scalar.activation(pt[:, u % 2, slots_, :], ps[:, 4 + u % 2, :].rearrange("p (s q) -> p s q", q=P)[:, slots_, :],
                                     ACT.Copy).then_inc(pt_sb, 1)

            exponentials(0)
            for u in range(NU):
                if u + 1 < NU:
                    exponentials(u + 1)
                copy_pt(u)
            for k in range(KD):
                act.wait_ge(x1_ready, k + 1)
                nc.scalar.activation(h2T[:, k, :], res[:, k, :], ACT.Square).then_inc(sq2, 1)
            act.wait_ge(var2, 1)
            nc.scalar.activation(rstd2[:], rstd2[:], ACT.Sqrt).then_inc(sd2, 1)
            for k in range(KD):
                act.wait_ge(h2_scaled, k + 1)
                nc.scalar.activation(h2T[:, k, :], h2T[:, k, :], ACT.Identity, bias=ada[:, 3 * KD + k:3 * KD + k + 1])\
                    .then_inc(h2_ready, 1)
            for k in range(KD):
                act.wait_ge(h2_ready, k + 1)
                nc.scalar.activation(h2hi[:, k, :], h2T[:, k, :], ACT.Copy).then_inc(h2_hi, 1)
            for h in range(PH):
                act.wait_ge(qp_ps, h + 1)
                nc.scalar.activation(qpT[:, h, :], ps[:, h % 4, :], ACT.Copy).then_inc(qp_sb, 1)

            def high_u(n, r, count):
                act.wait_ge(u_in[r % 2], count)
                act.wait_ge(a_ps, n + 1)
                nc.scalar.activation(uhi[r % 2][:], uraw[r % 2][:], ACT.Copy).then_inc(u_hi, 1)

            for n in range(2):
                high_u(n, n, 16)
            for tt in range(TT):
                act.wait_ge(key_ps, tt + 1)
                if tt >= 2:
                    act.wait_ge(s_out[tt % 2], 16)
                for f in range(4):
                    last = nc.scalar.activation(sout[tt % 2][:, 4 * f:4 * f + 4, :],
                                                ps[:, 4 + f, :].rearrange("p (a n) -> p a n", n=NK), ACT.Copy)
                last.then_inc(s_copied, 1)

            def gelu(n, r, count):
                act.wait_ge(a_ps, n + 3)
                act.wait_ge(a_out[r % 2], count)
                nc.scalar.activation(act_out[r % 2][:], ps[:, r % 2, :], ACT.Gelu).then_inc(gelu_done, 1)
                act.wait_ge(gelu_done, n + 3)
                act.dma_start(gelus[bass.ds(n, 1), :, :].rearrange("a p c -> p (a c)"), act_out[r % 2][:]).then_inc(a_out[r % 2], 16)

            def copy_gates(q, col, half):
                act.wait_ge(oh_used, q + 3)
                nc.scalar.activation(stage[:].rearrange("p i t -> p t i")[:, bass.ds(col, HB), :],
                                     ps[:, 2 + half, :].rearrange("p (t i) -> p t i", i=NT), ACT.Copy).then_inc(g_sb, 1)

            def alone(first, pair, steps, send):
                with act.Fori(0, steps // 4) as i:
                    for r in range(4):
                        pairs = i * 2 + (pair + r // 2)
                        high_u(i * 4 + (first + r + 2), r, pairs * 16 + 32)
                        gelu(i * 4 + (first + r), r, pairs * 16 + 16)
                        if send is not None:
                            rows = bass.ds(i * (4 * P // GP) + r * (P // GP), P // GP)
                            act.dma_start(gates[rows, :, bass.ds(send * P, P)].rearrange("i j t -> j i t"),
                                          stage[:, rows, :]).then_inc(g_out, 16)

            def weights():
                nc.scalar.activation(eW[:], eW[:], ACT.Exp).then_inc(best_exp, 1)

            def segment(tt):
                first_half = tt * (SEG // 2) + SOLO // 2
                act.wait_ge(g_out, tt * (16 * GP) + 16 * GP)
                with act.Fori(0, BOTH // 4) as i:
                    for r in range(4):
                        n, pairs = i * 4 + (tt * SEG + (SOLO + r)), i * 2 + (first_half + r // 2)
                        high_u(n + 2, r, pairs * 16 + 32)
                        gelu(n, r, pairs * 16 + 16)
                        for half in range(2):
                            copy_gates(i * 8 + (tt * (2 * BOTH) + (2 * r + half)), i * (8 * HB) + HB * (2 * r + half), half)
                act.wait_ge(g_sb, tt * (2 * BOTH) + (2 * BOTH + 2))

            alone(0, 0, GP, None)
            act.wait_ge(best_ready, 1)
            weights()
            alone(GP, GP // 2, SOLO - GP, None)
            with act.Fori(0, TT - 1) as tt:
                segment(tt)
                first, pair = tt * SEG + (SOLO + BOTH), tt * (SEG // 2) + (SOLO + BOTH) // 2
                alone(first, pair, GP, tt)
                act.wait_ge(best_ready, tt + 2)
                weights()
                alone(first + GP, pair + GP // 2, SOLO - GP, None)
            segment(TT - 1)
            alone(TT * SEG, TT * SEG // 2, GP, TT - 1)
            alone(TT * SEG + GP, (TT * SEG + GP) // 2, SOLO - GP, None)
            for n in range(NT - 4, NT):
                if n + 2 < NT:
                    high_u(n + 2, n, n // 2 * 16 + 32)
                gelu(n, n, n // 2 * 16 + 16)

            def high_v(n, r, count, first):
                act.wait_ge(v_in[r], count)
                if not first:
                    act.wait_ge(y_ps, n - 3)
                nc.scalar.activation(vhi[r][:], vraw[r][:], ACT.Copy).then_inc(v_hi, 1)

            for r in range(4):
                high_v(r, r, 16, True)
            with act.Fori(1, NT // 4) as i:
                for r in range(4):
                    high_v(i * 4 + r, r, i * 16 + 16, False)

        @block.tensor
        def _(pe):
            def arrived(n):
                pe.wait_ge(ring_in[n % 3], 16 * (n // 3 + 1))

            def modulation(j):
                n = place["ada", j]
                order = ada_order.index(j)
                pe.wait_ge(acc_done, order + 1)
                for q in range(CH // P):
                    col = j * (CH // P) + q
                    last = nc.tensor.matmul(ada_ps[:, col:col + 1], accs[:, order % 2, q * P:(q + 1) * P],
                                            ones[:, 0:1], start=True, stop=True)
                last.then_inc(ada_done, 1)

            pe.sem_inc(oh_used, 2)
            pe.sem_inc(a_ps, 2)
            pe.wait_ge(const, 3)
            for k in range(KD):
                pe.wait_ge(sq1, k + 1)
                last = nc.tensor.matmul(ps[:, 6, :], ones[:], hT[:, k, :], start=(k == 0), stop=(k == KD - 1))
            last.then_inc(ms1, 1)
            for j in ada_order[:4]:
                modulation(j)
            pe.wait_ge(h_ready, KD)
            for n in range(3):
                at = place["in", n]
                arrived(at)
                cols = chunks[at][3]
                for tt in range(TT):
                    q = n * TT + tt
                    if q >= 6:
                        pe.wait_ge(z_sb, q - 5)
                    for k in range(KD):
                        last = nc.tensor.matmul(ps[:, q % 6, 0:cols], hT[:, k, tt * P:(tt + 1) * P],
                                                ring[at % 3][:, k, 0:cols], start=(k == 0), stop=(k == KD - 1))
                    last.then_inc(z_ps, 1)
                pe.wait_ge(z_ps, n * TT + TT)
                pe.sem_inc(ring_free[at % 3], 1)
            modulation(ada_order[4])
            for tt in range(TT):
                pe.wait_ge(zn_ready, tt + 1)
                if tt == 0:
                    pe.wait_ge(z_sb, 3 * TT)
                if tt >= 2:
                    pe.wait_ge(zt_sb, tt - 1)
                b0 = 2 * (tt % 2)
                for g in range(SG):
                    nc.tensor.transpose(ps[:, b0, g * P:(g + 1) * P], z[:, tt, g * P:(g + 1) * P], ident[:])
                for f, c0 in enumerate((Z_K, Z_CQ, Z_CQ + P, Z_CKV)):
                    last = nc.tensor.transpose(ps[:, b0 + 1, f * P:(f + 1) * P], z[:, tt, c0:c0 + P], ident[:])
                last.then_inc(zt_ps, 1)
            pe.wait_ge(up_in, 32)
            pe.wait_ge(zt_sb, TT)

            def project(tt):
                cols = slice(tt * P, (tt + 1) * P)
                if tt >= 1:
                    pe.wait_ge(up_sb, tt)
                for bank, c0, n in ((0, 0, 512), (1, 512, 256)):
                    for k in range(2):
                        nc.tensor.matmul(ps[:, bank, 0:n], kcT[:, 1 + k, cols], wuq[:, k, c0:c0 + n],
                                         start=(k == 0), stop=(k == 1))
                for bank, c0 in ((2, 0), (3, 512)):
                    last = nc.tensor.matmul(ps[:, bank, :], kcT[:, 3, cols], wukv[:, c0:c0 + 512], start=True, stop=True)
                last.then_inc(up_ps, 1)

            def turn_heads(tt):
                pe.wait_ge(m_ready, tt + 1)
                for f in range(4):
                    if 4 * tt + f >= 2:
                        pe.wait_ge(mt_sb, 4 * tt + f - 1)
                    for h in range(4):
                        last = nc.tensor.transpose(ps[0:QK, 4 + f % 2, h * P:(h + 1) * P], m2[:, tt % 2, 4 * f + h, :], ident[:])
                    last.then_inc(mt_ps, 1)

            project(0)
            for tt in range(TT):
                if tt + 1 < TT:
                    project(tt + 1)
                turn_heads(tt)
            pe.wait_ge(mt_sb, 4 * TT)

            def scores(u):
                kind, b, sub, j0 = units[u]
                if u >= 3:
                    pe.wait_ge(exp_done, u - 2)
                q = slice(b * P, (b + 1) * P)
                tiles = key_tiles(kind, b)
                keys_ = slice(tiles[0] * P, (b + 1) * P)
                if kind == "s":
                    rows = slice(sub * SD, (sub + 1) * SD)
                    for j in range(2):
                        c0 = j * 256 + (256 - len(tiles) * P)
                        last = nc.tensor.matmul(ps[:, u % 3, c0:c0 + len(tiles) * P], qTs[rows, j0 + j, q], kcT[rows, 0, keys_],
                                                start=True, stop=True)
                else:
                    last = nc.tensor.matmul(ps[:, u % 3, 0:len(tiles) * P], qkT[0:QK, sub, q], qkT[0:QK, MH + sub, keys_],
                                            start=True, stop=True)
                last.then_inc(s_done, 1)

            def transposes(u):
                kind, b, _, _ = units[u]
                pe.wait_ge(p_ready, u + 1)
                if u >= 2:
                    pe.wait_ge(pt_sb, u - 1)
                for slot, j, c0, _ in pt_slots(kind, b):
                    last = nc.tensor.transpose(ps[:, 4 + u % 2, slot * P:(slot + 1) * P],
                                               p_view(u, kind)[:, j, c0:c0 + P], ident[:])
                last.then_inc(pt_ps, 1)

            def values(u):
                kind, b, sub, j0 = units[u]
                pe.wait_ge(pt_sb, u + 1)
                if u >= 2:
                    pe.wait_ge(o_sb, u - 1)
                tiles = key_tiles(kind, b)
                for slot, j, _, kb in pt_slots(kind, b):
                    half = j if kind == "s" else sub % 2
                    if kind == "s":
                        v = z[:, kb, Z_V + sub * SD:Z_V + (sub + 1) * SD]
                    else:
                        v0 = sub * (NOPE + VD) + NOPE
                        v = kvm[:, kb, v0:v0 + VD]
                    last = nc.tensor.matmul(ps[64 * half:64 * half + 64, 3 * (u % 2) + 3, 0:P], v, pt[:, u % 2, slot, :],
                                            start=(kb == tiles[0]), stop=(kb == tiles[-1]))
                last.then_inc(o_ps, 1)

            rest = ada_order[5:]
            scores(0)
            scores(1)
            for u in range(NU):
                if u + 2 < NU:
                    scores(u + 2)
                transposes(u)
                if u >= 1:
                    values(u - 1)
                if u % 6 == 5 and rest:
                    modulation(rest.pop(0))
            values(NU - 1)
            assert not rest
            pe.wait_ge(o_sb, NU)
            for m in range(KD):
                n = place["out", m // 4]
                arrived(n)
                if m >= 4:
                    pe.wait_ge(x1_ready, m - 3)
                for k in range(KD):
                    last = nc.tensor.matmul(ps[:, m % 4, :], ring[n % 3][:, k, (m % 4) * P:(m % 4 + 1) * P],
                                            oT[:, k, :], start=(k == 0), stop=(k == KD - 1))
                last.then_inc(mix_ps, 1)
                if m % 4 == 3:
                    pe.wait_ge(mix_ps, m + 1)
                    pe.sem_inc(ring_free[n % 3], 1)
            for k in range(KD):
                pe.wait_ge(sq2, k + 1)
                last = nc.tensor.matmul(ps[:, 5, :], ones[:], h2T[:, k, :], start=(k == 0), stop=(k == KD - 1))
            last.then_inc(ms2, 1)
            pe.wait_ge(h2_ready, KD)
            for h in range(PH):
                n = place["query", h // 4]
                arrived(n)
                if h >= 4:
                    pe.wait_ge(qp_sb, h - 3)
                for k in range(KD):
                    last = nc.tensor.matmul(ps[:, h % 4, :], ring[n % 3][:, k, (h % 4) * P:(h % 4 + 1) * P],
                                            h2T[:, k, :], start=(k == 0), stop=(k == KD - 1))
                last.then_inc(qp_ps, 1)
                if h % 4 == 3:
                    pe.wait_ge(qp_ps, h + 1)
                    pe.sem_inc(ring_free[n % 3], 1)
            pe.wait_ge(sk_in, 16)
            pe.wait_ge(qp_sb, PH)

            def key_scores(tt):
                for h in range(PH):
                    for half in range(2):
                        rows = slice(PD * half, PD * (half + 1))
                        last = nc.tensor.matmul(ps[:, 4 + 2 * half + h // 4, (h % 4) * P:(h % 4 + 1) * P],
                                                qpT[rows, h, tt * P:(tt + 1) * P], skT[rows, h, :], start=True, stop=True)
                last.then_inc(key_ps, 1)

            for tt in range(TT):
                if tt >= 1:
                    pe.wait_ge(s_copied, tt)
                key_scores(tt)

            pe.wait_ge(h2_split, KD)
            pe.wait_ge(s_copied, TT)

            def dot(n, r):
                pe.wait_ge(u_lo, n + 3)
                pe.wait_ge(gelu_done, n + 1)
                for k in range(KD):
                    cols = slice(k * P, (k + 1) * P)
                    nc.tensor.matmul(ps[:, r % 2, :], uhi[r % 2][:, cols], h2hi[:, k, :], start=(k == 0), stop=False)
                    nc.tensor.matmul(ps[:, r % 2, :], uhi[r % 2][:, cols], h2lo[:, k, :], start=False, stop=False)
                    last = nc.tensor.matmul(ps[:, r % 2, :], ulo[r % 2][:, cols], h2hi[:, k, :], start=False, stop=(k == KD - 1))
                last.then_inc(a_ps, 1)

            def token_gates(q, half):
                pe.wait_ge(oh_ready, q + 1)
                pe.wait_ge(g_sb, q + 1)
                for t in range(HB):
                    out = ps[:, 2 + half, t * P:(t + 1) * P]
                    nc.tensor.matmul(out, ohJ[half][:, t, :], ohH[half][:, t, :], start=True, stop=False)
                    last = nc.tensor.matmul(out, ohJ[half][:, t, :], ohL[half][:, t, :], start=False, stop=True)
                last.then_inc(oh_used, 1)

            def dots(first, steps):
                with pe.Fori(0, steps // 4) as i:
                    for r in range(4):
                        dot(i * 4 + (first + r), r)

            dots(0, SOLO)
            with pe.Fori(0, TT) as tt:
                pe.wait_ge(ijw_ready, tt + 1)
                for f in range(3):
                    last = nc.tensor.transpose(ps[:, 4, f * P:(f + 1) * P], IJW[:, f, :, :], ident[:])
                last.then_inc(ijw_ps, 1)
                with pe.Fori(0, BOTH // 4) as i:
                    for r in range(4):
                        dot(tt * SEG + i * 4 + (SOLO + r), r)
                        for half in range(2):
                            token_gates(tt * (2 * BOTH) + i * 8 + (2 * r + half), half)
                pe.wait_ge(oh_used, tt * (2 * BOTH) + (2 * BOTH + 2))
                pe.sem_inc(c_space, 1)
                dots(tt * SEG + (SOLO + BOTH), SOLO)
            dots(TT * SEG + SOLO, NT - TT * SEG - SOLO)

            def mix(n, r, first, last_tile):
                pe.wait_ge(v_lo, n + 1)
                pe.wait_ge(c_lo, n + 1)
                for d in range(KD):
                    cols = slice(d * P, (d + 1) * P)
                    nc.tensor.matmul(ps[:, d, :], vhi[r][:, cols], chi[r][:], start=first, stop=False)
                    nc.tensor.matmul(ps[:, d, :], vhi[r][:, cols], clo[r][:], start=False, stop=False)
                    last = nc.tensor.matmul(ps[:, d, :], vlo[r][:, cols], chi[r][:], start=False, stop=last_tile)
                last.then_inc(y_ps, 1)

            pe.wait_ge(gelu_done, NT + 2)
            for r in range(4):
                mix(r, r, r == 0, False)
            with pe.Fori(1, NT // 4 - 1) as i:
                for r in range(4):
                    mix(i * 4 + r, r, False, False)
            for n in range(NT - 4, NT):
                mix(n, n % 4, False, n == NT - 1)

        @block.vector
        def _(dve):
            steps = [0]

            def settled(ins):
                steps[0] += 1
                ins.then_inc(dve_step, 1)
                dve.wait_ge(dve_step, steps[0])

            tt_ = nc.vector.tensor_tensor
            def norm(bank, rstd, sums, var, sd):
                dve.wait_ge(sums, 1)
                nc.vector.tensor_scalar(rstd, ps[:, bank, :], 1.0 / D, EPS, ALU.mult, ALU.add).then_inc(var, 1)
                dve.wait_ge(sd, 1)
                settled(nc.vector.reciprocal(rstd, rstd))

            def modulate(j):
                n = place["ada", j]
                order = ada_order.index(j)
                dve.wait_ge(ring_in[n % 3], 16 * (n // 3 + 1))
                if order >= 2:
                    dve.wait_ge(ada_done, order - 1)
                acc = accs[:, order % 2, :]
                settled(nc.vector.tensor_scalar(acc, ring[n % 3][:, 0, :], cT[:, 0:1], None, ALU.mult))
                for k in range(1, KD):
                    settled(nc.vector.scalar_tensor_tensor(out=acc, in0=ring[n % 3][:, k, :], scalar=cT[:, k:k + 1],
                                                           in1=acc, op0=ALU.mult, op1=ALU.add))
                dve.sem_inc(ring_free[n % 3], 1)
                dve.sem_inc(acc_done, 1)

            def modulation(piece, chunks_done):
                dve.wait_ge(ada_done, chunks_done)
                cols = slice(piece * KD, (piece + 1) * KD)
                settled(tt_(ada[:, cols], ada_ps[:, cols], b_cols[:, cols], ALU.add))

            dve.wait_ge(small_in, 16 * NSMALL)
            norm(6, rstd1, ms1, var1, sd1)
            for j in ada_order[:4]:
                modulate(j)
            modulation(1, 4)
            settled(nc.vector.scalar_tensor_tensor(out=gs[:], in0=ada[:, KD:2 * KD], scalar=1.0, in1=g1[:],
                                                   op0=ALU.add, op1=ALU.mult))
            modulation(0, 4)
            for k in range(KD):
                nc.vector.scalar_tensor_tensor(out=hT[:, k, :], in0=res[:, k, :], scalar=gs[:, k:k + 1], in1=rstd1,
                                               op0=ALU.mult, op1=ALU.mult).then_inc(h_scaled, 1)
            for f in range(ROPE // 2):
                last = nc.vector.memset(freq[:, f:f + 1], ROPE_THETA ** (-2.0 * f / ROPE))
            settled(last)
            settled(nc.vector.tensor_scalar(g_swa[:, 0, :], g_swa[:, 0, :], SD ** -0.5, None, ALU.mult))
            nc.vector.tensor_copy(g_swa[:, 1:SH, :], g_swa[:, 0, :].unsqueeze(1).to_broadcast([P, SH - 1, SD]))
            nc.vector.tensor_copy(g_swa[:, SH + 1, :], g_swa[:, SH, :])
            nc.vector.tensor_scalar(g_mla[:, 0, :], g_mla[:, 0, :], QK ** -0.5, None, ALU.mult)
            nc.vector.tensor_copy(posk, posk_i)
            settled(nc.vector.tensor_copy(posqf[:], posq[:]))
            for sc in range(2):
                settled(tt_(ang[:, :, sc, :], posqf[:].unsqueeze(2).to_broadcast([P, TT, ROPE // 2]),
                            freq[:].unsqueeze(1).to_broadcast([P, TT, ROPE // 2]), ALU.mult))
                nc.vector.tensor_scalar(turns[:, :, sc, :], ang[:, :, sc, :], 0.15915494309189535,
                                        0.25 if sc == 0 else 0.0, ALU.mult, ALU.add)
            settled(nc.vector.memset(sm[:], 0.0))
            settled(nc.vector.tensor_scalar(turns, turns, ROUND, None, ALU.add))
            settled(nc.vector.tensor_scalar(turns, turns, ROUND, None, ALU.subtract))
            for part in (PI2_A, PI2_B, PI2_C):
                settled(nc.vector.scalar_tensor_tensor(out=ang.rearrange("p t s f -> p (t s f)"),
                                                       in0=turns.rearrange("p t s f -> p (t s f)"), scalar=-part,
                                                       in1=ang.rearrange("p t s f -> p (t s f)"), op0=ALU.mult, op1=ALU.add))
            settled(nc.vector.tensor_scalar(ang[:, :, 0, :], ang[:, :, 0, :], 1.5707963267948966, None, ALU.add))
            nc.vector.tensor_scalar(ang, ang, 3.1415925, -3.1415925, ALU.min, ALU.max).then_inc(ang_ready, 1)
            for b in range(TT):
                k0 = 0 if b else P
                settled(nc.vector.tensor_scalar(distm[:, b, k0:256], posk[:, (b - 1) * P + k0:(b + 1) * P],
                                                posqf[:, b:b + 1], None, ALU.subtract))
                settled(nc.vector.scalar_tensor_tensor(out=distm[:, b, k0:256], in0=distm[:, b, k0:256], scalar=-1.0,
                                                       in1=distm[:, b, k0:256], op0=ALU.mult, op1=ALU.max))
                if b:
                    nc.vector.memset(distm[0:64, b, 0:64], MASKED)
                    nc.vector.memset(distm[64:128, b, 0:128], MASKED)
                settled(nc.vector.memset(distm[0:64, b, 192:256], MASKED))

            modulate(ada_order[4])
            for tt in range(TT):
                dve.wait_ge(z_stat, tt + 1)
                nc.vector.tensor_reduce(ss[:, tt, 0:10], zsq[:, tt, :].rearrange("p (h d) -> p h d", d=SD), X, ALU.add)
            dve.wait_ge(z_stat, 2 * TT)
            nc.vector.tensor_scalar(rz[:, :, 10:11], ss[:, :, 10:11], 1.0 / QRANK, EPS, ALU.mult, ALU.add)
            settled(nc.vector.tensor_scalar(rz[:, :, 11:12], ss[:, :, 11:12], 1.0 / KVRANK, EPS, ALU.mult, ALU.add))
            nc.vector.tensor_scalar(rz[:, :, 0:10], ss[:, :, 0:10], 1.0 / SD, EPS, ALU.mult, ALU.add).then_inc(z_var, 1)
            dve.wait_ge(z_sd, 1)
            settled(nc.vector.reciprocal(rz[:], rz[:]))
            for tt in range(TT):
                zh = z[:, tt, 0:640].rearrange("p (h d) -> p h d", d=SD)
                zc, zk = z[:, tt, Z_CQ:Z_CKV], z[:, tt, Z_CKV:Z_KR]
                tt_(zh, zh, rz[:, tt, 0:10].unsqueeze(2).to_broadcast([P, 10, SD]), ALU.mult)
                nc.vector.scalar_tensor_tensor(out=zc, in0=zc, scalar=rz[:, tt, 10:11], in1=g_cq[:],
                                               op0=ALU.mult, op1=ALU.mult)
                settled(nc.vector.scalar_tensor_tensor(out=zk, in0=zk, scalar=rz[:, tt, 11:12], in1=g_ckv[:],
                                                       op0=ALU.mult, op1=ALU.mult))
                tt_(zh, zh, g_swa[:], ALU.mult).then_inc(zn_ready, 1)
            dve.wait_ge(trig_ready, 1)
            for tt in range(TT):
                dve.wait_ge(m_built, tt + 1)
                m = m2[:, tt % 2, :, :]
                x1, x2 = m[:, :, NOPE:NOPE + 16], m[:, :, NOPE + 16:QK]
                cos = trig[:, tt, 0, :].unsqueeze(1).to_broadcast([P, 2 * MH, 16])
                sin = trig[:, tt, 1, :].unsqueeze(1).to_broadcast([P, 2 * MH, 16])
                tt_(ropet[0], x1, cos, ALU.mult)
                tt_(ropet[1], x2, sin, ALU.mult)
                tt_(ropet[2], x1, sin, ALU.mult)
                settled(tt_(ropet[3], x2, cos, ALU.mult))
                tt_(x1, ropet[0], ropet[1], ALU.subtract)
                tt_(x2, ropet[2], ropet[3], ALU.add).then_inc(m_roped, 1)
                dve.wait_ge(m_sq, tt + 1)
                settled(nc.vector.tensor_reduce(mss[:], msq, X, ALU.add))
                nc.vector.tensor_scalar(mrz[:], mss[:], 1.0 / QK, EPS, ALU.mult, ALU.add).then_inc(m_var, 1)
                dve.wait_ge(m_sd, tt + 1)
                settled(nc.vector.reciprocal(mrz[:], mrz[:]))
                settled(tt_(m, m, mrz[:].unsqueeze(2).to_broadcast([P, 2 * MH, QK]), ALU.mult))
                mg = m.rearrange("p (a h) d -> p a h d", a=2)
                tt_(mg, mg, g_mla[:].unsqueeze(2).to_broadcast([P, 2, MH, QK]), ALU.mult).then_inc(m_ready, 1)

            def bias_and_max(u):
                kind, b, sub, j0 = units[u]
                dve.wait_ge(s_done, u + 1)
                if u >= 4:
                    dve.wait_ge(pt_ps, u - 3)
                nk = len(key_tiles(kind, b)) * P
                if kind == "s":
                    k0 = 256 - nk
                    for j in range(2):
                        nc.vector.scalar_tensor_tensor(out=pb[:, u % 4, j, k0:256], in0=distm[:, b, k0:256],
                                                       scalar=-slope(sub * SG + j0 + j), in1=ps[:, u % 3, j * 256 + k0:j * 256 + 256],
                                                       op0=ALU.mult, op1=ALU.add)
                    h0 = sub * SG + j0
                    settled(nc.vector.tensor_copy(pb[:, u % 4, :, 256:257], sinks[:, h0:h0 + 2].unsqueeze(2)))
                    nc.vector.tensor_reduce(nm[:, u % 4, :], pb[:, u % 4, :, k0:257], X, ALU.max, negate=True).then_inc(biased, 1)
                else:
                    settled(nc.vector.memset(ps[0:64, u % 3, b * P + 64:(b + 1) * P], NEG))
                    nc.vector.tensor_reduce(nm[:, u % 4, 0:1], ps[:, u % 3, 0:nk], X, ALU.max, negate=True).then_inc(biased, 1)

            def scale_probs(u):
                kind, b, _, _ = units[u]
                dve.wait_ge(exp_done, u + 1)
                nj = heads_of(kind)
                nk = len(key_tiles(kind, b)) * P
                settled(nc.vector.reciprocal(rsm[:, u % 4, 0:nj], sm[:, u % 4, 0:nj]))
                for j in range(nj):
                    v = pb[:, u % 4, j, 256 - nk:256] if kind == "s" else p_view(u, kind)[:, 0, 0:nk]
                    last = nc.vector.tensor_scalar(v, v, rsm[:, u % 4, j:j + 1], None, ALU.mult)
                last.then_inc(p_ready, 1)

            def copy_out(u):
                kind, b, sub, j0 = units[u]
                dve.wait_ge(o_ps, u + 1)
                cols = slice(b * P, (b + 1) * P)
                if kind == "s":
                    ins = nc.vector.tensor_copy(oT[:, 2 * sub + j0 // 2, cols], ps[:, 3 * (u % 2) + 3, 0:P])
                else:
                    rows = slice(64 * (sub % 2), 64 * (sub % 2) + 64)
                    ins = nc.vector.tensor_copy(oT[rows, 4 + sub // 2, cols], ps[rows, 3 * (u % 2) + 3, 0:P])
                ins.then_inc(o_sb, 1)

            rest = ada_order[5:]
            bias_and_max(0)
            for u in range(NU):
                if u + 1 < NU:
                    bias_and_max(u + 1)
                scale_probs(u)
                if u >= 2:
                    copy_out(u - 2)
                if u % 6 == 4 and rest:
                    modulate(rest.pop(0))
            copy_out(NU - 2)
            copy_out(NU - 1)
            for piece in (2, 4, 3, 5):
                modulation(piece, 12)
            settled(nc.vector.scalar_tensor_tensor(out=gs[:], in0=ada[:, 4 * KD:5 * KD], scalar=1.0, in1=g2[:],
                                                   op0=ALU.add, op1=ALU.mult))
            for m in range(KD):
                dve.wait_ge(mix_ps, m + 1)
                nc.vector.scalar_tensor_tensor(out=res[:, m, :], in0=ps[:, m % 4, :], scalar=ada[:, 2 * KD + m:2 * KD + m + 1],
                                               in1=res[:, m, :], op0=ALU.mult, op1=ALU.add).then_inc(x1_ready, 1)
            norm(5, rstd2[:], ms2, var2, sd2)
            for k in range(KD):
                nc.vector.scalar_tensor_tensor(out=h2T[:, k, :], in0=res[:, k, :], scalar=gs[:, k:k + 1], in1=rstd2[:],
                                               op0=ALU.mult, op1=ALU.mult).then_inc(h2_scaled, 1)
            for k in range(KD):
                dve.wait_ge(h2_hi, k + 1)
                tt_(h2lo[:, k, :], h2T[:, k, :], h2hi[:, k, :].bitcast(F32), ALU.subtract).then_inc(h2_split, 1)

            def top16(vals, idx, rows, n):
                for a in range(n):
                    last = nc.vector.max(vals(a)[:, 0:8], rows(a))
                settled(last)
                for a in range(n):
                    last = nc.vector.max_index(idx(a)[:, 0:8], vals(a)[:, 0:8], rows(a))
                settled(last)
                for a in range(n):
                    last = nc.vector.match_replace(rows(a), vals(a)[:, 0:8], rows(a), -3.0e38)
                settled(last)
                for a in range(n):
                    last = nc.vector.max(vals(a)[:, 8:16], rows(a))
                settled(last)
                for a in range(n):
                    last = nc.vector.max_index(idx(a)[:, 8:16], vals(a)[:, 8:16], rows(a))
                settled(last)

            for tt in range(TT):
                dve.wait_ge(s_in, tt * 16 + 16)
                top16(lambda a: sv[:, a % PH, a // PH, :], lambda a: six[:, a % PH, a // PH, :], lambda a: s[:, a, :], 2 * PH)
                nc.vector.tensor_copy(sixf[:], six[:])
                settled(tt_(cand[:], sv[:, :, 0, :].unsqueeze(3).to_broadcast([P, PH, KTOP, KTOP]),
                           sv[:, :, 1, :].unsqueeze(2).to_broadcast([P, PH, KTOP, KTOP]), ALU.add))
                top16(lambda a: best[:, a, :], lambda a: bi[:, a, :],
                      lambda a: cand[:, a, :, :].rearrange("p i j -> p (i j)"), PH)
                tt_(eW[:], best[:], best[:, :, 0:1].to_broadcast([P, PH, KTOP]), ALU.subtract).then_inc(best_ready, 1)
                nc.vector.tensor_scalar(bia[:, 0, :, :], bi[:], 4, None, ALU.logical_shift_right)
                settled(nc.vector.tensor_scalar(bia[:, 1, :, :], bi[:], 15, None, ALU.bitwise_and))
                settled(nc.vector.tensor_copy(abf[:], bia[:]))
                for half in range(2):
                    settled(tt_(eq, abf[:, half, :, :].unsqueeze(3).to_broadcast([P, PH, KTOP, KTOP]),
                               iota[:, 0:KTOP].unsqueeze(1).unsqueeze(1).to_broadcast([P, PH, KTOP, KTOP]), ALU.is_equal))
                    settled(tt_(eq, eq, sixf[:, :, half, :].unsqueeze(2).to_broadcast([P, PH, KTOP, KTOP]), ALU.mult))
                    settled(nc.vector.tensor_reduce(IJW[:, half, :, :], eq, X, ALU.add))
                dve.sem_inc(s_free, 1)
                dve.wait_ge(best_exp, tt + 1)
                settled(nc.vector.tensor_reduce(eS[:], eW[:], X, ALU.add))
                settled(nc.vector.reciprocal(eR[:], eS[:]))
                tt_(IJW[:, 2, :, :], eW[:], eR[:].unsqueeze(2).to_broadcast([P, PH, KTOP]), ALU.mult).then_inc(ijw_ready, 1)
                dve.wait_ge(ijw_ps, tt + 1)
                settled(nc.vector.tensor_copy(slots[:, 0:3, :], ps[:, 4, 0:3 * P].rearrange("p (a t) -> p a t", a=3)))
                settled(nc.vector.tensor_copy(slots[:, 3, :].bitcast(F32R), slots[:, 2, :]))
                settled(tt_(slots[:, 4, :], slots[:, 2, :], slots[:, 3, :], ALU.subtract))
                with dve.Fori(0, BOTH) as i:
                    for half in range(2):
                        q = i * 2 + (tt * 2 * BOTH + half)
                        cols = bass.ds(i * (2 * HB) + HB * half, HB)

                        def spread(row):
                            return slots[:, row, cols].unsqueeze(2).to_broadcast([P, HB, P])

                        each = iota[:].unsqueeze(1).to_broadcast([P, HB, P])
                        dve.wait_ge(oh_used, q + 1)
                        tt_(eqI[:, half, :, :], each, spread(0), ALU.is_equal).then_inc(eq_ready, 1)
                        tt_(ohJ[half][:], each, spread(1), ALU.is_equal)
                        dve.wait_ge(eq_ready, q + 1)
                        tt_(ohH[half][:], eqI[:, half, :, :], spread(3), ALU.mult)
                        tt_(ohL[half][:], eqI[:, half, :, :], spread(4), ALU.mult).then_inc(oh_ready, 1)

            def low_v(n, r):
                dve.wait_ge(v_hi, n + 1)
                tt_(vlo[r][:], vraw[r][:], vhi[r][:].bitcast(F32), ALU.subtract).then_inc(v_lo, 1)

            def weigh(n, r, count, first):
                dve.wait_ge(gate_in[r], count)
                dve.wait_ge(act_back[r], count)
                if not first or r >= 2:
                    dve.wait_ge(c_lo, n - 1)
                c = cf[r % 2]
                tt_(c[:], act_in[r][:], gate[r][:], ALU.mult).then_inc(c_mul, 1)
                dve.wait_ge(c_mul, n + 1)
                nc.vector.tensor_copy(chi[r][:], c[:]).then_inc(c_hi, 1)
                dve.wait_ge(c_hi, n + 1)
                tt_(clo[r][:], c[:], chi[r][:].bitcast(F32), ALU.subtract).then_inc(c_lo, 1)

            for r in range(4):
                low_v(r, r)
                weigh(r, r, 16, True)
            with dve.Fori(1, NT // 4) as i:
                for r in range(4):
                    low_v(i * 4 + r, r)
                    weigh(i * 4 + r, r, i * 16 + 16, False)
            dve.wait_ge(y_ps, NT)
            for d in range(KD):
                nc.vector.scalar_tensor_tensor(out=res[:, d, :], in0=ps[:, d, :], scalar=ada[:, 5 * KD + d:5 * KD + d + 1],
                                               in1=res[:, d, :], op0=ALU.mult, op1=ALU.add).then_inc(y_sb, 1)


def kernel(**inputs):
    import numpy as np
    import concourse.bacc as bacc
    from concourse.bass_utils import run_bass_kernel_spmd as run

    a = {n: np.asarray(v) for n, v in inputs.items()}

    def cols(v):
        return np.ascontiguousarray(v.reshape(-1, P).T)

    sent = {
        "xT": np.ascontiguousarray(a["x"][0].T.reshape(KD, P, T).transpose(1, 0, 2)),
        "c": cols(a["c"][0]),
        "positions": np.ascontiguousarray(a["positions"][0]),
        "position_cols": cols(a["positions"][0]),
        "w_ada": a["w_ada"][0], "b_ada": cols(a["b_ada"][0]),
        "norm1_g": cols(a["norm1_g"][0]), "norm2_g": cols(a["norm2_g"][0]),
        "w_in": a["w_in"][0],
        "swa_q_norm": a["swa_q_norm"][0], "swa_k_norm": a["swa_k_norm"][0], "swa_sinks": a["swa_sinks"][0],
        "mla_q_a_norm": a["mla_q_a_norm"][0], "mla_kv_a_norm": a["mla_kv_a_norm"][0],
        "mla_w_uq": a["mla_w_uq"][0], "mla_w_ukv": a["mla_w_ukv"][0],
        "mla_q_norm": a["mla_q_norm"][0], "mla_k_norm": a["mla_k_norm"][0],
        "w_out": a["w_out"][0], "peer_w_query": a["peer_w_query"][0],
        "sub_keys": a["peer_sub_keys"][0].transpose(1, 3, 0, 2).reshape(P, PH, NK),
        "u_tiles": a["peer_u"][0].reshape(NT, P, KD, P).transpose(0, 3, 2, 1).reshape(NT, P, D),
        "v_tiles": a["peer_v"][0].reshape(NT, P, D),
    }
    sent = {n: np.ascontiguousarray(v) for n, v in sent.items()}
    nc = bacc.Bacc("TRN2", target_bir_lowering=False, num_devices=1)
    args = {n: nc.dram_tensor(f"in_{n}", v.shape, mybir.dt.from_np(v.dtype), kind="ExternalInput").ap()
            for n, v in sent.items()}
    args["outT"] = nc.dram_tensor("out_T", (KD, P, T), F32, kind="ExternalOutput").ap()
    build(nc, **args)
    r = run(nc, [{f"in_{n}": v for n, v in sent.items()}], core_ids=[0])
    return np.ascontiguousarray(r.results[0]["out_T"].reshape(D, T).T)[None]
```

```python
import concourse.bass as bass
from concourse import mybir
from concourse.alu_op_type import AluOpType as ALU
from contextlib import ExitStack

F32 = mybir.dt.float32
F32R = mybir.dt.float32r
I32 = mybir.dt.int32
U32 = mybir.dt.uint32
ACT = mybir.ActivationFunctionType
X = mybir.AxisListType.X

P = 128
D = 1024
T = 512
KD = D // P
TT = T // P
EPS = 1e-6
NEG = -1e30
SH, SKV, SD = 8, 2, 64
SG = SH // SKV
MH, NOPE, ROPE, VD = 8, 64, 32, 64
QK = NOPE + ROPE
QRANK, KVRANK = 256, 128
IN_COLS = SH * SD + 2 * SKV * SD + QRANK + KVRANK + ROPE
Z_K = SH * SD
Z_V = Z_K + SKV * SD
Z_CQ = Z_V + SKV * SD
Z_CKV = Z_CQ + QRANK
Z_KR = Z_CKV + KVRANK
ROPE_THETA = 10000.0
PH, NK, KTOP, PD = 8, 128, 16, 64
NT = NK
HB = 4
SOLO, BOTH, GP = 12, P // (2 * HB), 8
SEG = SOLO + BOTH
CH = 512
MASKED = 1e33
PW = 260

PI2_A, PI2_B, PI2_C = 6.28125, 0.0019350051879882812, 3.019916050e-07
ROUND = 12582912.0


def slope(h):
    return 2.0 ** (-8.0 * (h + 1) / SH)


def build(nc, xT, c, positions, position_cols, w_ada, b_ada, norm1_g, norm2_g, w_in, swa_q_norm, swa_k_norm,
          swa_sinks, mla_q_a_norm, mla_kv_a_norm, mla_w_uq, mla_w_ukv, mla_q_norm, mla_k_norm,
          w_out, peer_w_query, sub_keys, u_tiles, v_tiles, outT):
    ctx = ExitStack()
    with ctx:
        def sem(name):
            return ctx.enter_context(nc.semaphore(name))

        BASE = 16512
        END = 229344

        def region(start, entries):
            out, at = [], start
            for name, shape, dt in entries:
                size = 4
                for s in shape[1:]:
                    size *= s
                out.append(nc.alloc_sbuf_tensor_at(name, shape, dt, offset=at))
                at += (size + 31) // 32 * 32
            assert at <= END, (name, at - END)
            return out, at

        (res, ident, ones, iota, cT, b_cols, ada, g1, g2, gs), at0 = region(BASE, [
            ("res", [P, KD, T], F32),
            ("ident", [P, P], F32), ("ones", [P, P], F32), ("iota", [P, P], F32),
            ("cT", [P, KD], F32), ("b_cols", [P, 6 * KD], F32), ("ada", [P, 6 * KD], F32),
            ("g1", [P, KD], F32), ("g2", [P, KD], F32), ("gs", [P, KD], F32)])
        ring, at1 = region(at0, [(f"ring{i}", [P, KD, CH], F32) for i in range(3)])
        (hT,), at2 = region(at1, [("hT", [P, KD, T], F32)])
        (oT,), _ = region(at1, [("oT", [P, KD, T], F32)])
        (m_late,), at_m = region(at1, [("m_late", [P, 2, 2 * MH, QK], F32)])
        assert at_m <= at2
        (wlo0, whi0, wlo2), _ = region(at0, [("wlo0", [P, KD, CH], F32R), ("whi0", [P, KD, CH], F32R), ("wlo2", [P, KD, CH], F32R)])
        (oTlo,), _ = region(at1, [("oTlo", [P, KD, T], F32R)])
        (z, qkc, wuq, wukv, kvm, m2, distm, pb, qkT, g_swa, g_cq, g_ckv, g_mla, trig, posq,
         posqf, ss, rz, mss, mrz, nm, sm, rsm, sinks, freq), _ = region(at2, [
            ("z", [P, TT, IN_COLS], F32), ("qkc", [P, 2, 4, T], F32),
            ("wuq", [P, 2, MH * QK], F32), ("wukv", [P, MH * (NOPE + VD)], F32),
            ("kvm", [P, TT, MH * (NOPE + VD)], F32), ("m2", [P, 2, 2 * MH, QK], F32),
            ("distm", [P, TT, 256], F32), ("pb", [P, 4, 2, PW], F32), ("qkT", [P, 2 * MH, T], F32),
            ("g_swa", [P, SH + SKV, SD], F32), ("g_cq", [P, QRANK], F32), ("g_ckv", [P, KVRANK], F32),
            ("g_mla", [P, 2, QK], F32), ("trig", [P, TT, 2, ROPE // 2], F32), ("posq", [P, TT], I32),
            ("posqf", [P, TT], F32), ("ss", [P, TT, 12], F32), ("rz", [P, TT, 12], F32),
            ("mss", [P, 2 * MH], F32), ("mrz", [P, 2 * MH], F32), ("nm", [P, 4, 2], F32),
            ("sm", [P, 4, 2], F32), ("rsm", [P, 4, 2], F32), ("sinks", [P, SH], F32),
            ("freq", [P, ROPE // 2], F32)])

        def heads(tt):
            return m2[:, tt, :, :] if tt < 2 else m_late[:, tt - 2, :, :]

        qTs, kcT = qkc[:, 0, :, :], qkc[:, 1, :, :]
        pt = m2[:].rearrange("p a h d -> p (a h d)")[:, 0:1024].rearrange("p (a s q) -> p a s q", a=2, q=P)
        accs = m2[:].rearrange("p a h d -> p (a h d)")[:, 1024:2048].rearrange("p (a c) -> p a c", a=2)
        zsq = qkT[:].rearrange("p a t -> p (a t)")[:, 0:TT * 640].rearrange("p (t c) -> p t c", t=TT)
        zsq_cq = qkT[:].rearrange("p a t -> p (a t)")[:, TT * 640:TT * 640 + 384]
        msq = pb[:].rearrange("p a j k -> p (a j k)")[:, 0:2 * MH * QK].rearrange("p (h d) -> p h d", h=2 * MH)
        kvm_flat = kvm[:].rearrange("p t c -> p (t c)")
        posk_i = kvm_flat[:, 0:T].bitcast(I32)
        posk = kvm_flat[:, T:2 * T]
        ang = kvm_flat[:, 1024:1024 + TT * 32].rearrange("p (t s f) -> p t s f", t=TT, s=2)
        turns = kvm_flat[:, 1280:1280 + TT * 32].rearrange("p (t s f) -> p t s f", t=TT, s=2)
        ropet = [pb[:].rearrange("p a j k -> p (a j k)")[:, 256 * n:256 * n + 256].rearrange("p (h d) -> p h d", h=16) for n in range(4)]
        spare = [qkT[:].rearrange("p a t -> p (a t)")[:, 4096:8192].rearrange("p (k n) -> p k n", k=KD),
                 qkc[:].rearrange("p a g t -> p (a g t)").rearrange("p (k n) -> p k n", k=KD)]
        rstd1 = pb[:].rearrange("p a j k -> p (a j k)")[:, 0:T]
        (stage,), at_c = region(at0, [("stage", [P, NT, P], F32)])
        assert at_c == at2
        (qpT,), _ = region(at1, [("qpT", [P, PH, T], F32)])
        (h2hi, h2lo), at3 = region(at2, [("h2hi", [P, KD, T], F32R), ("h2lo", [P, KD, T], F32R)])
        (h2T,), at_h = region(at3, [("h2T", [P, KD, T], F32)])
        (skT, rstd2), at_h = region(at_h, [("skT", [P, PH, NK], F32), ("rstd2", [P, T], F32)])
        (whi1,), _ = region(at_h, [("whi1", [P, KD, CH], F32R)])
        (oThi,), _ = region(at2, [("oThi", [P, KD, T], F32R)])
        (sout0, sout1), at_h = region(at_h, [("sout0", [P, 2 * PH, NK], F32), ("sout1", [P, 2 * PH, NK], F32)])
        sout = (sout0, sout1)
        (s, sv, six, sixf, cand, best, bi, bia, abf, IJW, slots, eW, eS, eR, eqI), at_t = region(at3, [
            ("s", [P, 2 * PH, NK], F32), ("sv", [P, PH, 2, KTOP], F32), ("six", [P, PH, 2, KTOP], U32),
            ("sixf", [P, PH, 2, KTOP], F32), ("cand", [P, PH, KTOP, KTOP], F32),
            ("best", [P, PH, KTOP], F32), ("bi", [P, PH, KTOP], U32), ("bia", [P, 2, PH, KTOP], U32),
            ("abf", [P, 2, PH, KTOP], F32), ("IJW", [P, 3, PH, KTOP], F32), ("slots", [P, 5, P], F32),
            ("eW", [P, PH, KTOP], F32), ("eS", [P, PH], F32), ("eR", [P, PH], F32), ("eqI", [P, 2, HB, P], F32)])
        eq = s[:].rearrange("p a (b c) -> p (a b c)", c=16).rearrange("p (h k m) -> p h k m", h=PH, k=KTOP)
        ohJ, at_t = region(at_t, [(f"ohJ{b}", [P, HB, P], F32R) for b in range(2)])
        gpart, at_t = region(at_t, [(f"gpart{b}", [P, HB, 2, P], F32) for b in range(2)])
        ohW, at_t = region(at_t, [(f"ohW{b}", [P, HB, 2, P], F32R) for b in range(2)])
        at4 = max(at_t, at_h)
        uraw, at4 = region(at4, [(f"uraw{b}", [P, D], F32) for b in range(2)])
        uhi, at4 = region(at4, [(f"uhi{b}", [P, D], F32R) for b in range(2)])
        ulo, at4 = region(at4, [(f"ulo{b}", [P, D], F32R) for b in range(2)])
        act_out, at4 = region(at4, [(f"act_out{b}", [P, T], F32) for b in range(2)])
        vraw, at_v = region(at0, [(f"vraw{b}", [P, D], F32) for b in range(4)])
        vhi, at_v = region(at_v, [(f"vhi{b}", [P, D], F32R) for b in range(4)])
        vlo, at_v = region(at_v, [(f"vlo{b}", [P, D], F32R) for b in range(4)])
        assert at_v <= at2
        gate, at5 = region(at3, [(f"gate{b}", [P, T], F32) for b in range(4)])
        act_in, at5 = region(at5, [(f"act_in{b}", [P, T], F32) for b in range(4)])
        cf, at5 = region(at5, [(f"cf{b}", [P, T], F32) for b in range(2)])
        chi, at5 = region(at5, [(f"chi{b}", [P, T], F32R) for b in range(4)])
        clo, at5 = region(at5, [(f"clo{b}", [P, T], F32R) for b in range(4)])
        assert at5 <= at_t

        ps = ctx.enter_context(nc.psum_tensor("ps", [P, 8, 512], F32))
        ada_ps = ps[:, 7, 0:6 * KD]
        gates = nc.dram_tensor("gates", (NT, P, T), F32).ap()
        gelus = nc.dram_tensor("gelus", (NT, P, T), F32).ap()
        keys = nc.dram_tensor("keys", (TT, P, 2 * PH * NK), F32).ap()

        x_in = sem("x_in")
        c_in = sem("c_in")
        small_in = sem("small_in")
        up_in = sem("up_in")
        chunk_in = [sem(f"chunk_in{i}") for i in range(5)]
        chunk_used = [sem(f"chunk_used{i}") for i in range(5)]
        acc_done = sem("acc_done")
        const = sem("const")
        sq1 = sem("sq1")
        ms1 = sem("ms1")
        var1 = sem("var1")
        sd1 = sem("sd1")
        ada_done = sem("ada_done")
        h_scaled = sem("h_scaled")
        h_ready = sem("h_ready")
        z_ps = sem("z_ps")
        z_sb = sem("z_sb")
        z_stat = sem("z_stat")
        z_var = sem("z_var")
        z_sd = sem("z_sd")
        zn_ready = sem("zn_ready")
        zt_ps = sem("zt_ps")
        zt_sb = sem("zt_sb")
        up_ps = sem("up_ps")
        up_sb = sem("up_sb")
        m_built = sem("m_built")
        m_roped = sem("m_roped")
        m_sq = sem("m_sq")
        m_var = sem("m_var")
        m_sd = sem("m_sd")
        m_ready = sem("m_ready")
        mt_ps = sem("mt_ps")
        mt_sb = sem("mt_sb")
        ang_ready = sem("ang_ready")
        trig_ready = sem("trig_ready")
        s_done = sem("s_done")
        biased = sem("biased")
        exp_done = sem("exp_done")
        p_ready = sem("p_ready")
        pt_ps = sem("pt_ps")
        pt_sb = sem("pt_sb")
        o_ps = sem("o_ps")
        o_sb = sem("o_sb")
        o_hi = sem("o_hi")
        o_split = sem("o_split")
        out0_hi = sem("out0_hi")
        out0_split = sem("out0_split")
        w_hi = sem("w_hi")
        w_split = sem("w_split")
        mix_ps = sem("mix_ps")
        x1_ready = sem("x1_ready")
        sq2 = sem("sq2")
        sq2_sum = sem("sq2_sum")
        ms2 = sem("ms2")
        var2 = sem("var2")
        sd2 = sem("sd2")
        h2_scaled = sem("h2_scaled")
        h2_hi = sem("h2_hi")
        h2_split = sem("h2_split")
        sk_in = sem("sk_in")
        qp_ps = sem("qp_ps")
        qp_sb = sem("qp_sb")
        key_ps = sem("key_ps")
        key_sb = sem("key_sb")
        best_ready = sem("best_ready")
        best_exp = sem("best_exp")
        ijw_ready = sem("ijw_ready")
        ijw_ps = sem("ijw_ps")
        slots_ready = sem("slots_ready")
        oh_ready = sem("oh_ready")
        oh_used = sem("oh_used")
        g_parts = sem("g_parts")
        g_sb = sem("g_sb")
        g_out = sem("g_out")
        s_copied = sem("s_copied")
        s_out = [sem(f"s_out{b}") for b in range(2)]
        s_in = sem("s_in")
        s_free = sem("s_free")
        eq_ready = sem("eq_ready")
        c_space = sem("c_space")
        u_in = [sem(f"u_in{b}") for b in range(2)]
        v_in = [sem(f"v_in{b}") for b in range(4)]
        gate_in = [sem(f"gate_in{b}") for b in range(4)]
        act_back = [sem(f"act_back{b}") for b in range(4)]
        u_hi = sem("u_hi")
        u_lo = sem("u_lo")
        a_ps = sem("a_ps")
        gelu_done = sem("gelu_done")
        a_out = [sem(f"a_out{b}") for b in range(2)]
        v_hi = sem("v_hi")
        v_lo = sem("v_lo")
        c_mul = sem("c_mul")
        c_hi = sem("c_hi")
        c_lo = sem("c_lo")
        y_ps = sem("y_ps")
        y_sb = sem("y_sb")
        out_done = sem("out_done")
        dve_step = sem("dve_step")
        act_step = sem("act_step")
        pool_step = sem("pool_step")

        weights_of = {"ada": w_ada, "in": w_in, "out": w_out, "query": peer_w_query}
        chunks, slot, place, uses = [], [], {}, [0] * 5
        for kind, j, at in (("ada", 2, 0), ("ada", 3, 1), ("ada", 0, 3), ("ada", 1, 4), ("in", 0, 2), ("in", 1, 0), ("in", 2, 1),
                            ("ada", 4, 3), ("ada", 5, 4), ("ada", 8, 3), ("ada", 9, 4), ("ada", 6, 3), ("ada", 7, 4),
                            ("ada", 10, 3), ("ada", 11, 4), ("out", 0, 2), ("out", 1, 0), ("query", 0, 2), ("query", 1, 0)):
            place[kind, j] = len(chunks)
            chunks.append((kind, weights_of[kind], j, min(CH, weights_of[kind].shape[1] - j * CH)))
            slot.append((at, uses[at]))
            uses[at] += 1
        ada_order = [j for kind, _, j, _ in chunks if kind == "ada"]

        def chunk(n):
            at = slot[n][0]
            return ring[at][:] if at < 3 else spare[at - 3]

        NSMALL = 12
        units = [("s", b, kv, j) for b in range(TT) for kv in range(SKV) for j in (0, 2)] + \
                [("m", b, h, 0) for b in range(TT) for h in range(MH)]
        NU = len(units)

        def heads_of(kind):
            return 2 if kind == "s" else 1

        def key_tiles(kind, b):
            if kind == "s":
                return [b] if b == 0 else [b - 1, b]
            return list(range(b + 1))

        def p_view(u, kind):
            if kind == "s":
                return pb[:, u % 4, :, :]
            return pb[:, u % 4, :, :].rearrange("p j k -> p (j k)")[:, 0:512].unsqueeze(1)

        def pt_slots(kind, b):
            if kind == "s":
                return [(2 * j + kb - (b - 1), j, (kb - (b - 1)) * P, kb) for j in range(2) for kb in key_tiles(kind, b)]
            return [(kb, 0, kb * P, kb) for kb in key_tiles(kind, b)]

        parts = {("out", 0): (whi0, wlo2), ("out", 1): (whi1, wlo0), ("query", 0): (whi0, wlo2), ("query", 1): (whi1, wlo0)}

        block = ctx.enter_context(nc.Block())

        @block.sync
        def _(sp):
            def load_chunk(n):
                at, before = slot[n]
                if before:
                    sp.wait_ge(chunk_used[at], before)
                _, w, j, cols = chunks[n]
                sp.dma_start(chunk(n)[:, :, 0:cols],
                             w[:, j * CH:j * CH + cols].rearrange("(k p) n -> p k n", p=P)).then_inc(chunk_in[at], 16)

            sp.dma_start(cT[:], c).then_inc(c_in, 16)
            load_chunk(0)
            load_chunk(1)
            sp.dma_start(res[:], xT).then_inc(x_in, 16)
            for n in range(2, len(chunks)):
                load_chunk(n)
            sp.wait_ge(mix_ps, KD)
            sp.dma_start(skT[:], sub_keys).then_inc(sk_in, 16)

            def load_u(n, r):
                sp.wait_ge(u_lo, n + 1)
                sp.dma_start(uraw[r % 2][:], u_tiles[bass.ds(n, 1), :, :].rearrange("a p c -> p (a c)")).then_inc(u_in[r % 2], 16)

            for n in range(4):
                load_u(n, n)
            for tt in range(TT):
                sp.wait_ge(s_copied, tt + 1)
                sp.dma_start(keys[tt], sout[tt % 2][:].rearrange("p a n -> p (a n)")).then_inc(s_out[tt % 2], 16)
            for b in range(2):
                sp.wait_ge(s_out[b], 16 * TT // 2)
            sp.wait_ge(h2_split, KD)
            sp.dma_start(s[:].rearrange("p a n -> p (a n)"), keys[0]).then_inc(s_in, 16)

            def load_us(first, steps):
                with sp.Fori(0, steps // 4) as i:
                    for r in range(4):
                        load_u(first + i * 4 + (r + 2), r)

            for n in range(4, SOLO + 2):
                load_u(n, n)
            with sp.Fori(0, TT - 1) as tt:
                sp.wait_ge(s_free, tt + 1)
                sp.dma_start(s[:].rearrange("p a n -> p (a n)"),
                             keys[bass.ds(tt + 1, 1), :, :].rearrange("a p c -> p (a c)")).then_inc(s_in, 16)
                load_us(tt * SEG + SOLO, SEG)
            load_us((TT - 1) * SEG + SOLO, SEG)
            for n in range(TT * SEG + SOLO + 2, NT):
                load_u(n, n)

            sp.wait_ge(g_out, 16 * GP * (TT + 1))
            sp.wait_ge(c_space, TT)

            def load_v(n, r, first):
                if not first:
                    sp.wait_ge(v_lo, n - 3)
                sp.dma_start(vraw[r][:], v_tiles[bass.ds(n, 1), :, :].rearrange("a p c -> p (a c)")).then_inc(v_in[r], 16)
                if not first:
                    sp.wait_ge(c_mul, n - 3)
                sp.dma_start(gate[r][:], gates[bass.ds(n, 1), :, :].rearrange("a p c -> p (a c)")).then_inc(gate_in[r], 16)
                sp.dma_start(act_in[r][:], gelus[bass.ds(n, 1), :, :].rearrange("a p c -> p (a c)")).then_inc(act_back[r], 16)

            for b in range(2):
                sp.wait_ge(a_out[b], 16 * 3)
            for r in range(4):
                load_v(r, r, True)
            for b in range(2):
                sp.wait_ge(a_out[b], 16 * (NT // 2 + 1))
            with sp.Fori(1, NT // 4) as i:
                for r in range(4):
                    load_v(i * 4 + r, r, False)
            for d in range(KD):
                sp.wait_ge(y_sb, d + 1)
                sp.dma_start(outT[d], res[:, d, :]).then_inc(out_done, 16)
            sp.wait_ge(out_done, 16 * KD)
        @block.gpsimd
        def _(pool):
            nc.gpsimd.memset(ones[:], 1.0).then_inc(const, 1)
            nc.gpsimd.iota(iota[:], pattern=[[1, P]], base=0, channel_multiplier=0,
                           allow_small_or_imprecise_dtypes=True).then_inc(const, 1)
            nc.gpsimd.memset(ident[:], 0.0).then_inc(pool_step, 1)
            pool.wait_ge(pool_step, 1)
            nc.gpsimd.affine_select(out=ident[:], in_=ident[:], compare_op=ALU.not_equal, fill=1.0, base=0,
                                    pattern=[[-1, P]], channel_multiplier=1).then_inc(const, 1)
            for tt in range(TT):
                pool.wait_ge(up_sb, 2 * tt + 2)
                mk = heads(tt)[:, MH:2 * MH, :]
                nc.gpsimd.tensor_copy(mk[:, :, 0:NOPE],
                                      kvm[:, tt, :].rearrange("p (h c) -> p h c", h=MH)[:, :, 0:NOPE])
                nc.gpsimd.tensor_copy(mk[:, :, NOPE:QK],
                                      z[:, tt, Z_KR:Z_KR + ROPE].unsqueeze(1).to_broadcast([P, MH, ROPE])).then_inc(m_built, 1)
            n = place["out", 0]
            whi, wlo = parts["out", 0]
            pool.wait_ge(chunk_in[slot[n][0]], 16 * (slot[n][1] + 1))
            pool.wait_ge(chunk_used[1], uses[1])
            nc.gpsimd.tensor_copy(whi[:], chunk(n)).then_inc(out0_hi, 1)
            pool.wait_ge(out0_hi, 1)
            nc.gpsimd.tensor_tensor(wlo[:], chunk(n), whi[:].bitcast(F32), ALU.subtract).then_inc(out0_split, 1)
            for k in range(1, KD):
                pool.wait_ge(sq2, k + 1)
                if k > 1:
                    pool.wait_ge(sq2_sum, k - 1)
                nc.gpsimd.tensor_tensor(rstd2[:], h2T[:, 0, :] if k == 1 else rstd2[:], h2T[:, k, :], ALU.add).then_inc(sq2_sum, 1)
            pool.sem_inc(u_lo, 2)
            pool.sem_inc(g_sb, 2)

            def split_u(n, r):
                pool.wait_ge(u_hi, n + 1)
                nc.gpsimd.tensor_tensor(ulo[r % 2][:], uraw[r % 2][:], uhi[r % 2][:].bitcast(F32), ALU.subtract).then_inc(u_lo, 1)

            def sum_gates(q, col, half):
                pool.wait_ge(g_parts, q + 3)
                nc.gpsimd.tensor_tensor(stage[:].rearrange("p i t -> p t i")[:, bass.ds(col, HB), :],
                                        gpart[half][:, :, 0, :], gpart[half][:, :, 1, :], ALU.add).then_inc(g_sb, 1)

            def split_us(first, steps):
                with pool.Fori(0, steps // 4) as i:
                    for r in range(4):
                        split_u(i * 4 + (first + r), r)

            for n in range(2):
                split_u(n, n)
            split_us(2, SOLO)
            with pool.Fori(0, TT) as tt:
                with pool.Fori(0, BOTH // 4) as i:
                    for r in range(4):
                        split_u(i * 4 + (tt * SEG + (SOLO + 2 + r)), r)
                        if r == 0:
                            pool.wait_ge(g_out, tt * (16 * GP) + 16 * GP)
                        for half in range(2):
                            sum_gates(i * 8 + (tt * (2 * BOTH) + (2 * r + half)), i * (8 * HB) + HB * (2 * r + half), half)
                split_us(tt * SEG + (SOLO + BOTH + 2), SOLO)
            for n in range(TT * SEG + SOLO + 2, NT):
                split_u(n, n)

        @block.scalar
        def _(act):
            steps = [0]

            def settled(ins):
                steps[0] += 1
                ins.then_inc(act_step, 1)
                act.wait_ge(act_step, steps[0])

            act.sem_inc(gelu_done, 2)
            act.sem_inc(g_parts, 2)
            act.sem_inc(g_out, 16 * GP)
            for b in range(2):
                act.sem_inc(a_out[b], 16)
            act.dma_start(b_cols[:], b_ada).then_inc(small_in, 16)
            act.dma_start(g1[:], norm1_g).then_inc(small_in, 16)
            act.dma_start(g2[:], norm2_g).then_inc(small_in, 16)
            act.dma_start(posq[:], position_cols).then_inc(small_in, 16)
            act.dma_start(g_swa[:, 0, :], swa_q_norm.partition_broadcast(P)).then_inc(small_in, 16)
            act.dma_start(g_swa[:, SH, :], swa_k_norm.partition_broadcast(P)).then_inc(small_in, 16)
            act.dma_start(g_cq[:], mla_q_a_norm.partition_broadcast(P)).then_inc(small_in, 16)
            act.dma_start(g_ckv[:], mla_kv_a_norm.partition_broadcast(P)).then_inc(small_in, 16)
            act.dma_start(g_mla[:, 0, :], mla_q_norm.partition_broadcast(P)).then_inc(small_in, 16)
            act.dma_start(g_mla[:, 1, :], mla_k_norm.partition_broadcast(P)).then_inc(small_in, 16)
            act.dma_start(sinks[:], swa_sinks.partition_broadcast(P)).then_inc(small_in, 16)
            act.dma_start(posk_i, positions.partition_broadcast(P)).then_inc(small_in, 16)
            act.wait_ge(x_in, 16)
            for k in range(KD):
                nc.scalar.activation(hT[:, k, :], res[:, k, :], ACT.Square).then_inc(sq1, 1)
            act.wait_ge(var1, 1)
            nc.scalar.activation(rstd1, rstd1, ACT.Sqrt).then_inc(sd1, 1)
            for k in range(KD):
                act.wait_ge(h_scaled, k + 1)
                nc.scalar.activation(hT[:, k, :], hT[:, k, :], ACT.Identity, bias=ada[:, k:k + 1]).then_inc(h_ready, 1)
            act.dma_start(wuq[:], mla_w_uq.rearrange("(k p) n -> p k n", p=P)).then_inc(up_in, 16)
            act.dma_start(wukv[:], mla_w_ukv).then_inc(up_in, 16)
            for n in range(3):
                if n == 1:
                    act.wait_ge(ang_ready, 1)
                    nc.scalar.activation(trig[:].rearrange("p t s f -> p (t s f)"), kvm_flat[:, 1024:1024 + TT * 32],
                                         ACT.Sin).then_inc(trig_ready, 1)
                cols = chunks[place["in", n]][3]
                for tt in range(TT):
                    q = n * TT + tt
                    act.wait_ge(z_ps, q + 1)
                    dst, src = z[:, tt, n * CH:n * CH + cols], ps[:, q % 6, 0:cols]
                    if n == 0:
                        dst = dst.rearrange("p (g v d) -> p v g d", v=SKV, g=SG)
                        src = src.rearrange("p (v g d) -> p v g d", v=SKV, g=SG)
                    nc.scalar.activation(dst, src, ACT.Copy).then_inc(z_sb, 1)
                    act.wait_ge(z_sb, q + 1)
                    if n == 1:
                        nc.scalar.activation(zsq[:, tt, :], z[:, tt, 0:640], ACT.Square).then_inc(z_stat, 1)
                    if n == 2:
                        settled(nc.scalar.activation(zsq_cq[:, 0:QRANK], z[:, tt, Z_CQ:Z_CKV], ACT.Square,
                                                     accum_out=ss[:, tt, 10:11]))
                        nc.scalar.activation(zsq_cq[:, QRANK:QRANK + KVRANK], z[:, tt, Z_CKV:Z_KR], ACT.Square,
                                             accum_out=ss[:, tt, 11:12]).then_inc(z_stat, 1)
            act.wait_ge(z_var, 1)
            nc.scalar.activation(rz[:], rz[:], ACT.Sqrt).then_inc(z_sd, 1)
            for tt in range(TT):
                act.wait_ge(zt_ps, tt + 1)
                cols = slice(tt * P, (tt + 1) * P)
                b0 = 2 * (tt % 2)
                nc.scalar.activation(qTs[:, :, cols], ps[:, b0, :].rearrange("p (g t) -> p g t", g=SG), ACT.Copy)
                nc.scalar.activation(kcT[:, :, cols], ps[:, b0 + 1, :].rearrange("p (g t) -> p g t", g=4),
                                     ACT.Copy).then_inc(zt_sb, 1)
            def copy_projections(tt):
                act.wait_ge(up_ps, 2 * tt + 1)
                mq = heads(tt).rearrange("p h d -> p (h d)")
                nc.scalar.activation(mq[:, 0:512], ps[:, 0, :], ACT.Copy)
                nc.scalar.activation(mq[:, 512:768], ps[:, 1, 0:256], ACT.Copy).then_inc(up_sb, 1)
                act.wait_ge(up_ps, 2 * tt + 2)
                nc.scalar.activation(kvm[:, tt, :], ps[:, 2:4, :].rearrange("p a b -> p (a b)"), ACT.Copy).then_inc(up_sb, 1)

            def square_heads(tt):
                act.wait_ge(m_roped, tt + 1)
                nc.scalar.activation(msq, heads(tt), ACT.Square).then_inc(m_sq, 1)

            def root_heads(tt):
                act.wait_ge(m_var, tt + 1)
                nc.scalar.activation(mrz[:], mrz[:], ACT.Sqrt).then_inc(m_sd, 1)

            def copy_heads(tt):
                for f in range(4):
                    act.wait_ge(mt_ps, 4 * tt + f + 1)
                    nc.scalar.activation(qkT[0:QK, 4 * f:4 * f + 4, tt * P:(tt + 1) * P],
                                         ps[0:QK, 4 + f % 2, :].rearrange("p (h t) -> p h t", h=4), ACT.Copy).then_inc(mt_sb, 1)

            copy_projections(0)
            copy_projections(1)
            square_heads(0)
            for tt in range(TT):
                root_heads(tt)
                if tt + 2 < TT:
                    copy_projections(tt + 2)
                if tt + 1 < TT:
                    square_heads(tt + 1)
                copy_heads(tt)

            def exponentials(u):
                kind, b, _, _ = units[u]
                act.wait_ge(biased, u + 1)
                nk = len(key_tiles(kind, b)) * P
                for j in range(heads_of(kind)):
                    if kind == "s":
                        src = pb[:, u % 4, j, 256 - nk:257]
                        dst = src
                    else:
                        src = ps[:, u % 3, 0:nk]
                        dst = p_view(u, kind)[:, 0, 0:nk]
                    last = nc.scalar.activation(dst, src, ACT.Exp, bias=nm[:, u % 4, j:j + 1], scale=1.0,
                                                accum_out=sm[:, u % 4, j:j + 1])
                last.then_inc(exp_done, 1)

            def copy_pt(u):
                kind, b, _, _ = units[u]
                act.wait_ge(pt_ps, u + 1)
                if u >= 2:
                    act.wait_ge(o_ps, u - 1)
                slots_ = slice(0, 4) if kind == "s" and b > 0 else slice(1, 4, 2) if kind == "s" else slice(0, b + 1)
                nc.scalar.activation(pt[:, u % 2, slots_, :], ps[:, 4 + u % 2, :].rearrange("p (s q) -> p s q", q=P)[:, slots_, :],
                                     ACT.Copy).then_inc(pt_sb, 1)

            exponentials(0)
            for u in range(NU):
                if u + 1 < NU:
                    exponentials(u + 1)
                copy_pt(u)
            def high_w(key):
                n = place[key]
                act.wait_ge(chunk_in[slot[n][0]], 16 * (slot[n][1] + 1))
                nc.scalar.activation(parts[key][0][:], chunk(n), ACT.Copy).then_inc(w_hi, 1)

            act.wait_ge(o_sb, NU)
            for k in range(KD):
                nc.scalar.activation(oThi[:, k, :], oT[:, k, :], ACT.Copy).then_inc(o_hi, 1)
            high_w(("out", 1))
            for k in range(KD):
                act.wait_ge(x1_ready, k + 1)
                nc.scalar.activation(h2T[:, k, :], res[:, k, :], ACT.Square).then_inc(sq2, 1)
                if k == 5:
                    high_w(("query", 0))
            act.wait_ge(var2, 1)
            nc.scalar.activation(rstd2[:], rstd2[:], ACT.Sqrt).then_inc(sd2, 1)
            for k in range(KD):
                act.wait_ge(h2_scaled, k + 1)
                nc.scalar.activation(h2hi[:, k, :], h2T[:, k, :], ACT.Identity, bias=ada[:, 3 * KD + k:3 * KD + k + 1])\
                    .then_inc(h2_hi, 1)
            high_w(("query", 1))
            for h in range(PH):
                act.wait_ge(qp_ps, h + 1)
                nc.scalar.activation(qpT[:, h, :], ps[:, h % 4, :], ACT.Copy).then_inc(qp_sb, 1)

            def high_u(n, r, count):
                act.wait_ge(u_in[r % 2], count)
                act.wait_ge(a_ps, n + 1)
                nc.scalar.activation(uhi[r % 2][:], uraw[r % 2][:], ACT.Copy).then_inc(u_hi, 1)

            for n in range(2):
                high_u(n, n, 16)
            for tt in range(TT):
                act.wait_ge(key_ps, tt + 1)
                if tt >= 2:
                    act.wait_ge(s_out[tt % 2], 16)
                for f in range(4):
                    last = nc.scalar.activation(sout[tt % 2][:, 4 * f:4 * f + 4, :],
                                                ps[:, 4 * (tt % 2) + f, :].rearrange("p (a n) -> p a n", n=NK), ACT.Copy)
                last.then_inc(s_copied, 1)

            def gelu(n, r, count):
                act.wait_ge(a_ps, n + 3)
                act.wait_ge(a_out[r % 2], count)
                nc.scalar.activation(act_out[r % 2][:], ps[:, r % 2, :], ACT.Gelu).then_inc(gelu_done, 1)
                act.wait_ge(gelu_done, n + 3)
                act.dma_start(gelus[bass.ds(n, 1), :, :].rearrange("a p c -> p (a c)"), act_out[r % 2][:]).then_inc(a_out[r % 2], 16)

            def copy_parts(q, half):
                act.wait_ge(oh_used, q + 3)
                act.wait_ge(g_sb, q + 1)
                nc.scalar.activation(gpart[half][:], ps[:, 2 + 2 * half:4 + 2 * half, :], ACT.Copy).then_inc(g_parts, 1)

            def alone(first, pair, steps, send):
                with act.Fori(0, steps // 4) as i:
                    for r in range(4):
                        pairs = i * 2 + (pair + r // 2)
                        high_u(i * 4 + (first + r + 2), r, pairs * 16 + 32)
                        gelu(i * 4 + (first + r), r, pairs * 16 + 16)
                        if send is not None:
                            rows = bass.ds(i * (4 * P // GP) + r * (P // GP), P // GP)
                            act.dma_start(gates[rows, :, bass.ds(send * P, P)].rearrange("i j t -> j i t"),
                                          stage[:, rows, :]).then_inc(g_out, 16)

            def weights():
                nc.scalar.activation(eW[:], eW[:], ACT.Exp).then_inc(best_exp, 1)

            def segment(tt):
                first_half = tt * (SEG // 2) + SOLO // 2
                with act.Fori(0, BOTH // 4) as i:
                    for r in range(4):
                        n, pairs = i * 4 + (tt * SEG + (SOLO + r)), i * 2 + (first_half + r // 2)
                        high_u(n + 2, r, pairs * 16 + 32)
                        gelu(n, r, pairs * 16 + 16)
                        for half in range(2):
                            copy_parts(i * 8 + (tt * (2 * BOTH) + (2 * r + half)), half)
                act.wait_ge(g_sb, tt * (2 * BOTH) + (2 * BOTH + 2))

            alone(0, 0, GP, None)
            act.wait_ge(best_ready, 1)
            weights()
            alone(GP, GP // 2, SOLO - GP, None)
            with act.Fori(0, TT - 1) as tt:
                segment(tt)
                first, pair = tt * SEG + (SOLO + BOTH), tt * (SEG // 2) + (SOLO + BOTH) // 2
                alone(first, pair, GP, tt)
                act.wait_ge(best_ready, tt + 2)
                weights()
                alone(first + GP, pair + GP // 2, SOLO - GP, None)
            segment(TT - 1)
            alone(TT * SEG, TT * SEG // 2, GP, TT - 1)
            alone(TT * SEG + GP, (TT * SEG + GP) // 2, SOLO - GP, None)
            for n in range(NT - 4, NT):
                if n + 2 < NT:
                    high_u(n + 2, n, n // 2 * 16 + 32)
                gelu(n, n, n // 2 * 16 + 16)

            def high_v(n, r, count, first):
                act.wait_ge(v_in[r], count)
                if not first:
                    act.wait_ge(y_ps, n - 3)
                nc.scalar.activation(vhi[r][:], vraw[r][:], ACT.Copy).then_inc(v_hi, 1)

            for r in range(4):
                high_v(r, r, 16, True)
            with act.Fori(1, NT // 4) as i:
                for r in range(4):
                    high_v(i * 4 + r, r, i * 16 + 16, False)

        @block.tensor
        def _(pe):
            def arrived(n):
                at, before = slot[n]
                pe.wait_ge(chunk_in[at], 16 * (before + 1))

            def modulation(j):
                n = place["ada", j]
                order = ada_order.index(j)
                pe.wait_ge(acc_done, order + 1)
                for q in range(CH // P):
                    col = j * (CH // P) + q
                    last = nc.tensor.matmul(ada_ps[:, col:col + 1], accs[:, order % 2, q * P:(q + 1) * P],
                                            ones[:, 0:1], start=True, stop=True)
                last.then_inc(ada_done, 1)

            pe.sem_inc(oh_used, 2)
            pe.sem_inc(a_ps, 2)
            pe.wait_ge(const, 3)
            for j in ada_order[:2]:
                modulation(j)
            for k in range(KD):
                pe.wait_ge(sq1, k + 1)
                last = nc.tensor.matmul(ps[:, 6, :], ones[:], hT[:, k, :], start=(k == 0), stop=(k == KD - 1))
            last.then_inc(ms1, 1)
            for j in ada_order[2:4]:
                modulation(j)
            for n in range(3):
                at = place["in", n]
                arrived(at)
                cols = chunks[at][3]
                for tt in range(TT):
                    q = n * TT + tt
                    if q >= 6:
                        pe.wait_ge(z_sb, q - 5)
                    for k in range(KD):
                        if q == 0:
                            pe.wait_ge(h_ready, k + 1)
                        last = nc.tensor.matmul(ps[:, q % 6, 0:cols], hT[:, k, tt * P:(tt + 1) * P],
                                                chunk(at)[:, k, 0:cols], start=(k == 0), stop=(k == KD - 1))
                    last.then_inc(z_ps, 1)
                    if 2 <= q < 8:
                        modulation(ada_order[q + 2])
                pe.wait_ge(z_ps, n * TT + TT)
                pe.sem_inc(chunk_used[slot[at][0]], 1)
            for j in ada_order[10:]:
                modulation(j)
            for tt in range(TT):
                pe.wait_ge(zn_ready, tt + 1)
                if tt == 0:
                    pe.wait_ge(z_sb, 3 * TT)
                if tt >= 2:
                    pe.wait_ge(zt_sb, tt - 1)
                b0 = 2 * (tt % 2)
                for g in range(SG):
                    nc.tensor.transpose(ps[:, b0, g * P:(g + 1) * P], z[:, tt, g * P:(g + 1) * P], ident[:])
                for f, c0 in enumerate((Z_K, Z_CQ, Z_CQ + P, Z_CKV)):
                    last = nc.tensor.transpose(ps[:, b0 + 1, f * P:(f + 1) * P], z[:, tt, c0:c0 + P], ident[:])
                last.then_inc(zt_ps, 1)
            pe.wait_ge(up_in, 32)
            pe.wait_ge(zt_sb, TT)

            def project(tt):
                cols = slice(tt * P, (tt + 1) * P)
                if tt >= 1:
                    pe.wait_ge(up_sb, 2 * tt - 1)
                for bank, c0, n in ((0, 0, 512), (1, 512, 256)):
                    for k in range(2):
                        last = nc.tensor.matmul(ps[:, bank, 0:n], kcT[:, 1 + k, cols], wuq[:, k, c0:c0 + n],
                                                start=(k == 0), stop=(k == 1))
                last.then_inc(up_ps, 1)
                if tt >= 1:
                    pe.wait_ge(up_sb, 2 * tt)
                for bank, c0 in ((2, 0), (3, 512)):
                    last = nc.tensor.matmul(ps[:, bank, :], kcT[:, 3, cols], wukv[:, c0:c0 + 512], start=True, stop=True)
                last.then_inc(up_ps, 1)

            def turn_heads(tt):
                pe.wait_ge(m_ready, tt + 1)
                for f in range(4):
                    if 4 * tt + f >= 2:
                        pe.wait_ge(mt_sb, 4 * tt + f - 1)
                    for h in range(4):
                        last = nc.tensor.transpose(ps[0:QK, 4 + f % 2, h * P:(h + 1) * P], heads(tt)[:, 4 * f + h, :], ident[:])
                    last.then_inc(mt_ps, 1)

            for tt in range(3):
                project(tt)
            turn_heads(0)
            project(3)
            for tt in range(1, TT):
                turn_heads(tt)
            pe.wait_ge(mt_sb, 4 * TT)

            def scores(u):
                kind, b, sub, j0 = units[u]
                if u >= 3:
                    pe.wait_ge(exp_done, u - 2)
                q = slice(b * P, (b + 1) * P)
                tiles = key_tiles(kind, b)
                keys_ = slice(tiles[0] * P, (b + 1) * P)
                if kind == "s":
                    rows = slice(sub * SD, (sub + 1) * SD)
                    for j in range(2):
                        c0 = j * 256 + (256 - len(tiles) * P)
                        last = nc.tensor.matmul(ps[:, u % 3, c0:c0 + len(tiles) * P], qTs[rows, j0 + j, q], kcT[rows, 0, keys_],
                                                start=True, stop=True)
                else:
                    last = nc.tensor.matmul(ps[:, u % 3, 0:len(tiles) * P], qkT[0:QK, sub, q], qkT[0:QK, MH + sub, keys_],
                                            start=True, stop=True)
                last.then_inc(s_done, 1)

            def transposes(u):
                kind, b, _, _ = units[u]
                pe.wait_ge(p_ready, u + 1)
                if u >= 2:
                    pe.wait_ge(pt_sb, u - 1)
                for slot, j, c0, _ in pt_slots(kind, b):
                    last = nc.tensor.transpose(ps[:, 4 + u % 2, slot * P:(slot + 1) * P],
                                               p_view(u, kind)[:, j, c0:c0 + P], ident[:])
                last.then_inc(pt_ps, 1)

            def values(u):
                kind, b, sub, j0 = units[u]
                pe.wait_ge(pt_sb, u + 1)
                if u >= 2:
                    pe.wait_ge(o_sb, u - 1)
                tiles = key_tiles(kind, b)
                for slot, j, _, kb in pt_slots(kind, b):
                    half = j if kind == "s" else sub % 2
                    if kind == "s":
                        v = z[:, kb, Z_V + sub * SD:Z_V + (sub + 1) * SD]
                    else:
                        v0 = sub * (NOPE + VD) + NOPE
                        v = kvm[:, kb, v0:v0 + VD]
                    last = nc.tensor.matmul(ps[64 * half:64 * half + 64, 3 * (u % 2) + 3, 0:P], v, pt[:, u % 2, slot, :],
                                            start=(kb == tiles[0]), stop=(kb == tiles[-1]))
                last.then_inc(o_ps, 1)

            scores(0)
            scores(1)
            for u in range(NU):
                if u + 2 < NU:
                    scores(u + 2)
                transposes(u)
                if u >= 1:
                    values(u - 1)
            values(NU - 1)
            pe.wait_ge(o_sb, NU)

            def product(out, key, at, hi, lo, ready):
                whi, wlo = parts[key]
                for k in range(KD):
                    if ready is not None:
                        pe.wait_ge(ready, k + 1)
                    nc.tensor.matmul(out, whi[:, k, at:at + P], hi[:, k, :], start=(k == 0), stop=False)
                    nc.tensor.matmul(out, whi[:, k, at:at + P], lo[:, k, :], start=False, stop=False)
                    last = nc.tensor.matmul(out, wlo[:, k, at:at + P], hi[:, k, :], start=False, stop=(k == KD - 1))
                return last

            for m in range(KD):
                n = place["out", m // 4]
                if m == 0:
                    pe.wait_ge(out0_split, 1)
                if m == 4:
                    pe.wait_ge(w_split, 1)
                if m >= 4:
                    pe.wait_ge(x1_ready, m - 3)
                product(ps[:, m % 4, :], ("out", m // 4), (m % 4) * P, oThi, oTlo, o_split if m == 0 else None).then_inc(mix_ps, 1)
                if m % 4 == 3:
                    pe.wait_ge(mix_ps, m + 1)
                    pe.sem_inc(chunk_used[slot[n][0]], 1)
            pe.wait_ge(sq2_sum, KD - 1)
            nc.tensor.matmul(ps[:, 5, :], ones[:], rstd2[:], start=True, stop=True).then_inc(ms2, 1)
            for h in range(PH):
                n = place["query", h // 4]
                if h % 4 == 0:
                    pe.wait_ge(w_split, 2 + h // 4)
                if h >= 4:
                    pe.wait_ge(qp_sb, h - 3)
                product(ps[:, h % 4, :], ("query", h // 4), (h % 4) * P, h2hi, h2lo, h2_split if h == 0 else None).then_inc(qp_ps, 1)
                if h % 4 == 3:
                    pe.wait_ge(qp_ps, h + 1)
                    pe.sem_inc(chunk_used[slot[n][0]], 1)
            pe.wait_ge(sk_in, 16)
            pe.wait_ge(qp_sb, PH)

            def key_scores(tt):
                for h in range(PH):
                    for half in range(2):
                        rows = slice(PD * half, PD * (half + 1))
                        last = nc.tensor.matmul(ps[:, 4 * (tt % 2) + 2 * half + h // 4, (h % 4) * P:(h % 4 + 1) * P],
                                                qpT[rows, h, tt * P:(tt + 1) * P], skT[rows, h, :], start=True, stop=True)
                last.then_inc(key_ps, 1)

            for tt in range(TT):
                if tt >= 2:
                    pe.wait_ge(s_copied, tt - 1)
                key_scores(tt)

            pe.wait_ge(h2_split, KD)
            pe.wait_ge(s_copied, TT - 1)

            def dot(n, r):
                pe.wait_ge(u_lo, n + 3)
                pe.wait_ge(gelu_done, n + 1)
                for k in range(KD):
                    cols = slice(k * P, (k + 1) * P)
                    nc.tensor.matmul(ps[:, r % 2, :], uhi[r % 2][:, cols], h2hi[:, k, :], start=(k == 0), stop=False)
                    nc.tensor.matmul(ps[:, r % 2, :], uhi[r % 2][:, cols], h2lo[:, k, :], start=False, stop=False)
                    last = nc.tensor.matmul(ps[:, r % 2, :], ulo[r % 2][:, cols], h2hi[:, k, :], start=False, stop=(k == KD - 1))
                last.then_inc(a_ps, 1)

            def token_gates(q, half):
                pe.wait_ge(oh_ready, q + 1)
                pe.wait_ge(g_parts, q + 1)
                for t in range(HB):
                    last = nc.tensor.matmul(ps[:, 2 + 2 * half + t // 2, (t % 2) * 2 * P:(t % 2 + 1) * 2 * P], ohJ[half][:, t, :],
                                            ohW[half][:, t, :, :].rearrange("p s i -> p (s i)"), start=True, stop=True)
                last.then_inc(oh_used, 1)

            def dots(first, steps):
                with pe.Fori(0, steps // 4) as i:
                    for r in range(4):
                        dot(i * 4 + (first + r), r)

            dots(0, SOLO)
            with pe.Fori(0, TT) as tt:
                pe.wait_ge(ijw_ready, tt + 1)
                for f in range(3):
                    last = nc.tensor.transpose(ps[:, 6, f * P:(f + 1) * P], IJW[:, f, :, :], ident[:])
                last.then_inc(ijw_ps, 1)
                with pe.Fori(0, BOTH // 4) as i:
                    for r in range(4):
                        dot(tt * SEG + i * 4 + (SOLO + r), r)
                        for half in range(2):
                            token_gates(tt * (2 * BOTH) + i * 8 + (2 * r + half), half)
                pe.wait_ge(oh_used, tt * (2 * BOTH) + (2 * BOTH + 2))
                pe.sem_inc(c_space, 1)
                dots(tt * SEG + (SOLO + BOTH), SOLO)
            dots(TT * SEG + SOLO, NT - TT * SEG - SOLO)

            def mix(n, r, first):
                pe.wait_ge(v_lo, n + 1)
                pe.wait_ge(c_lo, n + 1)
                for d in range(KD):
                    cols = slice(d * P, (d + 1) * P)
                    nc.tensor.matmul(ps[:, d, :], vhi[r][:, cols], chi[r][:], start=first, stop=False)
                    nc.tensor.matmul(ps[:, d, :], vhi[r][:, cols], clo[r][:], start=False, stop=False)
                    last = nc.tensor.matmul(ps[:, d, :], vlo[r][:, cols], chi[r][:], start=False, stop=False)
                last.then_inc(y_ps, 1)

            pe.wait_ge(gelu_done, NT + 2)
            for r in range(4):
                mix(r, r, r == 0)
            with pe.Fori(1, NT // 4 - 1) as i:
                for r in range(4):
                    mix(i * 4 + r, r, False)
            pe.wait_ge(v_lo, NT)
            pe.wait_ge(c_lo, NT)
            for d in range(KD):
                cols = slice(d * P, (d + 1) * P)
                for r in range(4):
                    nc.tensor.matmul(ps[:, d, :], vhi[r][:, cols], chi[r][:], start=False, stop=False)
                    nc.tensor.matmul(ps[:, d, :], vhi[r][:, cols], clo[r][:], start=False, stop=False)
                    last = nc.tensor.matmul(ps[:, d, :], vlo[r][:, cols], chi[r][:], start=False, stop=(r == 3))
                last.then_inc(y_ps, 1)

        @block.vector
        def _(dve):
            steps = [0]

            def settled(ins):
                steps[0] += 1
                ins.then_inc(dve_step, 1)
                dve.wait_ge(dve_step, steps[0])

            tt_ = nc.vector.tensor_tensor
            def norm(bank, rstd, sums, var, sd):
                dve.wait_ge(sums, 1)
                nc.vector.tensor_scalar(rstd, ps[:, bank, :], 1.0 / D, EPS, ALU.mult, ALU.add).then_inc(var, 1)
                dve.wait_ge(sd, 1)
                settled(nc.vector.reciprocal(rstd, rstd))

            def modulate(j):
                n = place["ada", j]
                order = ada_order.index(j)
                at, before = slot[n]
                dve.wait_ge(chunk_in[at], 16 * (before + 1))
                if order >= 2:
                    dve.wait_ge(ada_done, order - 1)
                acc = accs[:, order % 2, :]
                settled(nc.vector.tensor_scalar(acc, chunk(n)[:, 0, :], cT[:, 0:1], None, ALU.mult))
                for k in range(1, KD):
                    settled(nc.vector.scalar_tensor_tensor(out=acc, in0=chunk(n)[:, k, :], scalar=cT[:, k:k + 1],
                                                           in1=acc, op0=ALU.mult, op1=ALU.add))
                dve.sem_inc(chunk_used[at], 1)
                dve.sem_inc(acc_done, 1)

            def modulation(piece, chunks_done):
                dve.wait_ge(ada_done, chunks_done)
                cols = slice(piece * KD, (piece + 1) * KD)
                settled(tt_(ada[:, cols], ada_ps[:, cols], b_cols[:, cols], ALU.add))

            dve.wait_ge(c_in, 16)
            for j in ada_order[:3]:
                modulate(j)
            norm(6, rstd1, ms1, var1, sd1)
            modulate(ada_order[3])
            dve.wait_ge(small_in, 16 * NSMALL)
            modulation(1, 4)
            settled(nc.vector.scalar_tensor_tensor(out=gs[:], in0=ada[:, KD:2 * KD], scalar=1.0, in1=g1[:],
                                                   op0=ALU.add, op1=ALU.mult))
            modulation(0, 4)
            for k in range(KD):
                nc.vector.scalar_tensor_tensor(out=hT[:, k, :], in0=res[:, k, :], scalar=gs[:, k:k + 1], in1=rstd1,
                                               op0=ALU.mult, op1=ALU.mult).then_inc(h_scaled, 1)
            for f in range(ROPE // 2):
                last = nc.vector.memset(freq[:, f:f + 1], ROPE_THETA ** (-2.0 * f / ROPE))
            settled(last)
            tt_(g_mla[:, 0, :], g_mla[:, 0, :], g_mla[:, 1, :], ALU.mult)
            settled(tt_(g_swa[:, 0, :], g_swa[:, 0, :], g_swa[:, SH, :], ALU.mult))
            nc.vector.tensor_scalar(g_mla[:, 0, :], g_mla[:, 0, :], QK ** -0.5, None, ALU.mult)
            settled(nc.vector.tensor_scalar(g_swa[:, 0, :], g_swa[:, 0, :], SD ** -0.5, None, ALU.mult))
            nc.vector.tensor_copy(g_swa[:, 1:SH, :], g_swa[:, 0, :].unsqueeze(1).to_broadcast([P, SH - 1, SD]))
            nc.vector.tensor_copy(posk, posk_i)
            settled(nc.vector.tensor_copy(posqf[:], posq[:]))
            for sc in range(2):
                settled(tt_(ang[:, :, sc, :], posqf[:].unsqueeze(2).to_broadcast([P, TT, ROPE // 2]),
                            freq[:].unsqueeze(1).to_broadcast([P, TT, ROPE // 2]), ALU.mult))
                nc.vector.tensor_scalar(turns[:, :, sc, :], ang[:, :, sc, :], 0.15915494309189535,
                                        0.25 if sc == 0 else 0.0, ALU.mult, ALU.add)
            settled(nc.vector.memset(sm[:], 0.0))
            settled(nc.vector.tensor_scalar(turns, turns, ROUND, None, ALU.add))
            settled(nc.vector.tensor_scalar(turns, turns, ROUND, None, ALU.subtract))
            for part in (PI2_A, PI2_B, PI2_C):
                settled(nc.vector.scalar_tensor_tensor(out=ang.rearrange("p t s f -> p (t s f)"),
                                                       in0=turns.rearrange("p t s f -> p (t s f)"), scalar=-part,
                                                       in1=ang.rearrange("p t s f -> p (t s f)"), op0=ALU.mult, op1=ALU.add))
            settled(nc.vector.tensor_scalar(ang[:, :, 0, :], ang[:, :, 0, :], 1.5707963267948966, None, ALU.add))
            nc.vector.tensor_scalar(ang, ang, 3.1415925, -3.1415925, ALU.min, ALU.max).then_inc(ang_ready, 1)
            for b in range(TT):
                k0 = 0 if b else P
                settled(nc.vector.tensor_scalar(distm[:, b, k0:256], posk[:, (b - 1) * P + k0:(b + 1) * P],
                                                posqf[:, b:b + 1], None, ALU.subtract))
                settled(nc.vector.scalar_tensor_tensor(out=distm[:, b, k0:256], in0=distm[:, b, k0:256], scalar=-1.0,
                                                       in1=distm[:, b, k0:256], op0=ALU.mult, op1=ALU.max))
                if b:
                    nc.vector.memset(distm[0:64, b, 0:64], MASKED)
                    nc.vector.memset(distm[64:128, b, 0:128], MASKED)
                settled(nc.vector.memset(distm[0:64, b, 192:256], MASKED))

            for j in ada_order[4:]:
                modulate(j)
            for tt in range(TT):
                dve.wait_ge(z_stat, tt + 1)
                nc.vector.tensor_reduce(ss[:, tt, 0:10], zsq[:, tt, :].rearrange("p (h d) -> p h d", d=SD), X, ALU.add)
            dve.wait_ge(z_stat, 2 * TT)
            nc.vector.tensor_scalar(rz[:, :, 10:11], ss[:, :, 10:11], 1.0 / QRANK, EPS, ALU.mult, ALU.add)
            settled(nc.vector.tensor_scalar(rz[:, :, 11:12], ss[:, :, 11:12], 1.0 / KVRANK, EPS, ALU.mult, ALU.add))
            nc.vector.tensor_scalar(rz[:, :, 0:10], ss[:, :, 0:10], 1.0 / SD, EPS, ALU.mult, ALU.add).then_inc(z_var, 1)
            dve.wait_ge(z_sd, 1)
            settled(nc.vector.reciprocal(rz[:], rz[:]))
            for tt in range(TT):
                zh = z[:, tt, 0:640].rearrange("p (h d) -> p h d", d=SD)
                zc, zk = z[:, tt, Z_CQ:Z_CKV], z[:, tt, Z_CKV:Z_KR]
                tt_(zh, zh, rz[:, tt, 0:10].unsqueeze(2).to_broadcast([P, 10, SD]), ALU.mult)
                nc.vector.scalar_tensor_tensor(out=zc, in0=zc, scalar=rz[:, tt, 10:11], in1=g_cq[:],
                                               op0=ALU.mult, op1=ALU.mult)
                settled(nc.vector.scalar_tensor_tensor(out=zk, in0=zk, scalar=rz[:, tt, 11:12], in1=g_ckv[:],
                                                       op0=ALU.mult, op1=ALU.mult))
                tt_(zh[:, 0:SH, :], zh[:, 0:SH, :], g_swa[:, 0:SH, :], ALU.mult).then_inc(zn_ready, 1)
            dve.wait_ge(trig_ready, 1)

            def rope(tt):
                dve.wait_ge(m_built, tt + 1)
                m = heads(tt)
                x1, x2 = m[:, :, NOPE:NOPE + 16], m[:, :, NOPE + 16:QK]
                cos = trig[:, tt, 0, :].unsqueeze(1).to_broadcast([P, 2 * MH, 16])
                sin = trig[:, tt, 1, :].unsqueeze(1).to_broadcast([P, 2 * MH, 16])
                tt_(ropet[0], x1, cos, ALU.mult)
                tt_(ropet[1], x2, sin, ALU.mult)
                tt_(ropet[2], x1, sin, ALU.mult)
                settled(tt_(ropet[3], x2, cos, ALU.mult))
                tt_(x1, ropet[0], ropet[1], ALU.subtract)
                tt_(x2, ropet[2], ropet[3], ALU.add).then_inc(m_roped, 1)

            rope(0)
            for tt in range(TT):
                dve.wait_ge(m_sq, tt + 1)
                settled(nc.vector.tensor_reduce(mss[:], msq, X, ALU.add))
                nc.vector.tensor_scalar(mrz[:], mss[:], 1.0 / QK, EPS, ALU.mult, ALU.add).then_inc(m_var, 1)
                if tt + 1 < TT:
                    rope(tt + 1)
                dve.wait_ge(m_sd, tt + 1)
                m = heads(tt)
                settled(nc.vector.reciprocal(mrz[:], mrz[:]))
                settled(tt_(m, m, mrz[:].unsqueeze(2).to_broadcast([P, 2 * MH, QK]), ALU.mult))
                tt_(m[:, 0:MH, :], m[:, 0:MH, :], g_mla[:, 0, :].unsqueeze(1).to_broadcast([P, MH, QK]), ALU.mult).then_inc(m_ready, 1)

            def bias_and_max(u):
                kind, b, sub, j0 = units[u]
                dve.wait_ge(s_done, u + 1)
                if u >= 4:
                    dve.wait_ge(pt_ps, u - 3)
                nk = len(key_tiles(kind, b)) * P
                if kind == "s":
                    k0 = 256 - nk
                    for j in range(2):
                        nc.vector.scalar_tensor_tensor(out=pb[:, u % 4, j, k0:256], in0=distm[:, b, k0:256],
                                                       scalar=-slope(sub * SG + j0 + j), in1=ps[:, u % 3, j * 256 + k0:j * 256 + 256],
                                                       op0=ALU.mult, op1=ALU.add)
                    h0 = sub * SG + j0
                    settled(nc.vector.tensor_copy(pb[:, u % 4, :, 256:257], sinks[:, h0:h0 + 2].unsqueeze(2)))
                    nc.vector.tensor_reduce(nm[:, u % 4, :], pb[:, u % 4, :, k0:257], X, ALU.max, negate=True).then_inc(biased, 1)
                else:
                    settled(nc.vector.memset(ps[0:64, u % 3, b * P + 64:(b + 1) * P], NEG))
                    nc.vector.tensor_reduce(nm[:, u % 4, 0:1], ps[:, u % 3, 0:nk], X, ALU.max, negate=True).then_inc(biased, 1)

            def scale_probs(u):
                kind, b, _, _ = units[u]
                dve.wait_ge(exp_done, u + 1)
                nj = heads_of(kind)
                nk = len(key_tiles(kind, b)) * P
                settled(nc.vector.reciprocal(rsm[:, u % 4, 0:nj], sm[:, u % 4, 0:nj]))
                for j in range(nj):
                    v = pb[:, u % 4, j, 256 - nk:256] if kind == "s" else p_view(u, kind)[:, 0, 0:nk]
                    last = nc.vector.tensor_scalar(v, v, rsm[:, u % 4, j:j + 1], None, ALU.mult)
                last.then_inc(p_ready, 1)

            def copy_out(u):
                kind, b, sub, j0 = units[u]
                dve.wait_ge(o_ps, u + 1)
                cols = slice(b * P, (b + 1) * P)
                if kind == "s":
                    ins = nc.vector.tensor_copy(oT[:, 2 * sub + j0 // 2, cols], ps[:, 3 * (u % 2) + 3, 0:P])
                else:
                    rows = slice(64 * (sub % 2), 64 * (sub % 2) + 64)
                    ins = nc.vector.tensor_copy(oT[rows, 4 + sub // 2, cols], ps[rows, 3 * (u % 2) + 3, 0:P])
                ins.then_inc(o_sb, 1)

            for piece in (2, 4, 3, 5):
                modulation(piece, 12)
            settled(nc.vector.scalar_tensor_tensor(out=gs[:], in0=ada[:, 4 * KD:5 * KD], scalar=1.0, in1=g2[:],
                                                   op0=ALU.add, op1=ALU.mult))
            bias_and_max(0)
            for u in range(NU):
                if u + 1 < NU:
                    bias_and_max(u + 1)
                scale_probs(u)
                if u >= 2:
                    copy_out(u - 2)
            copy_out(NU - 2)
            copy_out(NU - 1)
            def low_w(key, count):
                dve.wait_ge(w_hi, count)
                hi, lo = parts[key]
                tt_(lo[:], chunk(place[key]), hi[:].bitcast(F32), ALU.subtract).then_inc(w_split, 1)

            for k in range(KD):
                dve.wait_ge(o_hi, k + 1)
                tt_(oTlo[:, k, :], oT[:, k, :], oThi[:, k, :].bitcast(F32), ALU.subtract).then_inc(o_split, 1)
            low_w(("out", 1), 1)
            for m in range(KD):
                dve.wait_ge(mix_ps, m + 1)
                nc.vector.scalar_tensor_tensor(out=res[:, m, :], in0=ps[:, m % 4, :], scalar=ada[:, 2 * KD + m:2 * KD + m + 1],
                                               in1=res[:, m, :], op0=ALU.mult, op1=ALU.add).then_inc(x1_ready, 1)
                if m == 5:
                    low_w(("query", 0), 2)
            norm(5, rstd2[:], ms2, var2, sd2)

            def low_h2(k):
                dve.wait_ge(h2_hi, k + 1)
                nc.vector.scalar_tensor_tensor(out=h2lo[:, k, :], in0=h2T[:, k, :], scalar=ada[:, 3 * KD + k:3 * KD + k + 1],
                                               in1=h2hi[:, k, :].bitcast(F32), op0=ALU.add, op1=ALU.subtract).then_inc(h2_split, 1)

            for k in range(KD):
                nc.vector.scalar_tensor_tensor(out=h2T[:, k, :], in0=res[:, k, :], scalar=gs[:, k:k + 1], in1=rstd2[:],
                                               op0=ALU.mult, op1=ALU.mult).then_inc(h2_scaled, 1)
                if k:
                    low_h2(k - 1)
            low_h2(KD - 1)
            low_w(("query", 1), 3)

            def top16(vals, idx, rows, n):
                for a in range(n):
                    last = nc.vector.max(vals(a)[:, 0:8], rows(a))
                settled(last)
                for a in range(n):
                    last = nc.vector.max_index(idx(a)[:, 0:8], vals(a)[:, 0:8], rows(a))
                settled(last)
                for a in range(n):
                    last = nc.vector.match_replace(rows(a), vals(a)[:, 0:8], rows(a), -3.0e38)
                settled(last)
                for a in range(n):
                    last = nc.vector.max(vals(a)[:, 8:16], rows(a))
                settled(last)
                for a in range(n):
                    last = nc.vector.max_index(idx(a)[:, 8:16], vals(a)[:, 8:16], rows(a))
                settled(last)

            for tt in range(TT):
                dve.wait_ge(s_in, tt * 16 + 16)
                top16(lambda a: sv[:, a % PH, a // PH, :], lambda a: six[:, a % PH, a // PH, :], lambda a: s[:, a, :], 2 * PH)
                nc.vector.tensor_copy(sixf[:], six[:])
                settled(tt_(cand[:], sv[:, :, 0, :].unsqueeze(3).to_broadcast([P, PH, KTOP, KTOP]),
                           sv[:, :, 1, :].unsqueeze(2).to_broadcast([P, PH, KTOP, KTOP]), ALU.add))
                top16(lambda a: best[:, a, :], lambda a: bi[:, a, :],
                      lambda a: cand[:, a, :, :].rearrange("p i j -> p (i j)"), PH)
                tt_(eW[:], best[:], best[:, :, 0:1].to_broadcast([P, PH, KTOP]), ALU.subtract).then_inc(best_ready, 1)
                nc.vector.tensor_scalar(bia[:, 0, :, :], bi[:], 4, None, ALU.logical_shift_right)
                settled(nc.vector.tensor_scalar(bia[:, 1, :, :], bi[:], 15, None, ALU.bitwise_and))
                settled(nc.vector.tensor_copy(abf[:], bia[:]))
                for half in range(2):
                    settled(tt_(eq, abf[:, half, :, :].unsqueeze(3).to_broadcast([P, PH, KTOP, KTOP]),
                               iota[:, 0:KTOP].unsqueeze(1).unsqueeze(1).to_broadcast([P, PH, KTOP, KTOP]), ALU.is_equal))
                    settled(tt_(eq, eq, sixf[:, :, half, :].unsqueeze(2).to_broadcast([P, PH, KTOP, KTOP]), ALU.mult))
                    settled(nc.vector.tensor_reduce(IJW[:, half, :, :], eq, X, ALU.add))
                dve.sem_inc(s_free, 1)
                dve.wait_ge(best_exp, tt + 1)
                settled(nc.vector.tensor_reduce(eS[:], eW[:], X, ALU.add))
                settled(nc.vector.reciprocal(eR[:], eS[:]))
                tt_(IJW[:, 2, :, :], eW[:], eR[:].unsqueeze(2).to_broadcast([P, PH, KTOP]), ALU.mult).then_inc(ijw_ready, 1)
                dve.wait_ge(ijw_ps, tt + 1)
                settled(nc.vector.tensor_copy(slots[:, 0:3, :], ps[:, 6, 0:3 * P].rearrange("p (a t) -> p a t", a=3)))
                settled(nc.vector.tensor_copy(slots[:, 3, :].bitcast(F32R), slots[:, 2, :]))
                settled(tt_(slots[:, 4, :], slots[:, 2, :], slots[:, 3, :], ALU.subtract))
                def one_hot(q, col, half):
                    dve.wait_ge(oh_used, q + 1)
                    cols = bass.ds(col, HB)
                    each = iota[:].unsqueeze(1).to_broadcast([P, HB, P])
                    tt_(eqI[:, half, :, :], each, slots[:, 0, cols].unsqueeze(2).to_broadcast([P, HB, P]), ALU.is_equal)\
                        .then_inc(eq_ready, 1)
                    tt_(ohJ[half][:], each, slots[:, 1, cols].unsqueeze(2).to_broadcast([P, HB, P]), ALU.is_equal)
                    dve.wait_ge(eq_ready, q + 1)
                    tt_(ohW[half][:], eqI[:, half, :, :].unsqueeze(2).to_broadcast([P, HB, 2, P]),
                        slots[:, 3:5, cols].rearrange("p s t -> p t s").unsqueeze(3).to_broadcast([P, HB, 2, P]), ALU.mult)\
                        .then_inc(oh_ready, 1)

                with dve.Fori(0, BOTH) as i:
                    for half in range(2):
                        one_hot(i * 2 + (tt * 2 * BOTH + half), i * (2 * HB) + HB * half, half)

            def low_v(n, r):
                dve.wait_ge(v_hi, n + 1)
                tt_(vlo[r][:], vraw[r][:], vhi[r][:].bitcast(F32), ALU.subtract).then_inc(v_lo, 1)

            def weigh(n, r, count, first):
                dve.wait_ge(gate_in[r], count)
                dve.wait_ge(act_back[r], count)
                if not first or r >= 2:
                    dve.wait_ge(c_lo, n - 1)
                c = cf[r % 2]
                tt_(c[:], act_in[r][:], gate[r][:], ALU.mult).then_inc(c_mul, 1)
                dve.wait_ge(c_mul, n + 1)
                nc.vector.tensor_copy(chi[r][:], c[:]).then_inc(c_hi, 1)
                dve.wait_ge(c_hi, n + 1)
                tt_(clo[r][:], c[:], chi[r][:].bitcast(F32), ALU.subtract).then_inc(c_lo, 1)

            for r in range(4):
                low_v(r, r)
                weigh(r, r, 16, True)
            with dve.Fori(1, NT // 4) as i:
                for r in range(4):
                    low_v(i * 4 + r, r)
                    weigh(i * 4 + r, r, i * 16 + 16, False)
            for d in range(KD):
                dve.wait_ge(y_ps, NT - 4 + d + 1)
                nc.vector.scalar_tensor_tensor(out=res[:, d, :], in0=ps[:, d, :], scalar=ada[:, 5 * KD + d:5 * KD + d + 1],
                                               in1=res[:, d, :], op0=ALU.mult, op1=ALU.add).then_inc(y_sb, 1)


def kernel(**inputs):
    import numpy as np
    import concourse.bacc as bacc
    from concourse.bass_utils import run_bass_kernel_spmd as run

    a = {n: np.asarray(v) for n, v in inputs.items()}

    def cols(v):
        return np.ascontiguousarray(v.reshape(-1, P).T)

    sent = {
        "xT": np.ascontiguousarray(a["x"][0].T.reshape(KD, P, T).transpose(1, 0, 2)),
        "c": cols(a["c"][0]),
        "positions": np.ascontiguousarray(a["positions"][0]),
        "position_cols": cols(a["positions"][0]),
        "w_ada": a["w_ada"][0], "b_ada": cols(a["b_ada"][0]),
        "norm1_g": cols(a["norm1_g"][0]), "norm2_g": cols(a["norm2_g"][0]),
        "w_in": a["w_in"][0],
        "swa_q_norm": a["swa_q_norm"][0], "swa_k_norm": a["swa_k_norm"][0], "swa_sinks": a["swa_sinks"][0],
        "mla_q_a_norm": a["mla_q_a_norm"][0], "mla_kv_a_norm": a["mla_kv_a_norm"][0],
        "mla_w_uq": a["mla_w_uq"][0], "mla_w_ukv": a["mla_w_ukv"][0],
        "mla_q_norm": a["mla_q_norm"][0], "mla_k_norm": a["mla_k_norm"][0],
        "w_out": a["w_out"][0], "peer_w_query": a["peer_w_query"][0],
        "sub_keys": a["peer_sub_keys"][0].transpose(1, 3, 0, 2).reshape(P, PH, NK),
        "u_tiles": a["peer_u"][0].reshape(NT, P, KD, P).transpose(0, 3, 2, 1).reshape(NT, P, D),
        "v_tiles": a["peer_v"][0].reshape(NT, P, D),
    }
    sent = {n: np.ascontiguousarray(v) for n, v in sent.items()}
    nc = bacc.Bacc("TRN2", target_bir_lowering=False, num_devices=1)
    args = {n: nc.dram_tensor(f"in_{n}", v.shape, mybir.dt.from_np(v.dtype), kind="ExternalInput").ap()
            for n, v in sent.items()}
    args["outT"] = nc.dram_tensor("out_T", (KD, P, T), F32, kind="ExternalOutput").ap()
    build(nc, **args)
    r = run(nc, [{f"in_{n}": v for n, v in sent.items()}], core_ids=[0])
    return np.ascontiguousarray(r.results[0]["out_T"].reshape(D, T).T)[None]
```

```python
import concourse.bass as bass
from concourse import mybir
from concourse.alu_op_type import AluOpType as ALU
from contextlib import ExitStack

F32 = mybir.dt.float32
F32R = mybir.dt.float32r
I32 = mybir.dt.int32
U32 = mybir.dt.uint32
ACT = mybir.ActivationFunctionType
X = mybir.AxisListType.X

P = 128
D = 1024
T = 512
KD = D // P
TT = T // P
EPS = 1e-6
NEG = -1e30
SH, SKV, SD = 8, 2, 64
SG = SH // SKV
MH, NOPE, ROPE, VD = 8, 64, 32, 64
QK = NOPE + ROPE
QRANK, KVRANK = 256, 128
IN_COLS = SH * SD + 2 * SKV * SD + QRANK + KVRANK + ROPE
Z_K = SH * SD
Z_V = Z_K + SKV * SD
Z_CQ = Z_V + SKV * SD
Z_CKV = Z_CQ + QRANK
Z_KR = Z_CKV + KVRANK
ROPE_THETA = 10000.0
PH, NK, KTOP, PD = 8, 128, 16, 64
NT = NK
HB = 4
SOLO, BOTH, GP = 12, P // (2 * HB), 8
SEG = SOLO + BOTH
CH = 512
DOT_BANKS = (7, 0)
MASKED = 1e33
PW = 260

PI2_A, PI2_B, PI2_C = 6.28125, 0.0019350051879882812, 3.019916050e-07
ROUND = 12582912.0


def slope(h):
    return 2.0 ** (-8.0 * (h + 1) / SH)


def build(nc, xT, c, positions, position_cols, w_ada, b_ada, norm1_g, norm2_g, w_in, swa_q_norm, swa_k_norm,
          swa_sinks, mla_q_a_norm, mla_kv_a_norm, mla_w_uq, mla_w_ukv, mla_q_norm, mla_k_norm,
          w_out, peer_w_query, sub_keys, u_tiles, v_tiles, outT):
    ctx = ExitStack()
    with ctx:
        def sem(name):
            return ctx.enter_context(nc.semaphore(name))

        BASE = 16512
        END = 229344

        def region(start, entries):
            out, at = [], start
            for name, shape, dt in entries:
                size = 4
                for s in shape[1:]:
                    size *= s
                out.append(nc.alloc_sbuf_tensor_at(name, shape, dt, offset=at))
                at += (size + 31) // 32 * 32
            assert at <= END, (name, at - END)
            return out, at

        (res, ident, ones, iota, cT, b_cols, ada, g1, g2, gs, eps), at0 = region(BASE, [
            ("res", [P, KD, T], F32),
            ("ident", [P, P], F32), ("ones", [P, P], F32), ("iota", [P, P], F32),
            ("cT", [P, KD], F32), ("b_cols", [P, 6 * KD], F32), ("ada", [P, 6 * KD], F32),
            ("g1", [P, KD], F32), ("g2", [P, KD], F32), ("gs", [P, KD], F32), ("eps", [P, 1], F32)])
        ring, at1 = region(at0, [(f"ring{i}", [P, KD, CH], F32) for i in range(3)])
        (hT,), at2 = region(at1, [("hT", [P, KD, T], F32)])
        (oT,), _ = region(at1, [("oT", [P, KD, T], F32)])
        (m_late,), _ = region(at0, [("m_late", [P, 2, 2 * MH, QK], F32)])
        (wlo0, whi0, wlo2), _ = region(at0, [("wlo0", [P, KD, CH], F32R), ("whi0", [P, KD, CH], F32R), ("wlo2", [P, KD, CH], F32R)])
        (oTlo,), _ = region(at1, [("oTlo", [P, KD, T], F32R)])
        (z, qkc, wuq, wukv, kvm, m2, distm, pb, qkT, g_swa, g_cq, g_ckv, g_mla, trig, posq,
         posqf, ss, rz, mss, mrz, nm, sm, rsm, sinks, freq), _ = region(at2, [
            ("z", [P, TT, IN_COLS], F32), ("qkc", [P, 2, 4, T], F32),
            ("wuq", [P, 2, MH * QK], F32), ("wukv", [P, MH * (NOPE + VD)], F32),
            ("kvm", [P, TT, MH * (NOPE + VD)], F32), ("m2", [P, 2, 2 * MH, QK], F32),
            ("distm", [P, TT, 256], F32), ("pb", [P, 4, 2, PW], F32), ("qkT", [P, 2 * MH, T], F32),
            ("g_swa", [P, SH + SKV, SD], F32), ("g_cq", [P, QRANK], F32), ("g_ckv", [P, KVRANK], F32),
            ("g_mla", [P, 2, QK], F32), ("trig", [P, TT, 2, ROPE // 2], F32), ("posq", [P, TT], I32),
            ("posqf", [P, TT], F32), ("ss", [P, TT, 12], F32), ("rz", [P, TT, 12], F32),
            ("mss", [P, 2 * MH], F32), ("mrz", [P, 2 * MH], F32), ("nm", [P, 4, 2], F32),
            ("sm", [P, 4, 2], F32), ("rsm", [P, 4, 2], F32), ("sinks", [P, SH], F32),
            ("freq", [P, ROPE // 2], F32)])

        def heads(tt):
            return m2[:, tt, :, :] if tt < 2 else m_late[:, tt - 2, :, :]

        qTs, kcT = qkc[:, 0, :, :], qkc[:, 1, :, :]
        pt = m2[:].rearrange("p a h d -> p (a h d)")[:, 0:1024].rearrange("p (a s q) -> p a s q", a=2, q=P)
        accs = m2[:].rearrange("p a h d -> p (a h d)")[:, 1024:2048].rearrange("p (a c) -> p a c", a=2)
        zsq_k = qkT[:].rearrange("p a t -> p (a t)")[:, 0:TT * P].rearrange("p (t c) -> p t c", t=TT)
        zsq_q = pb[:].rearrange("p a j k -> p (a j k)")[:, 1536:2048]
        zsq_cq = qkT[:].rearrange("p a t -> p (a t)")[:, TT * 640:TT * 640 + 384]
        msq = pb[:].rearrange("p a j k -> p (a j k)")[:, 0:2 * MH * QK].rearrange("p (h d) -> p h d", h=2 * MH)
        kvm_flat = kvm[:].rearrange("p t c -> p (t c)")
        posk_i = kvm_flat[:, 0:T].bitcast(I32)
        posk = kvm_flat[:, T:2 * T]
        ang = kvm_flat[:, 1024:1024 + TT * 32].rearrange("p (t s f) -> p t s f", t=TT, s=2)
        turns = kvm_flat[:, 1280:1280 + TT * 32].rearrange("p (t s f) -> p t s f", t=TT, s=2)
        ropet = [pb[:].rearrange("p a j k -> p (a j k)")[:, 256 * n:256 * n + 256].rearrange("p (h d) -> p h d", h=16) for n in range(4)]
        spare = [qkT[:].rearrange("p a t -> p (a t)")[:, 4096:8192].rearrange("p (k n) -> p k n", k=KD),
                 qkc[:].rearrange("p a g t -> p (a g t)").rearrange("p (k n) -> p k n", k=KD)]
        rstd1 = pb[:].rearrange("p a j k -> p (a j k)")[:, 0:T]
        (stage,), at_c = region(at0, [("stage", [P, NT, P], F32)])
        assert at_c == at2
        (qpT,), _ = region(at1, [("qpT", [P, PH, T], F32)])
        (h2hi, h2lo), at3 = region(at2, [("h2hi", [P, KD, T], F32R), ("h2lo", [P, KD, T], F32R)])
        (h2T,), at_h = region(at3, [("h2T", [P, KD, T], F32)])
        (skT, rstd2), at_h = region(at_h, [("skT", [P, PH, NK], F32), ("rstd2", [P, T], F32)])
        (whi1,), _ = region(at_h, [("whi1", [P, KD, CH], F32R)])
        (oThi,), _ = region(at2, [("oThi", [P, KD, T], F32R)])
        (sout0, sout1), at_h = region(at_h, [("sout0", [P, 2 * PH, NK], F32), ("sout1", [P, 2 * PH, NK], F32)])
        sout = (sout0, sout1)
        (accs_late,), at_a = region(at_h, [("accs_late", [P, 2, CH], F32)])
        (s, sv, six, sixf, cand, best, bi, bia, abf, IJW, slots, eW, eS, eR, eqI), at_t = region(at3, [
            ("s", [P, 2 * PH, NK], F32), ("sv", [P, PH, 2, KTOP], F32), ("six", [P, PH, 2, KTOP], U32),
            ("sixf", [P, PH, 2, KTOP], F32), ("cand", [P, PH, KTOP, KTOP], F32),
            ("best", [P, PH, KTOP], F32), ("bi", [P, PH, KTOP], U32), ("bia", [P, 2, PH, KTOP], U32),
            ("abf", [P, 2, PH, KTOP], F32), ("IJW", [P, 3, PH, KTOP], F32), ("slots", [P, 5, P], F32),
            ("eW", [P, PH, KTOP], F32), ("eS", [P, PH], F32), ("eR", [P, PH], F32), ("eqI", [P, 2, HB, P], F32)])
        eq = s[:].rearrange("p a (b c) -> p (a b c)", c=16).rearrange("p (h k m) -> p h k m", h=PH, k=KTOP)
        ohJ, at_t = region(at_t, [(f"ohJ{b}", [P, HB, P], F32R) for b in range(2)])
        gpart, at_t = region(at_t, [(f"gpart{b}", [P, HB, 2, P], F32) for b in range(2)])
        ohW, at_t = region(at_t, [(f"ohW{b}", [P, HB, 2, P], F32R) for b in range(2)])
        at4 = max(at_t, at_h)
        assert at_a <= at4
        uraw, at4 = region(at4, [(f"uraw{b}", [P, D], F32) for b in range(2)])
        at_u = at4
        uhi, at4 = region(at4, [(f"uhi{b}", [P, D], F32R) for b in range(2)])
        ulo, at4 = region(at4, [(f"ulo{b}", [P, D], F32R) for b in range(2)])
        act_out, at4 = region(at4, [(f"act_out{b}", [P, T], F32) for b in range(2)])
        (late,), _ = region(at_u, [("late", [P, KD, CH], F32)])
        spare.append(late[:])
        vraw, at_v = region(at0, [(f"vraw{b}", [P, D], F32) for b in range(4)])
        vhi, at_v = region(at_v, [(f"vhi{b}", [P, D], F32R) for b in range(4)])
        vlo, at_v = region(at_v, [(f"vlo{b}", [P, D], F32R) for b in range(4)])
        assert at_v <= at2
        gate, at5 = region(at3, [(f"gate{b}", [P, T], F32) for b in range(4)])
        act_in, at5 = region(at5, [(f"act_in{b}", [P, T], F32) for b in range(4)])
        cf, at5 = region(at5, [(f"cf{b}", [P, T], F32) for b in range(2)])
        chi, at5 = region(at5, [(f"chi{b}", [P, T], F32R) for b in range(4)])
        clo, at5 = region(at5, [(f"clo{b}", [P, T], F32R) for b in range(4)])
        assert at5 <= at_t

        ps = ctx.enter_context(nc.psum_tensor("ps", [P, 8, 512], F32))
        ada_ps = ps[:, 7, 0:6 * KD]
        gates = nc.dram_tensor("gates", (NT, P, T), F32).ap()
        gelus = nc.dram_tensor("gelus", (NT, P, T), F32).ap()
        keys = nc.dram_tensor("keys", (TT, P, 2 * PH * NK), F32).ap()

        x_in = sem("x_in")
        c_in = sem("c_in")
        small_in = sem("small_in")
        up_in = sem("up_in")
        chunk_in = [sem(f"chunk_in{i}") for i in range(6)]
        chunk_used = [sem(f"chunk_used{i}") for i in range(6)]
        acc_done = sem("acc_done")
        const = sem("const")
        sq1 = sem("sq1")
        sq1_sum = sem("sq1_sum")
        ms1 = sem("ms1")
        sd1 = sem("sd1")
        ada_done = sem("ada_done")
        ada_read = sem("ada_read")
        h_scaled = sem("h_scaled")
        h_ready = sem("h_ready")
        z_ps = sem("z_ps")
        z_sb = sem("z_sb")
        z_stat = sem("z_stat")
        z_var = sem("z_var")
        z_sd = sem("z_sd")
        zn_ready = sem("zn_ready")
        zq_stat = sem("zq_stat")
        zq_summed = sem("zq_summed")
        zqn_ready = sem("zqn_ready")
        zq_ps = sem("zq_ps")
        zq_sb = sem("zq_sb")
        zt_ps = sem("zt_ps")
        zt_sb = sem("zt_sb")
        up_ps = sem("up_ps")
        up_sb = sem("up_sb")
        m_built = sem("m_built")
        m_roped = sem("m_roped")
        m_sq = sem("m_sq")
        m_var = sem("m_var")
        m_sd = sem("m_sd")
        m_ready = sem("m_ready")
        mt_ps = sem("mt_ps")
        mt_sb = sem("mt_sb")
        ang_ready = sem("ang_ready")
        trig_ready = sem("trig_ready")
        s_done = sem("s_done")
        biased = sem("biased")
        exp_done = sem("exp_done")
        p_ready = sem("p_ready")
        pt_ps = sem("pt_ps")
        pt_sb = sem("pt_sb")
        o_ps = sem("o_ps")
        o_sb = sem("o_sb")
        o_hi = sem("o_hi")
        o_split = sem("o_split")
        out0_hi = sem("out0_hi")
        out0_split = sem("out0_split")
        w_hi = sem("w_hi")
        w_split = sem("w_split")
        mix_ps = sem("mix_ps")
        x1_ready = sem("x1_ready")
        sq2 = sem("sq2")
        sq2_sum = sem("sq2_sum")
        ms2 = sem("ms2")
        sd2 = sem("sd2")
        h2_scaled = sem("h2_scaled")
        h2_hi = sem("h2_hi")
        h2_split = sem("h2_split")
        sk_in = sem("sk_in")
        qp_ps = sem("qp_ps")
        qp_sb = sem("qp_sb")
        key_ps = sem("key_ps")
        best_ready = sem("best_ready")
        best_exp = sem("best_exp")
        ijw_ready = sem("ijw_ready")
        ijw_ps = sem("ijw_ps")
        oh_ready = sem("oh_ready")
        oh_used = sem("oh_used")
        g_parts = sem("g_parts")
        g_sb = sem("g_sb")
        g_out = sem("g_out")
        s_copied = sem("s_copied")
        s_out = [sem(f"s_out{b}") for b in range(2)]
        s_in = sem("s_in")
        s_free = sem("s_free")
        eq_ready = sem("eq_ready")
        c_space = sem("c_space")
        u_in = [sem(f"u_in{b}") for b in range(2)]
        v_in = [sem(f"v_in{b}") for b in range(4)]
        gate_in = [sem(f"gate_in{b}") for b in range(4)]
        act_back = [sem(f"act_back{b}") for b in range(4)]
        u_hi = sem("u_hi")
        u_lo = sem("u_lo")
        a_ps = sem("a_ps")
        gelu_done = sem("gelu_done")
        a_out = [sem(f"a_out{b}") for b in range(2)]
        v_hi = sem("v_hi")
        v_lo = sem("v_lo")
        c_mul = sem("c_mul")
        c_hi = sem("c_hi")
        c_lo = sem("c_lo")
        y_ps = sem("y_ps")
        y_sb = sem("y_sb")
        out_done = sem("out_done")
        dve_step = sem("dve_step")
        act_step = sem("act_step")
        pool_step = sem("pool_step")

        weights_of = {"ada": w_ada, "in": w_in, "out": w_out, "query": peer_w_query}
        chunks, slot, place, uses = [], [], {}, [0] * 6
        for kind, j, at in (("ada", 2, 0), ("ada", 3, 1), ("ada", 0, 3), ("ada", 1, 4), ("in", 1, 2), ("in", 2, 0), ("in", 0, 1),
                            ("ada", 4, 3), ("ada", 5, 4), ("ada", 8, 3), ("ada", 9, 4), ("out", 0, 2), ("out", 1, 0),
                            ("ada", 6, 5), ("ada", 7, 5), ("query", 0, 2), ("query", 1, 0), ("ada", 10, 5), ("ada", 11, 5)):
            place[kind, j] = len(chunks)
            chunks.append((kind, weights_of[kind], j, min(CH, weights_of[kind].shape[1] - j * CH)))
            slot.append((at, uses[at]))
            uses[at] += 1
        ada_order = [j for kind, _, j, _ in chunks if kind == "ada"]

        direct = [ada_order[1]]
        prepared = [j for j in ada_order if j not in direct]

        def acc(j):
            return (accs_late if j in (6, 7, 10, 11) else accs)[:, prepared.index(j) % 2, :]

        def chunk(n):
            at = slot[n][0]
            return ring[at][:] if at < 3 else spare[at - 3]

        NSMALL = 12
        units = [("s", b, kv, j) for b in range(TT) for kv in range(SKV) for j in (0, 2)] + \
                [("m", b, h, 0) for b in range(TT) for h in range(MH)]
        NU = len(units)

        def heads_of(kind):
            return 2 if kind == "s" else 1

        def key_tiles(kind, b):
            if kind == "s":
                return [b] if b == 0 else [b - 1, b]
            return list(range(b + 1))

        def p_view(u, kind):
            if kind == "s":
                return pb[:, u % 4, :, :]
            return pb[:, u % 4, :, :].rearrange("p j k -> p (j k)")[:, 0:512].unsqueeze(1)

        def pt_slots(kind, b):
            if kind == "s":
                return [(2 * j + kb - (b - 1), j, (kb - (b - 1)) * P, kb) for j in range(2) for kb in key_tiles(kind, b)]
            return [(kb, 0, kb * P, kb) for kb in key_tiles(kind, b)]

        parts = {("out", 0): (whi0, wlo2), ("out", 1): (whi1, wlo0), ("query", 0): (whi0, wlo2), ("query", 1): (whi1, wlo0)}

        z_order = (1, 2, 0)

        def z_bank(q):
            return q % 6 if q < 2 * TT else 6

        block = ctx.enter_context(nc.Block())

        @block.sync
        def _(sp):
            def load_chunk(n):
                at, before = slot[n]
                if before:
                    sp.wait_ge(chunk_used[at], before)
                _, w, j, cols = chunks[n]
                sp.dma_start(chunk(n)[:, :, 0:cols],
                             w[:, j * CH:j * CH + cols].rearrange("(k p) n -> p k n", p=P)).then_inc(chunk_in[at], 16)

            sp.dma_start(cT[:], c).then_inc(c_in, 16)
            load_chunk(0)
            load_chunk(1)
            sp.dma_start(res[:], xT).then_inc(x_in, 16)
            for n in range(2, place["out", 1]):
                load_chunk(n)
            sp.wait_ge(mt_ps, 4 * TT)
            load_chunk(place["out", 1])
            sp.wait_ge(o_sb, NU)
            for n in range(place["ada", 6], place["ada", 10]):
                load_chunk(n)
            sp.wait_ge(mix_ps, KD)
            sp.dma_start(skT[:], sub_keys).then_inc(sk_in, 16)

            def load_u(n, r):
                sp.wait_ge(u_lo, n + 1)
                sp.dma_start(uraw[r % 2][:], u_tiles[bass.ds(n, 1), :, :].rearrange("a p c -> p (a c)")).then_inc(u_in[r % 2], 16)

            load_chunk(place["ada", 10])
            for n in range(2):
                load_u(n, n)
            load_chunk(place["ada", 11])
            for n in range(2, 4):
                load_u(n, n)
            for tt in range(TT):
                sp.wait_ge(s_copied, tt + 1)
                sp.dma_start(keys[tt], sout[tt % 2][:].rearrange("p a n -> p (a n)")).then_inc(s_out[tt % 2], 16)
            for b in range(2):
                sp.wait_ge(s_out[b], 16 * TT // 2)
            sp.wait_ge(h2_split, KD)
            sp.dma_start(s[:].rearrange("p a n -> p (a n)"), keys[0]).then_inc(s_in, 16)

            def load_us(first, steps):
                with sp.Fori(0, steps // 4) as i:
                    for r in range(4):
                        load_u(first + i * 4 + (r + 2), r)

            for n in range(4, SOLO + 2):
                load_u(n, n)
            with sp.Fori(0, TT - 1) as tt:
                sp.wait_ge(s_free, tt + 1)
                sp.dma_start(s[:].rearrange("p a n -> p (a n)"),
                             keys[bass.ds(tt + 1, 1), :, :].rearrange("a p c -> p (a c)")).then_inc(s_in, 16)
                load_us(tt * SEG + SOLO, SEG)
            load_us((TT - 1) * SEG + SOLO, SEG)
            for n in range(TT * SEG + SOLO + 2, NT):
                load_u(n, n)

            sp.wait_ge(g_out, 16 * GP * (TT + 1))
            sp.wait_ge(c_space, TT)

            def load_v(n, r, first):
                if not first:
                    sp.wait_ge(v_lo, n - 3)
                sp.dma_start(vraw[r][:], v_tiles[bass.ds(n, 1), :, :].rearrange("a p c -> p (a c)")).then_inc(v_in[r], 16)
                if not first:
                    sp.wait_ge(c_mul, n - 3)
                sp.dma_start(gate[r][:], gates[bass.ds(n, 1), :, :].rearrange("a p c -> p (a c)")).then_inc(gate_in[r], 16)
                sp.dma_start(act_in[r][:], gelus[bass.ds(n, 1), :, :].rearrange("a p c -> p (a c)")).then_inc(act_back[r], 16)

            for b in range(2):
                sp.wait_ge(a_out[b], 16 * 3)
            for r in range(4):
                load_v(r, r, True)
            for b in range(2):
                sp.wait_ge(a_out[b], 16 * (NT // 2 + 1))
            with sp.Fori(1, NT // 4) as i:
                for r in range(4):
                    load_v(i * 4 + r, r, False)
            for d in range(KD):
                sp.wait_ge(y_sb, d + 1)
                sp.dma_start(outT[d], res[:, d, :]).then_inc(out_done, 16)
            sp.wait_ge(out_done, 16 * KD)
        @block.gpsimd
        def _(pool):
            nc.gpsimd.memset(eps[:], EPS)
            nc.gpsimd.memset(ones[:], 1.0).then_inc(const, 1)
            nc.gpsimd.iota(iota[:], pattern=[[1, P]], base=0, channel_multiplier=0,
                           allow_small_or_imprecise_dtypes=True).then_inc(const, 1)
            nc.gpsimd.memset(ident[:], 0.0).then_inc(pool_step, 1)
            pool.wait_ge(pool_step, 1)
            nc.gpsimd.affine_select(out=ident[:], in_=ident[:], compare_op=ALU.not_equal, fill=1.0, base=0,
                                    pattern=[[-1, P]], channel_multiplier=1).then_inc(const, 1)
            def sum_squares(out, squares, ready, done):
                for k in range(1, KD):
                    pool.wait_ge(ready, k + 1)
                    if k > 1:
                        pool.wait_ge(done, k - 1)
                    nc.gpsimd.tensor_tensor(out, squares[:, 0, :] if k == 1 else out, squares[:, k, :], ALU.add).then_inc(done, 1)

            sum_squares(rstd1, hT, sq1, sq1_sum)
            for tt in range(TT):
                pool.wait_ge(up_sb, 2 * tt + 2)
                mk = heads(tt)[:, MH:2 * MH, :]
                nc.gpsimd.tensor_copy(mk[:, :, 0:NOPE],
                                      kvm[:, tt, :].rearrange("p (h c) -> p h c", h=MH)[:, :, 0:NOPE])
                nc.gpsimd.tensor_copy(mk[:, :, NOPE:QK],
                                      z[:, tt, Z_KR:Z_KR + ROPE].unsqueeze(1).to_broadcast([P, MH, ROPE])).then_inc(m_built, 1)
            n = place["out", 0]
            whi, wlo = parts["out", 0]
            pool.wait_ge(chunk_in[slot[n][0]], 16 * (slot[n][1] + 1))
            pool.wait_ge(chunk_used[1], uses[1])
            nc.gpsimd.tensor_copy(whi[:], chunk(n)).then_inc(out0_hi, 1)
            pool.wait_ge(out0_hi, 1)
            nc.gpsimd.tensor_tensor(wlo[:], chunk(n), whi[:].bitcast(F32), ALU.subtract).then_inc(out0_split, 1)
            sum_squares(rstd2[:], h2T, sq2, sq2_sum)
            pool.sem_inc(u_lo, 2)
            pool.sem_inc(g_sb, 2)

            def split_u(n, r):
                pool.wait_ge(u_hi, n + 1)
                nc.gpsimd.tensor_tensor(ulo[r % 2][:], uraw[r % 2][:], uhi[r % 2][:].bitcast(F32), ALU.subtract).then_inc(u_lo, 1)

            def sum_gates(q, col, half):
                pool.wait_ge(g_parts, q + 3)
                nc.gpsimd.tensor_tensor(stage[:].rearrange("p i t -> p t i")[:, bass.ds(col, HB), :],
                                        gpart[half][:, :, 0, :], gpart[half][:, :, 1, :], ALU.add).then_inc(g_sb, 1)

            def split_us(first, steps):
                with pool.Fori(0, steps // 4) as i:
                    for r in range(4):
                        split_u(i * 4 + (first + r), r)

            for n in range(2):
                split_u(n, n)
            split_us(2, SOLO)
            with pool.Fori(0, TT) as tt:
                with pool.Fori(0, BOTH // 4) as i:
                    for r in range(4):
                        split_u(i * 4 + (tt * SEG + (SOLO + 2 + r)), r)
                        if r == 0:
                            pool.wait_ge(g_out, tt * (16 * GP) + 16 * GP)
                        for half in range(2):
                            sum_gates(i * 8 + (tt * (2 * BOTH) + (2 * r + half)), i * (8 * HB) + HB * (2 * r + half), half)
                split_us(tt * SEG + (SOLO + BOTH + 2), SOLO)
            for n in range(TT * SEG + SOLO + 2, NT):
                split_u(n, n)

        @block.scalar
        def _(act):
            steps = [0]

            def settled(ins):
                steps[0] += 1
                ins.then_inc(act_step, 1)
                act.wait_ge(act_step, steps[0])

            act.sem_inc(gelu_done, 1)
            act.sem_inc(g_parts, 2)
            act.sem_inc(g_out, 16 * GP)
            for b in range(2):
                act.sem_inc(a_out[b], 16)
            act.dma_start(b_cols[:], b_ada).then_inc(small_in, 16)
            act.dma_start(g1[:], norm1_g).then_inc(small_in, 16)
            act.dma_start(g2[:], norm2_g).then_inc(small_in, 16)
            act.dma_start(posq[:], position_cols).then_inc(small_in, 16)
            act.dma_start(g_swa[:, 0, :], swa_q_norm.partition_broadcast(P)).then_inc(small_in, 16)
            act.dma_start(g_swa[:, SH, :], swa_k_norm.partition_broadcast(P)).then_inc(small_in, 16)
            act.dma_start(g_cq[:], mla_q_a_norm.partition_broadcast(P)).then_inc(small_in, 16)
            act.dma_start(g_ckv[:], mla_kv_a_norm.partition_broadcast(P)).then_inc(small_in, 16)
            act.dma_start(g_mla[:, 0, :], mla_q_norm.partition_broadcast(P)).then_inc(small_in, 16)
            act.dma_start(g_mla[:, 1, :], mla_k_norm.partition_broadcast(P)).then_inc(small_in, 16)
            act.dma_start(sinks[:], swa_sinks.partition_broadcast(P)).then_inc(small_in, 16)
            act.dma_start(posk_i, positions.partition_broadcast(P)).then_inc(small_in, 16)
            act.wait_ge(x_in, 16)
            for k in range(KD):
                nc.scalar.activation(hT[:, k, :], res[:, k, :], ACT.Square).then_inc(sq1, 1)
            act.wait_ge(const, 1)
            act.wait_ge(ms1, 1)
            nc.scalar.activation(rstd1, ps[:, 6, :], ACT.Sqrt, bias=eps[:], scale=1.0 / D).then_inc(sd1, 1)
            for k in range(KD):
                act.wait_ge(h_scaled, k + 1)
                nc.scalar.activation(hT[:, k, :], hT[:, k, :], ACT.Identity, bias=ada[:, k:k + 1]).then_inc(h_ready, 1)
            act.dma_start(wuq[:], mla_w_uq.rearrange("(k p) n -> p k n", p=P)).then_inc(up_in, 16)
            act.dma_start(wukv[:], mla_w_ukv).then_inc(up_in, 16)
            def copy_z(n, tt):
                q = z_order.index(n) * TT + tt
                cols = chunks[place["in", n]][3]
                act.wait_ge(z_ps, q + 1)
                dst, src = z[:, tt, n * CH:n * CH + cols], ps[:, z_bank(q), 0:cols]
                if n == 0:
                    dst = dst.rearrange("p (g v d) -> p v g d", v=SKV, g=SG)
                    src = src.rearrange("p (v g d) -> p v g d", v=SKV, g=SG)
                nc.scalar.activation(dst, src, ACT.Copy).then_inc(z_sb, 1)
                act.wait_ge(z_sb, q + 1)

            def square_queries(tt):
                if tt:
                    act.wait_ge(zq_summed, tt)
                nc.scalar.activation(zsq_q, z[:, tt, 0:Z_K], ACT.Square).then_inc(zq_stat, 1)

            for tt in range(TT):
                copy_z(1, tt)
                settled(nc.scalar.activation(zsq_cq[:, 0:QRANK], z[:, tt, Z_CQ:Z_CKV], ACT.Square,
                                             accum_out=ss[:, tt, 10:11]))
                nc.scalar.activation(zsq_k[:, tt, :], z[:, tt, Z_K:Z_V], ACT.Square).then_inc(z_stat, 1)
            act.wait_ge(ang_ready, 1)
            nc.scalar.activation(trig[:].rearrange("p t s f -> p (t s f)"), kvm_flat[:, 1024:1024 + TT * 32],
                                 ACT.Sin).then_inc(trig_ready, 1)
            for tt in range(TT):
                copy_z(2, tt)
                nc.scalar.activation(zsq_cq[:, QRANK:QRANK + KVRANK], z[:, tt, Z_CKV:Z_KR], ACT.Square,
                                     accum_out=ss[:, tt, 11:12]).then_inc(z_stat, 1)
            act.wait_ge(z_var, 1)
            nc.scalar.activation(rz[:, :, SH:12], rz[:, :, SH:12], ACT.Sqrt).then_inc(z_sd, 1)
            copy_z(0, 0)
            square_queries(0)
            for tt in range(TT):
                act.wait_ge(zt_ps, tt + 1)
                nc.scalar.activation(kcT[:, :, tt * P:(tt + 1) * P], ps[:, tt, :].rearrange("p (g t) -> p g t", g=4),
                                     ACT.Copy).then_inc(zt_sb, 1)
            def copy_projections(tt):
                act.wait_ge(up_ps, 2 * tt + 1)
                mq = heads(tt).rearrange("p h d -> p (h d)")
                nc.scalar.activation(mq[:, 0:512], ps[:, 0, :], ACT.Copy)
                nc.scalar.activation(mq[:, 512:768], ps[:, 1, 0:256], ACT.Copy).then_inc(up_sb, 1)
                act.wait_ge(up_ps, 2 * tt + 2)
                nc.scalar.activation(kvm[:, tt, :], ps[:, 2:4, :].rearrange("p a b -> p (a b)"), ACT.Copy).then_inc(up_sb, 1)

            def square_heads(tt):
                act.wait_ge(m_roped, tt + 1)
                nc.scalar.activation(msq, heads(tt), ACT.Square).then_inc(m_sq, 1)

            def root_heads(tt):
                act.wait_ge(m_var, tt + 1)
                nc.scalar.activation(mrz[:], mrz[:], ACT.Sqrt).then_inc(m_sd, 1)

            def copy_heads(tt):
                for f in range(4):
                    act.wait_ge(mt_ps, 4 * tt + f + 1)
                    nc.scalar.activation(qkT[0:QK, 4 * f:4 * f + 4, tt * P:(tt + 1) * P],
                                         ps[0:QK, 4 + f % 2, :].rearrange("p (h t) -> p h t", h=4), ACT.Copy).then_inc(mt_sb, 1)

            def copy_queries(tt):
                act.wait_ge(zq_ps, tt + 1)
                nc.scalar.activation(qTs[:, :, tt * P:(tt + 1) * P], ps[:, tt, :].rearrange("p (g t) -> p g t", g=SG),
                                     ACT.Copy).then_inc(zq_sb, 1)

            copy_projections(0)
            copy_z(0, 1)
            square_heads(0)
            root_heads(0)
            square_queries(1)
            copy_projections(1)
            copy_z(0, 2)
            square_heads(1)
            copy_heads(0)
            root_heads(1)
            square_queries(2)
            act.wait_ge(chunk_used[0], 2)
            copy_projections(2)
            square_heads(2)
            root_heads(2)
            copy_z(0, 3)
            square_queries(3)
            act.wait_ge(z_var, 2)
            nc.scalar.activation(rz[:, :, 0:SH], rz[:, :, 0:SH], ACT.Sqrt).then_inc(z_sd, 1)
            copy_projections(3)
            copy_heads(1)
            copy_heads(2)
            for tt in range(2):
                copy_queries(tt)
            square_heads(3)
            for tt in range(2, TT):
                copy_queries(tt)
            root_heads(3)
            copy_heads(3)

            def exponentials(u):
                kind, b, _, _ = units[u]
                act.wait_ge(biased, u + 1)
                nk = len(key_tiles(kind, b)) * P
                for j in range(heads_of(kind)):
                    if kind == "s":
                        src = pb[:, u % 4, j, 256 - nk:257]
                        dst = src
                    else:
                        src = ps[:, u % 3, 0:nk]
                        dst = p_view(u, kind)[:, 0, 0:nk]
                    last = nc.scalar.activation(dst, src, ACT.Exp, bias=nm[:, u % 4, j:j + 1], scale=1.0,
                                                accum_out=sm[:, u % 4, j:j + 1])
                last.then_inc(exp_done, 1)

            def copy_pt(u):
                kind, b, _, _ = units[u]
                act.wait_ge(pt_ps, u + 1)
                if u >= 2:
                    act.wait_ge(o_ps, u - 1)
                slots_ = slice(0, 4) if kind == "s" and b > 0 else slice(1, 4, 2) if kind == "s" else slice(0, b + 1)
                nc.scalar.activation(pt[:, u % 2, slots_, :], ps[:, 4 + u % 2, :].rearrange("p (s q) -> p s q", q=P)[:, slots_, :],
                                     ACT.Copy).then_inc(pt_sb, 1)

            exponentials(0)
            for u in range(NU):
                if u + 1 < NU:
                    exponentials(u + 1)
                copy_pt(u)
            def high_w(key):
                n = place[key]
                act.wait_ge(chunk_in[slot[n][0]], 16 * (slot[n][1] + 1))
                nc.scalar.activation(parts[key][0][:], chunk(n), ACT.Copy).then_inc(w_hi, 1)

            act.wait_ge(o_sb, NU)
            for k in range(KD):
                nc.scalar.activation(oThi[:, k, :], oT[:, k, :], ACT.Copy).then_inc(o_hi, 1)
            high_w(("out", 1))
            for k in range(KD):
                act.wait_ge(x1_ready, k + 1)
                nc.scalar.activation(h2T[:, k, :], res[:, k, :], ACT.Square).then_inc(sq2, 1)
                if k == 5:
                    high_w(("query", 0))
            act.wait_ge(ms2, 1)
            nc.scalar.activation(rstd2[:], ps[:, 5, :], ACT.Sqrt, bias=eps[:], scale=1.0 / D).then_inc(sd2, 1)
            for k in range(KD):
                act.wait_ge(h2_scaled, k + 1)
                nc.scalar.activation(h2hi[:, k, :], h2T[:, k, :], ACT.Identity, bias=ada[:, 3 * KD + k:3 * KD + k + 1])\
                    .then_inc(h2_hi, 1)
            high_w(("query", 1))
            for h in range(PH):
                act.wait_ge(qp_ps, h + 1)
                nc.scalar.activation(qpT[:, h, :], ps[:, h % 4, :], ACT.Copy).then_inc(qp_sb, 1)

            def high_u(n, r, count):
                act.wait_ge(u_in[r % 2], count)
                act.wait_ge(a_ps, n + 1)
                nc.scalar.activation(uhi[r % 2][:], uraw[r % 2][:], ACT.Copy).then_inc(u_hi, 1)

            act.wait_ge(chunk_used[5], uses[5])
            for n in range(2):
                high_u(n, n, 16)
            for tt in range(TT):
                act.wait_ge(key_ps, tt + 1)
                if tt >= 2:
                    act.wait_ge(s_out[tt % 2], 16)
                for f in range(4):
                    last = nc.scalar.activation(sout[tt % 2][:, 4 * f:4 * f + 4, :],
                                                ps[:, 4 * (1 - tt % 2) + f, :].rearrange("p (a n) -> p a n", n=NK), ACT.Copy)
                last.then_inc(s_copied, 1)
            act.wait_ge(s_copied, TT)
            act.sem_inc(gelu_done, 1)

            def gelu(n, r, count):
                act.wait_ge(a_ps, n + 3)
                act.wait_ge(a_out[r % 2], count)
                nc.scalar.activation(act_out[r % 2][:], ps[:, DOT_BANKS[r % 2], :], ACT.Gelu).then_inc(gelu_done, 1)
                act.wait_ge(gelu_done, n + 3)
                act.dma_start(gelus[bass.ds(n, 1), :, :].rearrange("a p c -> p (a c)"), act_out[r % 2][:]).then_inc(a_out[r % 2], 16)

            def copy_parts(q, half):
                act.wait_ge(oh_used, q + 3)
                act.wait_ge(g_sb, q + 1)
                nc.scalar.activation(gpart[half][:], ps[:, 2 + 2 * half:4 + 2 * half, :], ACT.Copy).then_inc(g_parts, 1)

            def alone(first, pair, steps, send):
                with act.Fori(0, steps // 4) as i:
                    for r in range(4):
                        pairs = i * 2 + (pair + r // 2)
                        high_u(i * 4 + (first + r + 2), r, pairs * 16 + 32)
                        gelu(i * 4 + (first + r), r, pairs * 16 + 16)
                        if send is not None:
                            rows = bass.ds(i * (4 * P // GP) + r * (P // GP), P // GP)
                            act.dma_start(gates[rows, :, bass.ds(send * P, P)].rearrange("i j t -> j i t"),
                                          stage[:, rows, :]).then_inc(g_out, 16)

            def weights():
                nc.scalar.activation(eW[:], eW[:], ACT.Exp).then_inc(best_exp, 1)

            def segment(tt):
                first_half = tt * (SEG // 2) + SOLO // 2
                with act.Fori(0, BOTH // 4) as i:
                    for r in range(4):
                        n, pairs = i * 4 + (tt * SEG + (SOLO + r)), i * 2 + (first_half + r // 2)
                        high_u(n + 2, r, pairs * 16 + 32)
                        gelu(n, r, pairs * 16 + 16)
                        for half in range(2):
                            copy_parts(i * 8 + (tt * (2 * BOTH) + (2 * r + half)), half)
                act.wait_ge(g_sb, tt * (2 * BOTH) + (2 * BOTH + 2))

            alone(0, 0, GP, None)
            act.wait_ge(best_ready, 1)
            weights()
            alone(GP, GP // 2, SOLO - GP, None)
            with act.Fori(0, TT - 1) as tt:
                segment(tt)
                first, pair = tt * SEG + (SOLO + BOTH), tt * (SEG // 2) + (SOLO + BOTH) // 2
                alone(first, pair, GP, tt)
                act.wait_ge(best_ready, tt + 2)
                weights()
                alone(first + GP, pair + GP // 2, SOLO - GP, None)
            segment(TT - 1)
            alone(TT * SEG, TT * SEG // 2, GP, TT - 1)
            alone(TT * SEG + GP, (TT * SEG + GP) // 2, SOLO - GP, None)
            def high_v(n, r, count, first):
                act.wait_ge(v_in[r], count)
                if not first:
                    act.wait_ge(y_ps, n - 3)
                nc.scalar.activation(vhi[r][:], vraw[r][:], ACT.Copy).then_inc(v_hi, 1)

            for n in range(NT - 4, NT):
                if n + 2 < NT:
                    high_u(n + 2, n, n // 2 * 16 + 32)
                else:
                    high_v(n - (NT - 2), n - (NT - 2), 16, True)
                gelu(n, n, n // 2 * 16 + 16)

            for r in range(2, 4):
                high_v(r, r, 16, True)
            with act.Fori(1, NT // 4) as i:
                for r in range(4):
                    high_v(i * 4 + r, r, i * 16 + 16, False)

        @block.tensor
        def _(pe):
            def arrived(n):
                at, before = slot[n]
                pe.wait_ge(chunk_in[at], 16 * (before + 1))

            def modulation(j):
                order = prepared.index(j)
                pe.wait_ge(acc_done, order + 1)
                for q in range(CH // P):
                    col = j * (CH // P) + q
                    last = nc.tensor.matmul(ada_ps[:, col:col + 1], acc(j)[:, q * P:(q + 1) * P],
                                            ones[:, 0:1], start=True, stop=True)
                last.then_inc(ada_done, 1)

            def modulation_direct(j):
                n = place["ada", j]
                arrived(n)
                for q in range(CH // P):
                    col = j * (CH // P) + q
                    for k in range(KD):
                        last = nc.tensor.matmul(ada_ps[:, col:col + 1], chunk(n)[:, k, q * P:(q + 1) * P], cT[:, k:k + 1],
                                                start=(k == 0), stop=(k == KD - 1))
                last.then_inc(ada_done, 1)
                pe.wait_ge(ada_done, ada_order.index(j) + 1)
                pe.sem_inc(chunk_used[slot[n][0]], 1)

            pe.sem_inc(oh_used, 2)
            pe.sem_inc(a_ps, 2)
            pe.wait_ge(const, 3)
            pe.wait_ge(c_in, 16)
            modulation(ada_order[0])
            modulation_direct(ada_order[1])
            pe.wait_ge(sq1_sum, KD - 1)
            nc.tensor.matmul(ps[:, 6, :], ones[:], rstd1, start=True, stop=True).then_inc(ms1, 1)
            modulation(ada_order[2])
            modulation(ada_order[3])
            def z_tile(n, tt):
                at = place["in", n]
                q = z_order.index(n) * TT + tt
                if tt == 0:
                    arrived(at)
                if q >= 2 * TT:
                    pe.wait_ge(z_sb, max(q, 6))
                elif q >= 6:
                    pe.wait_ge(z_sb, q - 5)
                cols = chunks[at][3]
                for k in range(KD):
                    if q == 0:
                        pe.wait_ge(h_ready, k + 1)
                    last = nc.tensor.matmul(ps[:, z_bank(q), 0:cols], hT[:, k, tt * P:(tt + 1) * P],
                                            chunk(at)[:, k, 0:cols], start=(k == 0), stop=(k == KD - 1))
                last.then_inc(z_ps, 1)
                if q in (2, 3, 6, 8):
                    modulation({2: 4, 3: 5, 6: 8, 8: 9}[q])
                if tt == TT - 1:
                    pe.wait_ge(z_ps, q + 1)
                    pe.sem_inc(chunk_used[slot[at][0]], 1)

            for n in z_order[:2]:
                for tt in range(TT):
                    z_tile(n, tt)
            z_tile(0, 0)
            pe.wait_ge(z_sb, 2 * TT)
            for tt in range(TT):
                pe.wait_ge(zn_ready, tt + 1)
                for f, c0 in enumerate((Z_K, Z_CQ, Z_CQ + P, Z_CKV)):
                    last = nc.tensor.transpose(ps[:, tt, f * P:(f + 1) * P], z[:, tt, c0:c0 + P], ident[:])
                last.then_inc(zt_ps, 1)

            def turn_queries(tt):
                pe.wait_ge(zqn_ready, tt + 1)
                if tt == 0:
                    pe.wait_ge(up_sb, 2 * TT)
                for g in range(SG):
                    last = nc.tensor.transpose(ps[:, tt, g * P:(g + 1) * P], z[:, tt, g * P:(g + 1) * P], ident[:])
                last.then_inc(zq_ps, 1)

            pe.wait_ge(up_in, 32)
            pe.wait_ge(zt_sb, TT)

            def project(tt):
                cols = slice(tt * P, (tt + 1) * P)
                if tt >= 1:
                    pe.wait_ge(up_sb, 2 * tt - 1)
                for bank, c0, n in ((0, 0, 512), (1, 512, 256)):
                    for k in range(2):
                        last = nc.tensor.matmul(ps[:, bank, 0:n], kcT[:, 1 + k, cols], wuq[:, k, c0:c0 + n],
                                                start=(k == 0), stop=(k == 1))
                last.then_inc(up_ps, 1)
                if tt >= 1:
                    pe.wait_ge(up_sb, 2 * tt)
                for bank, c0 in ((2, 0), (3, 512)):
                    last = nc.tensor.matmul(ps[:, bank, :], kcT[:, 3, cols], wukv[:, c0:c0 + 512], start=True, stop=True)
                last.then_inc(up_ps, 1)

            def turn_heads(tt):
                pe.wait_ge(m_ready, tt + 1)
                for f in range(4):
                    if 4 * tt + f >= 2:
                        pe.wait_ge(mt_sb, 4 * tt + f - 1)
                    for h in range(4):
                        last = nc.tensor.transpose(ps[0:QK, 4 + f % 2, h * P:(h + 1) * P], heads(tt)[:, 4 * f + h, :], ident[:])
                    last.then_inc(mt_ps, 1)

            project(0)
            z_tile(0, 1)
            project(1)
            z_tile(0, 2)
            turn_heads(0)
            project(2)
            z_tile(0, 3)
            project(3)
            turn_heads(1)
            turn_heads(2)
            for tt in range(TT):
                turn_queries(tt)
            turn_heads(3)
            pe.wait_ge(mt_sb, 4 * TT)
            pe.wait_ge(zq_sb, TT)

            def scores(u):
                kind, b, sub, j0 = units[u]
                if u >= 3:
                    pe.wait_ge(exp_done, u - 2)
                q = slice(b * P, (b + 1) * P)
                tiles = key_tiles(kind, b)
                keys_ = slice(tiles[0] * P, (b + 1) * P)
                if kind == "s":
                    rows = slice(sub * SD, (sub + 1) * SD)
                    for j in range(2):
                        c0 = j * 256 + (256 - len(tiles) * P)
                        last = nc.tensor.matmul(ps[:, u % 3, c0:c0 + len(tiles) * P], qTs[rows, j0 + j, q], kcT[rows, 0, keys_],
                                                start=True, stop=True)
                else:
                    last = nc.tensor.matmul(ps[:, u % 3, 0:len(tiles) * P], qkT[0:QK, sub, q], qkT[0:QK, MH + sub, keys_],
                                            start=True, stop=True)
                last.then_inc(s_done, 1)

            def transposes(u):
                kind, b, _, _ = units[u]
                pe.wait_ge(p_ready, u + 1)
                if u >= 2:
                    pe.wait_ge(pt_sb, u - 1)
                for slot, j, c0, _ in pt_slots(kind, b):
                    last = nc.tensor.transpose(ps[:, 4 + u % 2, slot * P:(slot + 1) * P],
                                               p_view(u, kind)[:, j, c0:c0 + P], ident[:])
                last.then_inc(pt_ps, 1)

            def values(u):
                kind, b, sub, j0 = units[u]
                pe.wait_ge(pt_sb, u + 1)
                if u >= 2:
                    pe.wait_ge(o_sb, u - 1)
                tiles = key_tiles(kind, b)
                for slot, j, _, kb in pt_slots(kind, b):
                    half = j if kind == "s" else sub % 2
                    if kind == "s":
                        v = z[:, kb, Z_V + sub * SD:Z_V + (sub + 1) * SD]
                    else:
                        v0 = sub * (NOPE + VD) + NOPE
                        v = kvm[:, kb, v0:v0 + VD]
                    last = nc.tensor.matmul(ps[64 * half:64 * half + 64, 3 * (u % 2) + 3, 0:P], v, pt[:, u % 2, slot, :],
                                            start=(kb == tiles[0]), stop=(kb == tiles[-1]))
                last.then_inc(o_ps, 1)

            scores(0)
            scores(1)
            for u in range(NU):
                if u + 2 < NU:
                    scores(u + 2)
                transposes(u)
                if u >= 1:
                    values(u - 1)
            values(NU - 1)
            pe.wait_ge(o_sb, NU)

            def product(out, key, at, hi, lo, ready):
                whi, wlo = parts[key]
                for k in range(KD):
                    if ready is not None:
                        pe.wait_ge(ready, k + 1)
                    nc.tensor.matmul(out, whi[:, k, at:at + P], hi[:, k, :], start=(k == 0), stop=False)
                    nc.tensor.matmul(out, whi[:, k, at:at + P], lo[:, k, :], start=False, stop=False)
                    last = nc.tensor.matmul(out, wlo[:, k, at:at + P], hi[:, k, :], start=False, stop=(k == KD - 1))
                return last

            for m in range(KD):
                n = place["out", m // 4]
                if m == 0:
                    pe.wait_ge(out0_split, 1)
                if m == 4:
                    pe.wait_ge(w_split, 1)
                if m >= 4:
                    pe.wait_ge(x1_ready, m - 3)
                product(ps[:, m % 4, :], ("out", m // 4), (m % 4) * P, oThi, oTlo, o_split if m == 0 else None).then_inc(mix_ps, 1)
                if m in (4, 7):
                    modulation({4: 6, 7: 7}[m])
                if m % 4 == 3:
                    pe.wait_ge(mix_ps, m + 1)
                    pe.sem_inc(chunk_used[slot[n][0]], 1)
            pe.wait_ge(sq2_sum, KD - 1)
            nc.tensor.matmul(ps[:, 5, :], ones[:], rstd2[:], start=True, stop=True).then_inc(ms2, 1)
            for h in range(PH):
                n = place["query", h // 4]
                if h % 4 == 0:
                    pe.wait_ge(w_split, 2 + h // 4)
                if h >= 4:
                    pe.wait_ge(qp_sb, h - 3)
                product(ps[:, h % 4, :], ("query", h // 4), (h % 4) * P, h2hi, h2lo, h2_split if h == 0 else None).then_inc(qp_ps, 1)
                if h in (3, 6):
                    modulation({3: 10, 6: 11}[h])
                if h % 4 == 3:
                    pe.wait_ge(qp_ps, h + 1)
                    pe.sem_inc(chunk_used[slot[n][0]], 1)
            pe.wait_ge(sk_in, 16)

            def key_scores(tt):
                for h in range(PH):
                    if tt == 0:
                        pe.wait_ge(qp_sb, h + 1)
                    for half in range(2):
                        rows = slice(PD * half, PD * (half + 1))
                        last = nc.tensor.matmul(ps[:, 4 * (1 - tt % 2) + 2 * half + h // 4, (h % 4) * P:(h % 4 + 1) * P],
                                                qpT[rows, h, tt * P:(tt + 1) * P], skT[rows, h, :], start=True, stop=True)
                last.then_inc(key_ps, 1)

            for tt in range(TT):
                if tt == 0:
                    pe.wait_ge(ada_read, 1)
                if tt >= 2:
                    pe.wait_ge(s_copied, tt - 1)
                key_scores(tt)

            pe.wait_ge(h2_split, KD)
            pe.wait_ge(s_copied, TT - 1)

            def dot(n, r):
                pe.wait_ge(u_lo, n + 3)
                pe.wait_ge(gelu_done, n + 1)
                for k in range(KD):
                    cols = slice(k * P, (k + 1) * P)
                    nc.tensor.matmul(ps[:, DOT_BANKS[r % 2], :], uhi[r % 2][:, cols], h2hi[:, k, :], start=(k == 0), stop=False)
                    nc.tensor.matmul(ps[:, DOT_BANKS[r % 2], :], uhi[r % 2][:, cols], h2lo[:, k, :], start=False, stop=False)
                    last = nc.tensor.matmul(ps[:, DOT_BANKS[r % 2], :], ulo[r % 2][:, cols], h2hi[:, k, :], start=False, stop=(k == KD - 1))
                last.then_inc(a_ps, 1)

            def token_gates(q, half):
                pe.wait_ge(oh_ready, q + 1)
                pe.wait_ge(g_parts, q + 1)
                for t in range(HB):
                    last = nc.tensor.matmul(ps[:, 2 + 2 * half + t // 2, (t % 2) * 2 * P:(t % 2 + 1) * 2 * P], ohJ[half][:, t, :],
                                            ohW[half][:, t, :, :].rearrange("p s i -> p (s i)"), start=True, stop=True)
                last.then_inc(oh_used, 1)

            def dots(first, steps):
                with pe.Fori(0, steps // 4) as i:
                    for r in range(4):
                        dot(i * 4 + (first + r), r)

            dots(0, SOLO)
            with pe.Fori(0, TT) as tt:
                pe.wait_ge(ijw_ready, tt + 1)
                for f in range(3):
                    last = nc.tensor.transpose(ps[:, 6, f * P:(f + 1) * P], IJW[:, f, :, :], ident[:])
                last.then_inc(ijw_ps, 1)
                with pe.Fori(0, BOTH // 4) as i:
                    for r in range(4):
                        dot(tt * SEG + i * 4 + (SOLO + r), r)
                        for half in range(2):
                            token_gates(tt * (2 * BOTH) + i * 8 + (2 * r + half), half)
                pe.wait_ge(oh_used, tt * (2 * BOTH) + (2 * BOTH + 2))
                pe.sem_inc(c_space, 1)
                dots(tt * SEG + (SOLO + BOTH), SOLO)
            dots(TT * SEG + SOLO, NT - TT * SEG - SOLO)

            def mix(n, r, first):
                pe.wait_ge(v_lo, n + 1)
                pe.wait_ge(c_lo, n + 1)
                last_bank = DOT_BANKS[(NT - 1) % 2]
                for d in [b for b in range(KD) if b != last_bank] + [last_bank] if first else range(KD):
                    if first and d == last_bank:
                        pe.wait_ge(gelu_done, NT + 2)
                    cols = slice(d * P, (d + 1) * P)
                    nc.tensor.matmul(ps[:, d, :], vhi[r][:, cols], chi[r][:], start=first, stop=False)
                    nc.tensor.matmul(ps[:, d, :], vhi[r][:, cols], clo[r][:], start=False, stop=False)
                    last = nc.tensor.matmul(ps[:, d, :], vlo[r][:, cols], chi[r][:], start=False, stop=False)
                last.then_inc(y_ps, 1)

            pe.wait_ge(gelu_done, NT + 1)
            for r in range(4):
                mix(r, r, r == 0)
            with pe.Fori(1, NT // 4 - 1) as i:
                for r in range(4):
                    mix(i * 4 + r, r, False)
            pe.wait_ge(v_lo, NT)
            pe.wait_ge(c_lo, NT)
            for d in range(KD):
                cols = slice(d * P, (d + 1) * P)
                for r in range(4):
                    nc.tensor.matmul(ps[:, d, :], vhi[r][:, cols], chi[r][:], start=False, stop=False)
                    nc.tensor.matmul(ps[:, d, :], vhi[r][:, cols], clo[r][:], start=False, stop=False)
                    last = nc.tensor.matmul(ps[:, d, :], vlo[r][:, cols], chi[r][:], start=False, stop=(r == 3))
                last.then_inc(y_ps, 1)

        @block.vector
        def _(dve):
            steps = [0]

            def settled(ins):
                steps[0] += 1
                ins.then_inc(dve_step, 1)
                dve.wait_ge(dve_step, steps[0])

            tt_ = nc.vector.tensor_tensor
            def reverse(rstd, sd):
                dve.wait_ge(sd, 1)
                settled(nc.vector.reciprocal(rstd, rstd))

            def modulate(j):
                n = place["ada", j]
                order = prepared.index(j)
                at, before = slot[n]
                dve.wait_ge(chunk_in[at], 16 * (before + 1))
                if order >= 2:
                    dve.wait_ge(ada_done, ada_order.index(prepared[order - 2]) + 1)
                sums = acc(j)
                settled(nc.vector.tensor_scalar(sums, chunk(n)[:, 0, :], cT[:, 0:1], None, ALU.mult))
                for k in range(1, KD):
                    settled(nc.vector.scalar_tensor_tensor(out=sums, in0=chunk(n)[:, k, :], scalar=cT[:, k:k + 1],
                                                           in1=sums, op0=ALU.mult, op1=ALU.add))
                dve.sem_inc(chunk_used[at], 1)
                dve.sem_inc(acc_done, 1)

            def modulation(piece, chunks_done):
                dve.wait_ge(ada_done, chunks_done)
                cols = slice(piece * KD, (piece + 1) * KD)
                settled(tt_(ada[:, cols], ada_ps[:, cols], b_cols[:, cols], ALU.add))

            dve.wait_ge(c_in, 16)
            for j in prepared[:3]:
                modulate(j)
            reverse(rstd1, sd1)
            dve.wait_ge(small_in, 16 * NSMALL)
            modulation(1, 4)
            settled(nc.vector.scalar_tensor_tensor(out=gs[:], in0=ada[:, KD:2 * KD], scalar=1.0, in1=g1[:],
                                                   op0=ALU.add, op1=ALU.mult))
            modulation(0, 4)
            for k in range(KD):
                nc.vector.scalar_tensor_tensor(out=hT[:, k, :], in0=res[:, k, :], scalar=gs[:, k:k + 1], in1=rstd1,
                                               op0=ALU.mult, op1=ALU.mult).then_inc(h_scaled, 1)
            for f in range(ROPE // 2):
                last = nc.vector.memset(freq[:, f:f + 1], ROPE_THETA ** (-2.0 * f / ROPE))
            settled(last)
            tt_(g_mla[:, 0, :], g_mla[:, 0, :], g_mla[:, 1, :], ALU.mult)
            settled(tt_(g_swa[:, 0, :], g_swa[:, 0, :], g_swa[:, SH, :], ALU.mult))
            nc.vector.tensor_scalar(g_mla[:, 0, :], g_mla[:, 0, :], QK ** -0.5, None, ALU.mult)
            settled(nc.vector.tensor_scalar(g_swa[:, 0, :], g_swa[:, 0, :], SD ** -0.5, None, ALU.mult))
            nc.vector.tensor_copy(g_swa[:, 1:SH, :], g_swa[:, 0, :].unsqueeze(1).to_broadcast([P, SH - 1, SD]))
            nc.vector.tensor_copy(posk, posk_i)
            settled(nc.vector.tensor_copy(posqf[:], posq[:]))
            for sc in range(2):
                settled(tt_(ang[:, :, sc, :], posqf[:].unsqueeze(2).to_broadcast([P, TT, ROPE // 2]),
                            freq[:].unsqueeze(1).to_broadcast([P, TT, ROPE // 2]), ALU.mult))
                nc.vector.tensor_scalar(turns[:, :, sc, :], ang[:, :, sc, :], 0.15915494309189535,
                                        0.25 if sc == 0 else 0.0, ALU.mult, ALU.add)
            settled(nc.vector.memset(sm[:], 0.0))
            settled(nc.vector.tensor_scalar(turns, turns, ROUND, None, ALU.add))
            settled(nc.vector.tensor_scalar(turns, turns, ROUND, None, ALU.subtract))
            for part in (PI2_A, PI2_B, PI2_C):
                settled(nc.vector.scalar_tensor_tensor(out=ang.rearrange("p t s f -> p (t s f)"),
                                                       in0=turns.rearrange("p t s f -> p (t s f)"), scalar=-part,
                                                       in1=ang.rearrange("p t s f -> p (t s f)"), op0=ALU.mult, op1=ALU.add))
            settled(nc.vector.tensor_scalar(ang[:, :, 0, :], ang[:, :, 0, :], 1.5707963267948966, None, ALU.add))
            nc.vector.tensor_scalar(ang, ang, 3.1415925, -3.1415925, ALU.min, ALU.max).then_inc(ang_ready, 1)
            for b in range(TT):
                k0 = 0 if b else P
                settled(nc.vector.tensor_scalar(distm[:, b, k0:256], posk[:, (b - 1) * P + k0:(b + 1) * P],
                                                posqf[:, b:b + 1], None, ALU.subtract))
                settled(nc.vector.scalar_tensor_tensor(out=distm[:, b, k0:256], in0=distm[:, b, k0:256], scalar=-1.0,
                                                       in1=distm[:, b, k0:256], op0=ALU.mult, op1=ALU.max))
                if b:
                    nc.vector.memset(distm[0:64, b, 0:64], MASKED)
                    nc.vector.memset(distm[64:128, b, 0:128], MASKED)
                settled(nc.vector.memset(distm[0:64, b, 192:256], MASKED))

            for j in prepared[3:7]:
                modulate(j)
            for tt in range(TT):
                dve.wait_ge(z_stat, tt + 1)
                nc.vector.tensor_reduce(ss[:, tt, SH:10], zsq_k[:, tt, :].rearrange("p (h d) -> p h d", d=SD), X, ALU.add)
            dve.wait_ge(z_stat, 2 * TT)
            nc.vector.tensor_scalar(rz[:, :, 10:11], ss[:, :, 10:11], 1.0 / QRANK, EPS, ALU.mult, ALU.add)
            settled(nc.vector.tensor_scalar(rz[:, :, 11:12], ss[:, :, 11:12], 1.0 / KVRANK, EPS, ALU.mult, ALU.add))
            nc.vector.tensor_scalar(rz[:, :, SH:10], ss[:, :, SH:10], 1.0 / SD, EPS, ALU.mult, ALU.add).then_inc(z_var, 1)
            dve.wait_ge(z_sd, 1)
            settled(nc.vector.reciprocal(rz[:, :, SH:12], rz[:, :, SH:12]))
            for tt in range(TT):
                zh = z[:, tt, Z_K:Z_V].rearrange("p (h d) -> p h d", d=SD)
                zc, zk = z[:, tt, Z_CQ:Z_CKV], z[:, tt, Z_CKV:Z_KR]
                tt_(zh, zh, rz[:, tt, SH:10].unsqueeze(2).to_broadcast([P, SKV, SD]), ALU.mult)
                nc.vector.scalar_tensor_tensor(out=zc, in0=zc, scalar=rz[:, tt, 10:11], in1=g_cq[:],
                                               op0=ALU.mult, op1=ALU.mult)
                nc.vector.scalar_tensor_tensor(out=zk, in0=zk, scalar=rz[:, tt, 11:12], in1=g_ckv[:],
                                               op0=ALU.mult, op1=ALU.mult).then_inc(zn_ready, 1)

            def sum_queries(tt):
                dve.wait_ge(zq_stat, tt + 1)
                nc.vector.tensor_reduce(ss[:, tt, 0:SH], zsq_q.rearrange("p (h d) -> p h d", d=SD), X, ALU.add).then_inc(zq_summed, 1)

            dve.wait_ge(trig_ready, 1)

            def rope(tt):
                dve.wait_ge(m_built, tt + 1)
                m = heads(tt)
                x1, x2 = m[:, :, NOPE:NOPE + 16], m[:, :, NOPE + 16:QK]
                cos = trig[:, tt, 0, :].unsqueeze(1).to_broadcast([P, 2 * MH, 16])
                sin = trig[:, tt, 1, :].unsqueeze(1).to_broadcast([P, 2 * MH, 16])
                tt_(ropet[0], x1, cos, ALU.mult)
                tt_(ropet[1], x2, sin, ALU.mult)
                tt_(ropet[2], x1, sin, ALU.mult)
                settled(tt_(ropet[3], x2, cos, ALU.mult))
                tt_(x1, ropet[0], ropet[1], ALU.subtract)
                tt_(x2, ropet[2], ropet[3], ALU.add).then_inc(m_roped, 1)

            def sum_heads(tt):
                dve.wait_ge(m_sq, tt + 1)
                settled(nc.vector.tensor_reduce(mss[:], msq, X, ALU.add))
                nc.vector.tensor_scalar(mrz[:], mss[:], 1.0 / QK, EPS, ALU.mult, ALU.add).then_inc(m_var, 1)

            def norm_heads(tt):
                dve.wait_ge(m_sd, tt + 1)
                m = heads(tt)
                settled(nc.vector.reciprocal(mrz[:], mrz[:]))
                settled(tt_(m, m, mrz[:].unsqueeze(2).to_broadcast([P, 2 * MH, QK]), ALU.mult))
                tt_(m[:, 0:MH, :], m[:, 0:MH, :], g_mla[:, 0, :].unsqueeze(1).to_broadcast([P, MH, QK]), ALU.mult).then_inc(m_ready, 1)

            sum_queries(0)
            for tt in range(TT):
                rope(tt)
                sum_heads(tt)
                if tt < 2:
                    sum_queries(tt + 1)
                norm_heads(tt)
                if tt == 2:
                    sum_queries(3)
                    dve.wait_ge(zq_summed, TT)
                    nc.vector.tensor_scalar(rz[:, :, 0:SH], ss[:, :, 0:SH], 1.0 / SD, EPS, ALU.mult, ALU.add).then_inc(z_var, 1)
                    dve.wait_ge(z_sd, 2)
                    settled(nc.vector.reciprocal(rz[:, :, 0:SH], rz[:, :, 0:SH]))
                    for t in range(TT):
                        zh = z[:, t, 0:Z_K].rearrange("p (h d) -> p h d", d=SD)
                        settled(tt_(zh, zh, rz[:, t, 0:SH].unsqueeze(2).to_broadcast([P, SH, SD]), ALU.mult))
                        tt_(zh, zh, g_swa[:, 0:SH, :], ALU.mult).then_inc(zqn_ready, 1)

            def bias_and_max(u):
                kind, b, sub, j0 = units[u]
                dve.wait_ge(s_done, u + 1)
                if u >= 4:
                    dve.wait_ge(pt_ps, u - 3)
                nk = len(key_tiles(kind, b)) * P
                if kind == "s":
                    k0 = 256 - nk
                    for j in range(2):
                        nc.vector.scalar_tensor_tensor(out=pb[:, u % 4, j, k0:256], in0=distm[:, b, k0:256],
                                                       scalar=-slope(sub * SG + j0 + j), in1=ps[:, u % 3, j * 256 + k0:j * 256 + 256],
                                                       op0=ALU.mult, op1=ALU.add)
                    h0 = sub * SG + j0
                    settled(nc.vector.tensor_copy(pb[:, u % 4, :, 256:257], sinks[:, h0:h0 + 2].unsqueeze(2)))
                    nc.vector.tensor_reduce(nm[:, u % 4, :], pb[:, u % 4, :, k0:257], X, ALU.max, negate=True).then_inc(biased, 1)
                else:
                    settled(nc.vector.memset(ps[0:64, u % 3, b * P + 64:(b + 1) * P], NEG))
                    nc.vector.tensor_reduce(nm[:, u % 4, 0:1], ps[:, u % 3, 0:nk], X, ALU.max, negate=True).then_inc(biased, 1)

            def scale_probs(u):
                kind, b, _, _ = units[u]
                dve.wait_ge(exp_done, u + 1)
                nj = heads_of(kind)
                nk = len(key_tiles(kind, b)) * P
                settled(nc.vector.reciprocal(rsm[:, u % 4, 0:nj], sm[:, u % 4, 0:nj]))
                for j in range(nj):
                    v = pb[:, u % 4, j, 256 - nk:256] if kind == "s" else p_view(u, kind)[:, 0, 0:nk]
                    last = nc.vector.tensor_scalar(v, v, rsm[:, u % 4, j:j + 1], None, ALU.mult)
                last.then_inc(p_ready, 1)

            def copy_out(u):
                kind, b, sub, j0 = units[u]
                dve.wait_ge(o_ps, u + 1)
                cols = slice(b * P, (b + 1) * P)
                if kind == "s":
                    ins = nc.vector.tensor_copy(oT[:, 2 * sub + j0 // 2, cols], ps[:, 3 * (u % 2) + 3, 0:P])
                else:
                    rows = slice(64 * (sub % 2), 64 * (sub % 2) + 64)
                    ins = nc.vector.tensor_copy(oT[rows, 4 + sub // 2, cols], ps[rows, 3 * (u % 2) + 3, 0:P])
                ins.then_inc(o_sb, 1)

            for piece in (2, 4):
                modulation(piece, 8)
            settled(nc.vector.scalar_tensor_tensor(out=gs[:], in0=ada[:, 4 * KD:5 * KD], scalar=1.0, in1=g2[:],
                                                   op0=ALU.add, op1=ALU.mult))
            bias_and_max(0)
            for u in range(NU):
                if u + 1 < NU:
                    bias_and_max(u + 1)
                scale_probs(u)
                if u >= 2:
                    copy_out(u - 2)
            copy_out(NU - 2)
            copy_out(NU - 1)
            def low_w(key, count):
                dve.wait_ge(w_hi, count)
                hi, lo = parts[key]
                tt_(lo[:], chunk(place[key]), hi[:].bitcast(F32), ALU.subtract).then_inc(w_split, 1)

            for k in range(KD):
                dve.wait_ge(o_hi, k + 1)
                tt_(oTlo[:, k, :], oT[:, k, :], oThi[:, k, :].bitcast(F32), ALU.subtract).then_inc(o_split, 1)
            low_w(("out", 1), 1)
            modulate(6)
            for m in range(KD):
                dve.wait_ge(mix_ps, m + 1)
                nc.vector.scalar_tensor_tensor(out=res[:, m, :], in0=ps[:, m % 4, :], scalar=ada[:, 2 * KD + m:2 * KD + m + 1],
                                               in1=res[:, m, :], op0=ALU.mult, op1=ALU.add).then_inc(x1_ready, 1)
                if m == 4:
                    modulate(7)
            modulation(3, 10)
            low_w(("query", 0), 2)
            reverse(rstd2[:], sd2)

            def low_h2(k):
                dve.wait_ge(h2_hi, k + 1)
                nc.vector.scalar_tensor_tensor(out=h2lo[:, k, :], in0=h2T[:, k, :], scalar=ada[:, 3 * KD + k:3 * KD + k + 1],
                                               in1=h2hi[:, k, :].bitcast(F32), op0=ALU.add, op1=ALU.subtract).then_inc(h2_split, 1)

            for k in range(KD):
                nc.vector.scalar_tensor_tensor(out=h2T[:, k, :], in0=res[:, k, :], scalar=gs[:, k:k + 1], in1=rstd2[:],
                                               op0=ALU.mult, op1=ALU.mult).then_inc(h2_scaled, 1)
                if k:
                    low_h2(k - 1)
            low_h2(KD - 1)
            low_w(("query", 1), 3)
            modulate(10)
            modulate(11)
            modulation(5, 12)
            dve.sem_inc(ada_read, 1)

            def top16(vals, idx, rows, n):
                for a in range(n):
                    last = nc.vector.max(vals(a)[:, 0:8], rows(a))
                settled(last)
                for a in range(n):
                    last = nc.vector.max_index(idx(a)[:, 0:8], vals(a)[:, 0:8], rows(a))
                settled(last)
                for a in range(n):
                    last = nc.vector.match_replace(rows(a), vals(a)[:, 0:8], rows(a), -3.0e38)
                settled(last)
                for a in range(n):
                    last = nc.vector.max(vals(a)[:, 8:16], rows(a))
                settled(last)
                for a in range(n):
                    last = nc.vector.max_index(idx(a)[:, 8:16], vals(a)[:, 8:16], rows(a))
                settled(last)

            for tt in range(TT):
                dve.wait_ge(s_in, tt * 16 + 16)
                top16(lambda a: sv[:, a % PH, a // PH, :], lambda a: six[:, a % PH, a // PH, :], lambda a: s[:, a, :], 2 * PH)
                nc.vector.tensor_copy(sixf[:], six[:])
                settled(tt_(cand[:], sv[:, :, 0, :].unsqueeze(3).to_broadcast([P, PH, KTOP, KTOP]),
                           sv[:, :, 1, :].unsqueeze(2).to_broadcast([P, PH, KTOP, KTOP]), ALU.add))
                top16(lambda a: best[:, a, :], lambda a: bi[:, a, :],
                      lambda a: cand[:, a, :, :].rearrange("p i j -> p (i j)"), PH)
                tt_(eW[:], best[:], best[:, :, 0:1].to_broadcast([P, PH, KTOP]), ALU.subtract).then_inc(best_ready, 1)
                nc.vector.tensor_scalar(bia[:, 0, :, :], bi[:], 4, None, ALU.logical_shift_right)
                settled(nc.vector.tensor_scalar(bia[:, 1, :, :], bi[:], 15, None, ALU.bitwise_and))
                settled(nc.vector.tensor_copy(abf[:], bia[:]))
                for half in range(2):
                    settled(tt_(eq, abf[:, half, :, :].unsqueeze(3).to_broadcast([P, PH, KTOP, KTOP]),
                               iota[:, 0:KTOP].unsqueeze(1).unsqueeze(1).to_broadcast([P, PH, KTOP, KTOP]), ALU.is_equal))
                    settled(tt_(eq, eq, sixf[:, :, half, :].unsqueeze(2).to_broadcast([P, PH, KTOP, KTOP]), ALU.mult))
                    settled(nc.vector.tensor_reduce(IJW[:, half, :, :], eq, X, ALU.add))
                dve.sem_inc(s_free, 1)
                dve.wait_ge(best_exp, tt + 1)
                settled(nc.vector.tensor_reduce(eS[:], eW[:], X, ALU.add))
                settled(nc.vector.reciprocal(eR[:], eS[:]))
                tt_(IJW[:, 2, :, :], eW[:], eR[:].unsqueeze(2).to_broadcast([P, PH, KTOP]), ALU.mult).then_inc(ijw_ready, 1)
                dve.wait_ge(ijw_ps, tt + 1)
                settled(nc.vector.tensor_copy(slots[:, 0:3, :], ps[:, 6, 0:3 * P].rearrange("p (a t) -> p a t", a=3)))
                settled(nc.vector.tensor_copy(slots[:, 3, :].bitcast(F32R), slots[:, 2, :]))
                settled(tt_(slots[:, 4, :], slots[:, 2, :], slots[:, 3, :], ALU.subtract))
                def one_hot(q, col, half):
                    dve.wait_ge(oh_used, q + 1)
                    cols = bass.ds(col, HB)
                    each = iota[:].unsqueeze(1).to_broadcast([P, HB, P])
                    tt_(eqI[:, half, :, :], each, slots[:, 0, cols].unsqueeze(2).to_broadcast([P, HB, P]), ALU.is_equal)\
                        .then_inc(eq_ready, 1)
                    tt_(ohJ[half][:], each, slots[:, 1, cols].unsqueeze(2).to_broadcast([P, HB, P]), ALU.is_equal)
                    dve.wait_ge(eq_ready, q + 1)
                    tt_(ohW[half][:], eqI[:, half, :, :].unsqueeze(2).to_broadcast([P, HB, 2, P]),
                        slots[:, 3:5, cols].rearrange("p s t -> p t s").unsqueeze(3).to_broadcast([P, HB, 2, P]), ALU.mult)\
                        .then_inc(oh_ready, 1)

                with dve.Fori(0, BOTH) as i:
                    for half in range(2):
                        one_hot(i * 2 + (tt * 2 * BOTH + half), i * (2 * HB) + HB * half, half)

            def low_v(n, r):
                dve.wait_ge(v_hi, n + 1)
                tt_(vlo[r][:], vraw[r][:], vhi[r][:].bitcast(F32), ALU.subtract).then_inc(v_lo, 1)

            def weigh(n, r, count, first):
                dve.wait_ge(gate_in[r], count)
                dve.wait_ge(act_back[r], count)
                if not first or r >= 2:
                    dve.wait_ge(c_lo, n - 1)
                c = cf[r % 2]
                tt_(c[:], act_in[r][:], gate[r][:], ALU.mult).then_inc(c_mul, 1)
                dve.wait_ge(c_mul, n + 1)
                nc.vector.tensor_copy(chi[r][:], c[:]).then_inc(c_hi, 1)
                dve.wait_ge(c_hi, n + 1)
                tt_(clo[r][:], c[:], chi[r][:].bitcast(F32), ALU.subtract).then_inc(c_lo, 1)

            for r in range(4):
                low_v(r, r)
                weigh(r, r, 16, True)
            with dve.Fori(1, NT // 4) as i:
                for r in range(4):
                    low_v(i * 4 + r, r)
                    weigh(i * 4 + r, r, i * 16 + 16, False)
            for d in range(KD):
                dve.wait_ge(y_ps, NT - 4 + d + 1)
                nc.vector.scalar_tensor_tensor(out=res[:, d, :], in0=ps[:, d, :], scalar=ada[:, 5 * KD + d:5 * KD + d + 1],
                                               in1=res[:, d, :], op0=ALU.mult, op1=ALU.add).then_inc(y_sb, 1)


def kernel(**inputs):
    import numpy as np
    import concourse.bacc as bacc
    from concourse.bass_utils import run_bass_kernel_spmd as run

    a = {n: np.asarray(v) for n, v in inputs.items()}

    def cols(v):
        return np.ascontiguousarray(v.reshape(-1, P).T)

    sent = {
        "xT": np.ascontiguousarray(a["x"][0].T.reshape(KD, P, T).transpose(1, 0, 2)),
        "c": cols(a["c"][0]),
        "positions": np.ascontiguousarray(a["positions"][0]),
        "position_cols": cols(a["positions"][0]),
        "w_ada": a["w_ada"][0], "b_ada": cols(a["b_ada"][0]),
        "norm1_g": cols(a["norm1_g"][0]), "norm2_g": cols(a["norm2_g"][0]),
        "w_in": a["w_in"][0],
        "swa_q_norm": a["swa_q_norm"][0], "swa_k_norm": a["swa_k_norm"][0], "swa_sinks": a["swa_sinks"][0],
        "mla_q_a_norm": a["mla_q_a_norm"][0], "mla_kv_a_norm": a["mla_kv_a_norm"][0],
        "mla_w_uq": a["mla_w_uq"][0], "mla_w_ukv": a["mla_w_ukv"][0],
        "mla_q_norm": a["mla_q_norm"][0], "mla_k_norm": a["mla_k_norm"][0],
        "w_out": a["w_out"][0], "peer_w_query": a["peer_w_query"][0],
        "sub_keys": a["peer_sub_keys"][0].transpose(1, 3, 0, 2).reshape(P, PH, NK),
        "u_tiles": a["peer_u"][0].reshape(NT, P, KD, P).transpose(0, 3, 2, 1).reshape(NT, P, D),
        "v_tiles": a["peer_v"][0].reshape(NT, P, D),
    }
    sent = {n: np.ascontiguousarray(v) for n, v in sent.items()}
    nc = bacc.Bacc("TRN2", target_bir_lowering=False, num_devices=1)
    args = {n: nc.dram_tensor(f"in_{n}", v.shape, mybir.dt.from_np(v.dtype), kind="ExternalInput").ap()
            for n, v in sent.items()}
    args["outT"] = nc.dram_tensor("out_T", (KD, P, T), F32, kind="ExternalOutput").ap()
    build(nc, **args)
    r = run(nc, [{f"in_{n}": v for n, v in sent.items()}], core_ids=[0])
    return np.ascontiguousarray(r.results[0]["out_T"].reshape(D, T).T)[None]
```
